# Optimizing a Trainium2 kernel written in Bass

```python
import math
import jax, jax.numpy as jnp
from jax import lax
import numpy as np

D_MODEL = 1024
BATCH = 1
SEQ = 512
DEPTH = 2

GRID_W = 64
CTX_LEN = 256
HEAD_DIM = 64
ROPE_BASE = 10000.0
EPS = 1e-6
NEG_INF = -1e30
ATTN_SCALE = HEAD_DIM ** -0.5
Q_BLOCK = 128
CHUNK = 128
A_GROUPS = 4
A_GROUP_DIM = 128
A_WIDTH = A_GROUPS * A_GROUP_DIM
B_HEADS = 4
B_QK_WIDTH = 2 * B_HEADS * HEAD_DIM
B_V_DIM = 2 * HEAD_DIM
B_V_WIDTH = B_HEADS * B_V_DIM
KV_START = 2 * A_WIDTH + B_QK_WIDTH
EVEN_IN = 2 * A_WIDTH + 2 * B_QK_WIDTH + B_V_WIDTH
EVEN_OUT = A_WIDTH + B_V_WIDTH
C_HEADS = 16
C_KV_HEADS = 4
C_GROUP = C_HEADS // C_KV_HEADS
WINDOW = 128
C_Q_WIDTH = C_HEADS * HEAD_DIM
C_KV_WIDTH = C_KV_HEADS * HEAD_DIM
C_IN = C_Q_WIDTH + 2 * C_KV_WIDTH
FFN_HIDDEN = ((8 * D_MODEL + 3 * 256 - 1) // (3 * 256)) * 256
N_EVEN = (DEPTH + 1) // 2
N_ODD = DEPTH // 2


def rmsnorm(x, g):
    xf = x.astype(jnp.float32)
    y = xf * lax.rsqrt(jnp.mean(xf * xf, axis=-1, keepdims=True) + EPS)
    return (y * g.astype(jnp.float32)).astype(x.dtype)

def modulate(x, g, shift, scale):
    return rmsnorm(x, g) * (1 + scale) + shift

def rope_tables(s_len, dtype):
    rows = s_len // GRID_W
    row = jnp.repeat(jnp.arange(rows), GRID_W).astype(jnp.float32)
    col = jnp.tile(jnp.arange(GRID_W), rows).astype(jnp.float32)
    nf = HEAD_DIM // 4
    inv = ROPE_BASE ** (-jnp.arange(nf, dtype=jnp.float32) / nf)
    ang = jnp.stack([row[:, None] * inv, col[:, None] * inv], axis=1)
    ang = jnp.broadcast_to(ang[:, :, None, :], (s_len, 2, 2, nf)).reshape(s_len, HEAD_DIM)
    return jnp.cos(ang).astype(dtype), jnp.sin(ang).astype(dtype)

def apply_rope(x, cos, sin):
    xr = x.reshape(x.shape[:-1] + (2, 2, HEAD_DIM // 4))
    rot = jnp.stack([-xr[..., 1, :], xr[..., 0, :]], axis=-2).reshape(x.shape)
    return x * cos[None, :, None, :] + rot * sin[None, :, None, :]

def swiglu(h, w_in, w_out):
    g, u = jnp.split(h @ w_in, 2, axis=-1)
    return (jax.nn.silu(g) * u) @ w_out

def chunk_mlp(u, v, w_s, b_s):
    b, t, _ = u.shape
    shp = (b, t // CHUNK, CHUNK, A_GROUPS, A_GROUP_DIM)
    u = jax.nn.gelu(u, approximate=False).reshape(shp)
    vf = jax.nn.gelu(v.astype(jnp.float32), approximate=False).reshape(shp)
    mu = jnp.mean(vf, axis=-1, keepdims=True)
    vf = (vf - mu) * lax.rsqrt(jnp.mean(jnp.square(vf - mu), axis=-1, keepdims=True) + EPS)
    mixed = jnp.einsum('gpq,bnqgc->bnpgc', w_s.astype(jnp.float32), vf) + b_s.astype(jnp.float32).T[None, None, :, :, None]
    return (u * mixed.astype(u.dtype)).reshape(b, t, A_WIDTH)

def diff_attn(q, k, v, lam):
    b, tq = q.shape[0], q.shape[1]
    tk = k.shape[1]
    s = jnp.einsum('bqhd,bkhd->bhqk', q, k).astype(jnp.float32) * ATTN_SCALE
    p = jax.nn.softmax(s, axis=-1).reshape(b, B_HEADS, 2, tq, tk)
    a = p[:, :, 0] - lam * p[:, :, 1]
    return jnp.einsum('bhqk,bkhe->bqhe', a.astype(v.dtype), v)

def diff_out(o, g, lam_init):
    b, t = o.shape[0], o.shape[1]
    return (rmsnorm(o, g) * (1.0 - lam_init)).reshape(b, t, B_V_WIDTH)

def sink_attend(q, kvs, sink):
    scores = []
    for k, v, mask in kvs:
        s = jnp.einsum('bqhgd,bkhd->bhgqk', q, k).astype(jnp.float32) * ATTN_SCALE
        if mask is not None:
            s = jnp.where(mask, s, NEG_INF)
        scores.append(s)
    s_sink = jnp.broadcast_to(sink.astype(jnp.float32).reshape(1, C_KV_HEADS, C_GROUP, 1, 1), scores[0].shape[:-1] + (1,))
    p = jax.nn.softmax(jnp.concatenate(scores + [s_sink], axis=-1), axis=-1)
    out = None
    start = 0
    for k, v, _ in kvs:
        tk = k.shape[1]
        o = jnp.einsum('bhgqk,bkhd->bqhgd', p[..., start:start + tk].astype(v.dtype), v)
        out = o if out is None else out + o
        start += tk
    return out

def even_mixer(h, hc, w_in, w_out, w_s, b_s, lq1, lk1, lq2, lk2, subln_g, lam_init, cos, sin, need_ctx):
    b, s_len, _ = h.shape
    nb = s_len // Q_BLOCK
    f32 = jnp.float32
    lam = (jnp.exp(jnp.sum(lq1.astype(f32) * lk1.astype(f32)))
           - jnp.exp(jnp.sum(lq2.astype(f32) * lk2.astype(f32))) + lam_init)
    u, v, q, k, vv = jnp.split(h @ w_in, [A_WIDTH, 2 * A_WIDTH, KV_START, KV_START + B_QK_WIDTH], axis=-1)
    q = apply_rope(q.reshape(b, s_len, 2 * B_HEADS, HEAD_DIM), cos, sin)
    k = apply_rope(k.reshape(b, s_len, 2 * B_HEADS, HEAD_DIM), cos, sin)
    vv = vv.reshape(b, s_len, B_HEADS, B_V_DIM)
    kc, vvc = jnp.split(hc @ w_in[:, KV_START:], [B_QK_WIDTH], axis=-1)
    kc = kc.reshape(b, -1, 2 * B_HEADS, HEAD_DIM)
    vvc = vvc.reshape(b, -1, B_HEADS, B_V_DIM)
    k_all = jnp.concatenate([k, kc], axis=1)
    v_all = jnp.concatenate([vv, vvc], axis=1)
    q_blocks = q.reshape(b, nb, Q_BLOCK, 2 * B_HEADS, HEAD_DIM).transpose(1, 0, 2, 3, 4)
    o = lax.map(lambda qb: diff_attn(qb, k_all, v_all, lam), q_blocks)
    o = o.transpose(1, 0, 2, 3, 4).reshape(b, s_len, B_HEADS, B_V_DIM)
    y = jnp.concatenate([chunk_mlp(u, v, w_s, b_s), diff_out(o, subln_g, lam_init)], axis=-1) @ w_out
    yc = None
    if need_ctx:
        uc, vc_, qc = jnp.split(hc @ w_in[:, :KV_START], [A_WIDTH, 2 * A_WIDTH], axis=-1)
        qc = qc.reshape(b, -1, 2 * B_HEADS, HEAD_DIM)
        oc = diff_attn(qc, kc, vvc, lam)
        yc = jnp.concatenate([chunk_mlp(uc, vc_, w_s, b_s), diff_out(oc, subln_g, lam_init)], axis=-1) @ w_out
    return y, yc

def odd_mixer(h, hc, w_qkv, w_out, sink, cos, sin, need_ctx):
    b, s_len, _ = h.shape
    nb = s_len // Q_BLOCK
    q, k, v = jnp.split(h @ w_qkv, [C_Q_WIDTH, C_Q_WIDTH + C_KV_WIDTH], axis=-1)
    q = apply_rope(q.reshape(b, s_len, C_HEADS, HEAD_DIM), cos, sin).reshape(b, s_len, C_KV_HEADS, C_GROUP, HEAD_DIM)
    k = apply_rope(k.reshape(b, s_len, C_KV_HEADS, HEAD_DIM), cos, sin)
    v = v.reshape(b, s_len, C_KV_HEADS, HEAD_DIM)
    kc, vc = jnp.split(hc @ w_qkv[:, C_Q_WIDTH:], 2, axis=-1)
    kc = kc.reshape(b, -1, C_KV_HEADS, HEAD_DIM)
    vc = vc.reshape(b, -1, C_KV_HEADS, HEAD_DIM)
    pad = ((0, 0), (WINDOW, WINDOW), (0, 0), (0, 0))
    k_pad = jnp.pad(k, pad)
    v_pad = jnp.pad(v, pad)
    band = Q_BLOCK + 2 * WINDOW
    q_blocks = q.reshape(b, nb, Q_BLOCK, C_KV_HEADS, C_GROUP, HEAD_DIM).transpose(1, 0, 2, 3, 4, 5)

    def block(args):
        i, qb = args
        start = i * Q_BLOCK
        kb = lax.dynamic_slice_in_dim(k_pad, start, band, axis=1)
        vb = lax.dynamic_slice_in_dim(v_pad, start, band, axis=1)
        qpos = start + jnp.arange(Q_BLOCK)
        kpos = start - WINDOW + jnp.arange(band)
        mask = ((kpos >= 0)[None, :] & (kpos < s_len)[None, :]
                & (jnp.abs(qpos[:, None] - kpos[None, :]) <= WINDOW))
        return sink_attend(qb, [(kb, vb, mask), (kc, vc, None)], sink)

    o = lax.map(block, (jnp.arange(nb), q_blocks))
    y = o.transpose(1, 0, 2, 3, 4, 5).reshape(b, s_len, C_Q_WIDTH) @ w_out
    yc = None
    if need_ctx:
        qc = (hc @ w_qkv[:, :C_Q_WIDTH]).reshape(b, -1, C_KV_HEADS, C_GROUP, HEAD_DIM)
        yc = sink_attend(qc, [(kc, vc, None)], sink).reshape(b, -1, C_Q_WIDTH) @ w_out
    return y, yc

def first_inputs(seed: int = 0) -> dict:
    key = jax.random.key(seed)
    ks = jax.random.split(key, 24)
    n = jax.random.normal
    f32 = jnp.float32
    return {
        'x': n(ks[0], (BATCH, SEQ, D_MODEL), f32),
        'c': n(ks[1], (BATCH, D_MODEL), f32),
        'ctx': n(ks[2], (BATCH, CTX_LEN, D_MODEL), f32),
        'c_ctx': n(ks[3], (D_MODEL,), f32),
        'ada_w': n(ks[4], (DEPTH, D_MODEL, 6 * D_MODEL), f32) * (0.5 * D_MODEL ** -0.5),
        'ada_b': n(ks[5], (DEPTH, 6 * D_MODEL), f32) * 0.02,
        'norm1_g': 1.0 + 0.02 * n(ks[6], (DEPTH, D_MODEL), f32),
        'norm2_g': 1.0 + 0.02 * n(ks[7], (DEPTH, D_MODEL), f32),
        'ffn_w_in': n(ks[8], (DEPTH, D_MODEL, 2 * FFN_HIDDEN), f32) * D_MODEL ** -0.5,
        'ffn_w_out': n(ks[9], (DEPTH, FFN_HIDDEN, D_MODEL), f32) * FFN_HIDDEN ** -0.5,
        'even_w_in': n(ks[10], (N_EVEN, D_MODEL, EVEN_IN), f32) * D_MODEL ** -0.5,
        'even_w_out': n(ks[11], (N_EVEN, EVEN_OUT, D_MODEL), f32) * EVEN_OUT ** -0.5,
        'sgu_w': n(ks[12], (N_EVEN, A_GROUPS, CHUNK, CHUNK), f32) * CHUNK ** -0.5,
        'sgu_b': 1.0 + 0.1 * n(ks[13], (N_EVEN, A_GROUPS, CHUNK), f32),
        'diff_lq1': 0.1 * n(ks[14], (N_EVEN, HEAD_DIM), f32),
        'diff_lk1': 0.1 * n(ks[15], (N_EVEN, HEAD_DIM), f32),
        'diff_lq2': 0.1 * n(ks[16], (N_EVEN, HEAD_DIM), f32),
        'diff_lk2': 0.1 * n(ks[17], (N_EVEN, HEAD_DIM), f32),
        'diff_subln_g': 1.0 + 0.02 * n(ks[18], (N_EVEN, B_V_DIM), f32),
        'odd_w_qkv': n(ks[19], (N_ODD, D_MODEL, C_IN), f32) * D_MODEL ** -0.5,
        'odd_w_out': n(ks[20], (N_ODD, C_Q_WIDTH, D_MODEL), f32) * C_Q_WIDTH ** -0.5,
        'odd_sink': 0.5 * n(ks[21], (N_ODD, C_HEADS), f32),
        'final_g': 1.0 + 0.02 * n(ks[22], (D_MODEL,), f32),
    }

def first_block(x, c, ctx, c_ctx, ada_w, ada_b, norm1_g, norm2_g, ffn_w_in, ffn_w_out,
              even_w_in, even_w_out, sgu_w, sgu_b, diff_lq1, diff_lk1, diff_lq2, diff_lk2,
              diff_subln_g, odd_w_qkv, odd_w_out, odd_sink, final_g):
    s_len = x.shape[1]
    cos, sin = rope_tables(s_len, x.dtype)
    silu_c = jax.nn.silu(c)
    silu_cc = jax.nn.silu(c_ctx)
    h, hc = x, ctx
    for l in range(DEPTH):
        need_ctx = l < DEPTH - 1
        j = l // 2
        mod = silu_c @ ada_w[l] + ada_b[l]
        modc = silu_cc @ ada_w[l] + ada_b[l]
        sh1, sc1, g1, sh2, sc2, g2 = [m[:, None, :] for m in jnp.split(mod, 6, axis=-1)]
        csh1, csc1, cg1, csh2, csc2, cg2 = [m[None, None, :] for m in jnp.split(modc, 6, axis=-1)]
        a = modulate(h, norm1_g[l], sh1, sc1)
        ac = modulate(hc, norm1_g[l], csh1, csc1)
        if l % 2 == 0:
            lam_init = 0.8 - 0.6 * math.exp(-0.3 * l)
            y, yc = even_mixer(a, ac, even_w_in[j], even_w_out[j], sgu_w[j], sgu_b[j],
                               diff_lq1[j], diff_lk1[j], diff_lq2[j], diff_lk2[j], diff_subln_g[j],
                               lam_init, cos, sin, need_ctx)
        else:
            y, yc = odd_mixer(a, ac, odd_w_qkv[j], odd_w_out[j], odd_sink[j], cos, sin, need_ctx)
        h = h + g1 * y
        h = h + g2 * swiglu(modulate(h, norm2_g[l], sh2, sc2), ffn_w_in[l], ffn_w_out[l])
        if need_ctx:
            hc = hc + cg1 * yc
            hc = hc + cg2 * swiglu(modulate(hc, norm2_g[l], csh2, csc2), ffn_w_in[l], ffn_w_out[l])
    return rmsnorm(h, final_g)


N_MIXERS = 2
EXPAND = 2
D_INNER = EXPAND * D_MODEL
HG_HEAD_DIM = 128
HG_HEADS = D_INNER // HG_HEAD_DIM
HG_CHUNK = 32
N_HG_LAYERS = (DEPTH + 1) // 2
MLA_NOPE_DIM = 128
MLA_ROPE_DIM = 64
MLA_V_DIM = 128
MLA_HEADS = D_INNER // MLA_V_DIM
MLA_Q_RANK = D_MODEL // 4
MLA_KV_RANK = D_MODEL // 8
MLA_SCALE = (MLA_NOPE_DIM + MLA_ROPE_DIM) ** -0.5
N_MLA_LAYERS = DEPTH // 2
ROPE_THETA = 10000.0
ROPE_AXIS_DIM = MLA_ROPE_DIM // 2
NORM_EPS = 1e-6


def _rmsnorm(x, g):
    xf = x.astype(jnp.float32)
    y = xf * lax.rsqrt(jnp.mean(xf * xf, axis=-1, keepdims=True) + NORM_EPS)
    return (y * g.astype(jnp.float32)).astype(x.dtype)

def _axial_rope(n_tokens):
    rows = n_tokens // GRID_W
    row = jnp.repeat(jnp.arange(rows, dtype=jnp.float32), GRID_W)
    col = jnp.tile(jnp.arange(GRID_W, dtype=jnp.float32), rows)
    inv = ROPE_THETA ** (-jnp.arange(0, ROPE_AXIS_DIM, 2, dtype=jnp.float32) / ROPE_AXIS_DIM)
    ang = jnp.concatenate([row[:, None] * inv, col[:, None] * inv], axis=-1)
    return jnp.cos(ang), jnp.sin(ang)

def _apply_rope(x, cos, sin):
    half = x.shape[-1] // 2
    x1 = x[..., :half].astype(jnp.float32)
    x2 = x[..., half:].astype(jnp.float32)
    return jnp.concatenate([x1 * cos - x2 * sin, x1 * sin + x2 * cos], axis=-1).astype(x.dtype)

def _hgrn2_scan(q, k, v, log_f, s0):
    B, L, H, _ = q.shape
    DV = v.shape[-1]
    n = L // HG_CHUNK

    def chunks(t):
        return jnp.moveaxis(t.astype(jnp.float32).reshape(B, n, HG_CHUNK, H, t.shape[-1]), 1, 0)

    tri = jnp.tril(jnp.ones((HG_CHUNK, HG_CHUNK), dtype=bool))[None, :, :, None, None]

    def step(S, xs):
        qc, kc, vc, lfc = xs
        b = jnp.cumsum(lfc, axis=1)
        b_last = b[:, -1]
        o_inter = jnp.einsum('bthk,bhkv->bthv', qc * jnp.exp(b), S)
        decay = jnp.exp(jnp.where(tri, b[:, :, None] - b[:, None, :], -jnp.inf))
        scores = jnp.einsum('bthk,btshk,bshk->bhts', qc, decay, kc)
        o_intra = jnp.einsum('bhts,bshv->bthv', scores, vc)
        S_new = jnp.exp(b_last)[..., None] * S + jnp.einsum(
            'bshk,bshv->bhkv', kc * jnp.exp(b_last[:, None] - b), vc)
        return S_new, o_inter + o_intra

    S, o = lax.scan(step, s0, (chunks(q), chunks(k), chunks(v), chunks(log_f)))
    return jnp.moveaxis(o, 0, 1).reshape(B, L, H, DV), S

def _hgrn2_bidir(q, v, gates, init_states):
    (k_f, lf_f), (k_b, lf_b) = gates
    rev = lambda t: jnp.flip(t, axis=1)
    o_f, s_f = _hgrn2_scan(q, k_f, v, lf_f, init_states[0])
    o_b, s_b = _hgrn2_scan(rev(q), rev(k_b), rev(v), rev(lf_b), init_states[1])
    return o_f + rev(o_b), (s_f, s_b)

def _hgrn2_mixer(h_lat, h_ctx, w_in, lb, o_gain, w_out):
    def project(h):
        B, L, _ = h.shape
        heads = lambda t: t.reshape(B, L, HG_HEADS, HG_HEAD_DIM)
        q, i_in, f_fw, f_bw, z = jnp.split(h @ w_in, 5, axis=-1)
        gates = []
        for d, g in enumerate((f_fw, f_bw)):
            lbd = lb[d]
            gf = g.astype(jnp.float32)
            log_f = jnp.logaddexp(jnp.log(lbd), jnp.log1p(-lbd) + jax.nn.log_sigmoid(gf))
            k = (1.0 - lbd) * jax.nn.sigmoid(-gf)
            gates.append((heads(k), heads(log_f)))
        return heads(jax.nn.silu(q)), heads(i_in), gates, z

    def readout(o, z):
        B, L = o.shape[:2]
        o = _rmsnorm(o, o_gain).reshape(B, L, D_INNER).astype(z.dtype)
        return (o * jax.nn.silu(z)) @ w_out

    Bsz = h_lat.shape[0]
    s0 = jnp.zeros((Bsz, HG_HEADS, HG_HEAD_DIM, HG_HEAD_DIM), jnp.float32)
    q_c, v_c, gates_c, z_c = project(h_ctx)
    o_c, ctx_states = _hgrn2_bidir(q_c, v_c, gates_c, (s0, s0))
    q_l, v_l, gates_l, z_l = project(h_lat)
    o_l, _ = _hgrn2_bidir(q_l, v_l, gates_l, ctx_states)
    return readout(o_l, z_l), readout(o_c, z_c)

def _attend(q_nope, q_pe, k_nope, k_pe, v):
    s = (jnp.einsum('bqhd,bkhd->bhqk', q_nope, k_nope, preferred_element_type=jnp.float32)
         + jnp.einsum('bqhr,bkr->bhqk', q_pe, k_pe, preferred_element_type=jnp.float32))
    p = jax.nn.softmax(s * MLA_SCALE, axis=-1)
    return jnp.einsum('bhqk,bkhd->bqhd', p.astype(v.dtype), v)

def _blocked_attend(q_nope, q_pe, k_nope, k_pe, v):
    B, L, H, _ = q_nope.shape
    n = L // Q_BLOCK
    blk = lambda t: jnp.moveaxis(t.reshape(B, n, Q_BLOCK, H, t.shape[-1]), 1, 0)
    o = lax.map(lambda qs: _attend(qs[0], qs[1], k_nope, k_pe, v), (blk(q_nope), blk(q_pe)))
    return jnp.moveaxis(o, 0, 1).reshape(B, L, H, v.shape[-1])

def _mla_mixer(h_lat, h_ctx, w_in, qa_norm, w_qb, kva_norm, w_kvb, w_out, cos, sin, need_ctx):
    splits = [MLA_Q_RANK, MLA_Q_RANK + MLA_KV_RANK, MLA_Q_RANK + MLA_KV_RANK + MLA_ROPE_DIM]

    def queries(q_a):
        B, L, _ = q_a.shape
        q = (_rmsnorm(q_a, qa_norm) @ w_qb).reshape(B, L, MLA_HEADS, MLA_NOPE_DIM + MLA_ROPE_DIM)
        return q[..., :MLA_NOPE_DIM], q[..., MLA_NOPE_DIM:]

    def keys_values(kv_a):
        B, L, _ = kv_a.shape
        kv = (_rmsnorm(kv_a, kva_norm) @ w_kvb).reshape(B, L, MLA_HEADS, MLA_NOPE_DIM + MLA_V_DIM)
        return kv[..., :MLA_NOPE_DIM], kv[..., MLA_NOPE_DIM:]

    def readout(o, z):
        B, L = o.shape[:2]
        return (o.reshape(B, L, D_INNER) * jax.nn.silu(z)) @ w_out

    q_a, kv_a, k_pe, z = jnp.split(h_lat @ w_in, splits, axis=-1)
    q_nope, q_pe = queries(q_a)
    q_pe = _apply_rope(q_pe, cos[None, :, None, :], sin[None, :, None, :])
    k_pe = _apply_rope(k_pe, cos[None], sin[None])
    k_nope, v = keys_values(kv_a)

    if need_ctx:
        qc_a, kvc_a, kc_pe, z_c = jnp.split(h_ctx @ w_in, splits, axis=-1)
    else:
        kvc_a, kc_pe = jnp.split(h_ctx @ w_in[:, splits[0]:splits[2]], [MLA_KV_RANK], axis=-1)
    kc_nope, v_c = keys_values(kvc_a)

    o_lat = _blocked_attend(q_nope, q_pe,
                            jnp.concatenate([kc_nope, k_nope], axis=1),
                            jnp.concatenate([kc_pe, k_pe], axis=1),
                            jnp.concatenate([v_c, v], axis=1))
    y_lat = readout(o_lat, z)
    y_ctx = None
    if need_ctx:
        qc_nope, qc_pe = queries(qc_a)
        y_ctx = readout(_attend(qc_nope, qc_pe, kc_nope, kc_pe, v_c), z_c)
    return y_lat, y_ctx

def second_inputs(seed: int = 0) -> dict:
    key = jax.random.key(seed)
    ks = jax.random.split(key, 20)
    f32 = jnp.float32

    def w(k, shape, fan_in):
        return jax.random.normal(k, shape, f32) * fan_in ** -0.5

    def gain(k, shape):
        return 1.0 + 0.1 * jax.random.normal(k, shape, f32)

    mla_in = MLA_Q_RANK + MLA_KV_RANK + MLA_ROPE_DIM + D_INNER
    return {
        "x": jax.random.normal(ks[0], (BATCH, SEQ, D_MODEL), f32),
        "c": jax.random.normal(ks[1], (BATCH, D_MODEL), f32),
        "ctx": jax.random.normal(ks[2], (BATCH, CTX_LEN, D_MODEL), f32),
        "c_ctx": jax.random.normal(ks[3], (D_MODEL,), f32),
        "ada_w": w(ks[4], (DEPTH, D_MODEL, 3 * D_MODEL), D_MODEL),
        "ada_b": 0.02 * jax.random.normal(ks[5], (DEPTH, 3 * D_MODEL), f32),
        "norm_pre": gain(ks[6], (DEPTH, D_MODEL)),
        "norm_post": gain(ks[7], (DEPTH, D_MODEL)),
        "hg_w_in": w(ks[8], (N_HG_LAYERS, D_MODEL, 5 * D_INNER), D_MODEL),
        "hg_lb_logits": jax.random.normal(ks[9], (N_HG_LAYERS, 2, D_INNER), f32),
        "hg_o_norm": gain(ks[10], (N_HG_LAYERS, HG_HEAD_DIM)),
        "hg_w_out": w(ks[11], (N_HG_LAYERS, D_INNER, D_MODEL), D_INNER),
        "mla_w_in": w(ks[12], (N_MLA_LAYERS, D_MODEL, mla_in), D_MODEL),
        "mla_qa_norm": gain(ks[13], (N_MLA_LAYERS, MLA_Q_RANK)),
        "mla_w_qb": w(ks[14], (N_MLA_LAYERS, MLA_Q_RANK, MLA_HEADS * (MLA_NOPE_DIM + MLA_ROPE_DIM)), MLA_Q_RANK),
        "mla_kva_norm": gain(ks[15], (N_MLA_LAYERS, MLA_KV_RANK)),
        "mla_w_kvb": w(ks[16], (N_MLA_LAYERS, MLA_KV_RANK, MLA_HEADS * (MLA_NOPE_DIM + MLA_V_DIM)), MLA_KV_RANK),
        "mla_w_out": w(ks[17], (N_MLA_LAYERS, D_INNER, D_MODEL), D_INNER),
    }

def second_block(x, c, ctx, c_ctx, ada_w, ada_b, norm_pre, norm_post,
              hg_w_in, hg_lb_logits, hg_o_norm, hg_w_out,
              mla_w_in, mla_qa_norm, mla_w_qb, mla_kva_norm, mla_w_kvb, mla_w_out):
    cos, sin = _axial_rope(x.shape[1])
    p = jax.nn.softmax(hg_lb_logits.astype(jnp.float32), axis=0)
    lower_bounds = jnp.cumsum(p, axis=0) - p[0:1]
    silu_c = jax.nn.silu(c)
    silu_cc = jax.nn.silu(c_ctx)
    x_lat, x_ctx = x, ctx
    for i in range(DEPTH):
        need_ctx = i < DEPTH - 1
        j = i // N_MIXERS
        mod_lat = (silu_c @ ada_w[i] + ada_b[i])[:, None, :]
        mod_ctx = silu_cc @ ada_w[i] + ada_b[i]
        sh_l, sc_l, gt_l = jnp.split(mod_lat, 3, axis=-1)
        sh_c, sc_c, gt_c = jnp.split(mod_ctx, 3, axis=-1)
        h_lat = _rmsnorm(x_lat, norm_pre[i]) * (1.0 + sc_l) + sh_l
        h_ctx = _rmsnorm(x_ctx, norm_pre[i]) * (1.0 + sc_c) + sh_c
        if i % N_MIXERS == 0:
            y_lat, y_ctx = _hgrn2_mixer(h_lat, h_ctx, hg_w_in[j], lower_bounds[j],
                                        hg_o_norm[j], hg_w_out[j])
        else:
            y_lat, y_ctx = _mla_mixer(h_lat, h_ctx, mla_w_in[j], mla_qa_norm[j], mla_w_qb[j],
                                      mla_kva_norm[j], mla_w_kvb[j], mla_w_out[j],
                                      cos, sin, need_ctx)
        x_lat = x_lat + gt_l * _rmsnorm(y_lat, norm_post[i])
        if need_ctx:
            x_ctx = x_ctx + gt_c * _rmsnorm(y_ctx, norm_post[i])
    return x_lat


def setup_inputs(seed=0):
    out = dict(first_inputs(seed))
    for name, value in second_inputs(seed + 1).items():
        if name != "x":
            out[name + "_2"] = value
    return out


def reference(
    x, c, ctx, c_ctx, ada_w, ada_b, norm1_g, norm2_g, ffn_w_in, ffn_w_out, even_w_in,
    even_w_out, sgu_w, sgu_b, diff_lq1, diff_lk1, diff_lq2, diff_lk2, diff_subln_g, odd_w_qkv,
    odd_w_out, odd_sink, final_g, c_2, ctx_2, c_ctx_2, ada_w_2, ada_b_2, norm_pre_2,
    norm_post_2, hg_w_in_2, hg_lb_logits_2, hg_o_norm_2, hg_w_out_2, mla_w_in_2, mla_qa_norm_2,
    mla_w_qb_2, mla_kva_norm_2, mla_w_kvb_2, mla_w_out_2,
):
    x = first_block(
        x, c, ctx, c_ctx, ada_w, ada_b, norm1_g, norm2_g, ffn_w_in, ffn_w_out, even_w_in,
        even_w_out, sgu_w, sgu_b, diff_lq1, diff_lk1, diff_lq2, diff_lk2, diff_subln_g,
        odd_w_qkv, odd_w_out, odd_sink, final_g,
    )
    return second_block(
        x, c_2, ctx_2, c_ctx_2, ada_w_2, ada_b_2, norm_pre_2, norm_post_2, hg_w_in_2,
        hg_lb_logits_2, hg_o_norm_2, hg_w_out_2, mla_w_in_2, mla_qa_norm_2, mla_w_qb_2,
        mla_kva_norm_2, mla_w_kvb_2, mla_w_out_2,
    )


_drawn_inputs = setup_inputs


def setup_inputs(seed=0):
    import zlib

    import numpy as np

    out = dict(_drawn_inputs(seed))
    spreads = {}
    factors = {'norm1_g': 8.0,
     'norm2_g': 6.494,
     'sgu_b': 3.498,
     'diff_lq1': 200.0,
     'diff_lk1': 4.092,
     'diff_lq2': 4.177,
     'diff_subln_g': 8.0,
     'odd_sink': 8.0,
     'final_g': 2.7,
     'mla_qa_norm_2': 3.384,
     'ada_b_2': 3.043}
    for name, (base, spread) in spreads.items():
        noise = np.random.default_rng([zlib.crc32(name.encode()), seed]).standard_normal(out[name].shape)
        drawn = base * np.exp(spread * noise) if base else spread * noise
        out[name] = __import__('jax').numpy.asarray(drawn.astype(out[name].dtype))
    for name, factor in factors.items():
        out[name] = (out[name] * factor).astype(out[name].dtype)
    return out
```

```python
from contextlib import ExitStack
import math

import concourse.bass as bass
from concourse import mybir

F32 = mybir.dt.float32
U8 = mybir.dt.uint8
ALU = mybir.AluOpType
ACT = mybir.ActivationFunctionType
AX_X = mybir.AxisListType.X

P = 128
D = 1024
DC = D // P
LAT, CTX = 512, 256
T = LAT + CTX
NT = T // P
QT = LAT // P
HID = 2816
HC = HID // P
EPS = 1e-6
HEAD = 64
SCALE = HEAD ** -0.5
LAM_INIT = 0.8 - 0.6 * math.exp(0.0)
HEADS = 16
MLA_SCALE = (128 + 64) ** -0.5
LEVELS = 7
NEG = -1e30
RA, RB = 4, 5

SMALL = {}
_at = 0
for _name, _n in (("cvec", 16), ("cvec2", 16), ("ada_b", 288), ("norm1_g", 32), ("norm2_g", 32), ("final_g", 8),
                  ("norm_pre", 32), ("norm_post", 32), ("subln", 1), ("lamv", 4), ("sink", 16), ("lbl", 32),
                  ("o_norm", 1), ("qa_norm", 2), ("kva_norm", 1)):
    SMALL[_name] = (_at, _at + _n)
    _at += _n
N_SMALL = _at
CONST = {}
_at = 0
for _name, _n in (("ident", 128), ("ones", 128), ("rot128", 128), ("rot64", 128), ("cos128", LAT), ("sin128", LAT),
                  ("cos64", LAT), ("sin64", LAT), ("maskl", 128), ("maskr", 128)):
    CONST[_name] = (_at, _at + _n)
    _at += _n
N_CONST = _at

PLAN_A = [("ada1", 24, 4), ("ada2", 12, 4),
          ("even_out", 2, 4), ("ffn_in0", 11, 4), ("ffn_out0", 2, 12),
          ("odd", 4, 4), ("odd_out", 2, 4), ("ffn_in1", 11, 4), ("ffn_out1", 2, 12),
          ("hg_out", 4, 4), ("mla_low", 1, 4), ("mla", 8, 4), ("mla_out", 4, 4)]
PLAN_B = [("even", 4, 5), ("hg", 16, 5)]
ORDER = ["ada1", "ada2", "even", "even_out", "ffn_in0", "ffn_out0", "odd", "odd_out", "ffn_in1", "ffn_out1",
         "hg", "hg_out", "mla_low", "mla", "mla_out"]


def starts(plan):
    at, out = 0, {}
    for name, iters, per in plan:
        out[name] = at
        at += iters * per
    return out, at


START_A, N_A = starts(PLAN_A)
START_B, N_B = starts(PLAN_B)
COUNT = {name: (iters, per) for name, iters, per in PLAN_A + PLAN_B}

MOD = {}
for _l in range(2):
    for _i, _name in enumerate(("sh1", "sc1", "g1", "sh2", "sc2", "g2")):
        MOD[_name, _l] = 48 * _l + 8 * _i
    for _i, _name in enumerate(("sh", "sc", "gt")):
        MOD[_name, _l] = 96 + 24 * _l + 8 * _i


def build(nc, streamA, streamB, x_in, ctx2_in, smalls_in, consts_in, lvl_in, sgu_in, out):
    with ExitStack() as ctx:
        def sb(name, shape, dt=F32):
            return ctx.enter_context(nc.sbuf_tensor(name, shape, dt))

        sems = {}

        def sem(name):
            if name not in sems:
                sems[name] = ctx.enter_context(nc.semaphore(name))
            return sems[name]

        x = sb("x", [P, DC, T])
        a = sb("a", [P, DC, T])
        ringA = sb("ringA", [P, RA, D])
        ringB = sb("ringB", [P, RB, D])
        sq = sb("sq", [P, 2, T])
        rstd = sb("rstd", [P, T])
        consts = sb("consts", [P, N_CONST])
        smalls = sb("smalls", [P, N_SMALL])
        mod = sb("mod", [P, 144, 2])
        coef = sb("coef", [P, DC, 2])
        svec = sb("svec", [P, 32])
        st = sb("st", [P, 64])
        lvl = sb("lvl", [P, 2 * LEVELS, NT * 64], U8)
        FREE = 23808
        arena = sb("arena", [P, FREE])
        ps = ctx.enter_context(nc.psum_tensor("ps", [P, 8, 512], F32))
        psf = ps[:].rearrange("p b n -> p (b n)")

        def C(name):
            return consts[:, CONST[name][0]:CONST[name][1]]

        def SM(name):
            return smalls[:, SMALL[name][0]:SMALL[name][1]]

        ident, ones = C("ident"), C("ones")

        def carve():
            at = [0]

            def take(*shape):
                n = math.prod(shape)
                v = arena[:, at[0]:at[0] + n]
                at[0] += n
                assert at[0] <= FREE, at[0]
                if len(shape) == 2:
                    v = v.rearrange("p (a b) -> p a b", b=shape[1])
                elif len(shape) == 3:
                    v = v.rearrange("p (a b c) -> p a b c", b=shape[1], c=shape[2])
                return v
            return take

        def flat(ap):
            return ap.rearrange("p a t -> p (a t)")

        def one(ap, g, j):
            return ap[:, bass.ds(g, 1), j, :].rearrange("p a t -> p (a t)")

        landedA = [sem(f"landedA{s}") for s in range(RA)]
        landedB = [sem(f"landedB{s}") for s in range(RB)]
        readA, readB = sem("readA"), sem("readB")

        def readA_after(name, g, k):
            return RA + START_A[name] + g * COUNT[name][1] + k + 1

        def readB_after(name, g, k):
            return RB + START_B[name] + g * RB + k + 1

        def landedA_at(name, g, k):
            return 16 * ((START_A[name] + k) // RA + 1) + g * (16 * COUNT[name][1] // RA)

        def landedB_at(name, g):
            return 16 * (START_B[name] // RB + 1) + g * 16

        tk = carve()
        hidden, sg = tk(HC, T), tk(2, T)
        hidden_g = hidden.rearrange("p (g j) t -> p g j t", j=2)
        tk = carve()
        E = dict(cat=tk(DC, T), u=tk(T), q=tk(T), k=tk(T), vT=tk(T), vvT=tk(T), vtok=tk(NT, P), vvtok=tk(NT, P),
                 tmp=tk(2, LAT), p=tk(4, T), pT=tk(NT, LAT), pTc=tk(2, CTX), osq=tk(T), ro=tk(T), bst=tk(NT, 6),
                 mv=tk(NT, 2), lstd=tk(NT), sguw=tk(4, P), sgub=tk(4, P), mix=tk(T), lam=tk(8))
        lvl_f = arena[:, FREE - 2 * LEVELS * 64:FREE].rearrange("p (l j) -> p l j", j=64)
        tk = carve()
        O = dict(q=tk(2, LAT), k=tk(T), vT=tk(T), vtok=tk(NT, HEAD), p=tk(2, 640), pT=tk(2, 5 * P), o=tk(DC, LAT),
                 tmp=tk(3, LAT))
        tk = carve()
        H = dict(og=tk(HEADS, T), q=tk(T), z=tk(T), P=tk(2, T), k=tk(2, T), S=tk(2, T), v=tk(NT, P),
                 ql=tk(4, T // 2), kl=tk(4, T), A=rstd[:].rearrange("p (n c) -> p n c", c=P))
        tk = carve()
        M = dict(og=tk(HEADS, LAT), qa=tk(2, LAT), kva=tk(T), kpe=tk(T), qn=tk(LAT), qp=tk(LAT), kn=tk(T), v=tk(NT, P),
                 z=tk(LAT), p=tk(2, T), pT=tk(NT, LAT), tmp=tk(LAT), qsq=tk(2, LAT), kvsq=tk(T), rq=tk(LAT), rk=tk(T))
        lbs = sb("lbs", [P, 4, 32])

        def pieces(width):
            return [(0, LAT, 0)] + ([(LAT, CTX, 1)] if width == T else [])

        NORMS = [("norm1_g", 0, "sc1", "sh1", T), ("norm2_g", 0, "sc2", "sh2", T),
                 ("norm1_g", 1, "sc1", "sh1", T), ("norm2_g", 1, "sc2", "sh2", LAT),
                 ("final_g", 0, None, None, LAT),
                 ("norm_pre", 0, "sc", "sh", T), ("norm_post", 0, None, "gt", T),
                 ("norm_pre", 1, "sc", "sh", T), ("norm_post", 1, None, "gt", LAT)]
        MODULATED = [0, 1, 2, 3, 5, 7]
        X_READY = {1: 1, 2: 2, 3: 3, 4: 4, 5: 5, 7: 6}
        CHUNKS = [[4, 5, 0, 1, 2, 3], [5, 4, 3, 2, 1, 0]]

        def ktok(d):
            return H["ql"][:, 2 * d:2 * d + 2, :].rearrange("p a (b c) -> p (a b) c", c=P)

        def state(d, i):
            at = (d * 5 + i) * P
            return sq[:].rearrange("p a t -> p (a t)")[:, at:at + P]

        def one_col(ap, g, j):
            return ap.rearrange("p (g j) -> p g j", j=4)[:, bass.ds(g, 1), j]

        block = ctx.enter_context(nc.Block())

        @block.sync
        def _(sp):
            sp.dma_start(smalls[:], smalls_in).then_inc(sem("smalls_in"), 16)
            sp.dma_start(x[:], x_in).then_inc(sem("x_in"), 16)
            sp.dma_start(consts[:], consts_in).then_inc(sem("consts_in"), 16)
            sp.dma_start(lvl_f, lvl_in).then_inc(sem("lvl_in"), 16)
            sp.dma_start(E["sguw"].rearrange("p a b -> p (a b)"), sgu_in[:, 0:512]).then_inc(sem("sgu_in"), 16)
            sp.dma_start(E["sgub"].rearrange("p a b -> p (a b)"), sgu_in[:, 512:1024]).then_inc(sem("sgu_in"), 16)
            groupsA = streamA.rearrange("(g s) p n -> g s p n", s=RA)
            groupsB = streamB.rearrange("(g s) p n -> g s p n", s=RB)
            for name in ORDER:
                iters, per = COUNT[name]
                if name in START_A:
                    first = START_A[name] // RA
                    with sp.Fori(first, first + iters * per // RA) as g:
                        for s in range(RA):
                            sp.wait_ge(readA, g * RA + s + 1)
                            sp.dma_start(ringA[:, s, :], groupsA[bass.ds(g, 1), s].rearrange("a p n -> (a p) n")) \
                                .then_inc(landedA[s], 16)
                else:
                    first = START_B[name] // RB
                    with sp.Fori(first, first + iters) as g:
                        for s in range(RB):
                            sp.wait_ge(readB, g * RB + s + 1)
                            sp.dma_start(ringB[:, s, :], groupsB[bass.ds(g, 1), s].rearrange("a p n -> (a p) n")) \
                                .then_inc(landedB[s], 16)
            sp.wait_ge(sem("x_ready"), 7)
            sp.dma_start(out, x[:, :, 0:LAT]).then_inc(sem("stored"), 16)
            sp.wait_ge(sem("stored"), 16)

        @block.gpsimd
        def _(pool):
            pool.wait_ge(sem("lvl_in"), 16)
            for n in range(NT):
                nc.gpsimd.tensor_copy(lvl[:].rearrange("p l (n j) -> p l n j", j=64)[:, :, n, :], lvl_f) \
                    .then_inc(sem("lvl_ready"), 1)

        @block.tensor
        def _(pe):
            pe.sem_inc(readA, RA)
            pe.sem_inc(readB, RB)

            def product(ring, slot, src, bank, width, kc=DC, k0=0, start=True, stop=True, m=P, w0=0):
                for k in range(kc):
                    for t0, tn, half in pieces(width):
                        mm = nc.tensor.matmul(ps[0:m, bank + half, 0:tn], ring[:, slot, w0 + k * P:w0 + k * P + m],
                                              src[:, k0 + k, t0:t0 + tn], start=start and k == 0,
                                              stop=stop and k == kc - 1)
                return mm

            def norm_stats(n):
                for c in range(DC):
                    pe.wait_ge(sem("sq_ready"), DC * n + c + 1)
                    for t0, tn, half in pieces(NORMS[n][4]):
                        mm = nc.tensor.matmul(ps[:, half, 0:tn], ones, sq[:, c % 2, t0:t0 + tn],
                                              start=c == 0, stop=c == DC - 1)
                    mm.then_inc(sem("stat_done"), 1)

            def a_wait(n):
                pe.wait_ge(sem("a_ready"), MODULATED.index(n) + 1)

            def ada(name, vec):
                iters, _ = COUNT[name]
                with pe.Fori(0, iters) as g:
                    for s in range(RA):
                        pe.wait_ge(landedA[s], landedA_at(name, g, s))
                        pe.wait_ge(sem(name + "_free"), g * RA + s + 1)
                        for k in range(DC):
                            mm = nc.tensor.matmul(ps[:, s, 0:2], ringA[:, s, k * P:(k + 1) * P],
                                                  svec[:, vec + 2 * k:vec + 2 * k + 2], start=k == 0, stop=k == DC - 1)
                        mm.then_inc(readA, 1)

            def out_product(name, src, width, per_n):
                iters, per = COUNT[name]
                J = per // per_n
                kall = src.shape[1]
                with pe.Fori(0, iters) as g:
                    for j in range(J):
                        pe.wait_ge(sem(name + "_free"), g * J + j + 1)
                        for i in range(per_n):
                            k = j * per_n + i
                            kc = min(DC, kall - i * DC)
                            pe.wait_ge(landedA[k % RA], landedA_at(name, g, k))
                            product(ringA, k % RA, src, 2 * j, width, kc=kc, k0=i * DC, start=i == 0,
                                    stop=i == per_n - 1).then_inc(readA, 1)

            def ffn_in(l, width):
                name = f"ffn_in{l}"
                with pe.Fori(0, COUNT[name][0]) as g:
                    for s in range(RA):
                        pe.wait_ge(landedA[s], landedA_at(name, g, s))
                        pe.wait_ge(sem(f"ffn{l}_" + ("up_free" if s % 2 else "gate_free")), g * 2 + s // 2 + 1)
                        product(ringA, s, a, 2 * s, width).then_inc(readA, 1)

            def even():
                name = "even"
                pe.wait_ge(sem("consts_in"), 16)
                pe.wait_ge(sem("lam_prod"), 1)
                nc.tensor.matmul(ps[:, 2, 0:2], ones, E["lam"][:, 0:2], start=True, stop=True).then_inc(sem("lam_sum"), 1)
                a_wait(0)
                with pe.Fori(0, 4) as g:
                    for s, (bank, done) in enumerate(((0, "ev_u"), (2, "ev_q"), (4, "ev_k"), (6, "ev_v"), (0, "ev_vv"))):
                        pe.wait_ge(landedB[s], landedB_at(name, g))
                        if s == 0:
                            pe.wait_ge(sem("ev_free"), g + 1)
                        if s == 4:
                            pe.wait_ge(sem("ev_act"), g * 12 + 1)
                        product(ringB, s, a, bank, T).then_inc(readB, 1)
                    for i, (bank, src) in enumerate(((2, "q"), (4, "k"))):
                        pe.wait_ge(sem("ev_act"), g * 12 + 2 + i)
                        nc.tensor.matmul(ps[:, bank, :], C("rot128"), E[src][:, 0:LAT], start=True, stop=True) \
                            .then_inc(sem("ev_rot"), 1)
                    pe.wait_ge(sem("ev_act"), g * 12 + 4)
                    for n in range(NT):
                        mm = nc.tensor.transpose(psf[:, 6 * 512 + n * P:6 * 512 + (n + 1) * P],
                                                 E["vT"][:, n * P:(n + 1) * P], ident)
                    mm.then_inc(sem("ev_tr"), 1)
                    pe.wait_ge(sem("ev_act"), g * 12 + 5)
                    for n in range(NT):
                        mm = nc.tensor.transpose(psf[:, n * P:(n + 1) * P], E["vvT"][:, n * P:(n + 1) * P], ident)
                    mm.then_inc(sem("ev_tr"), 1)
                    pe.wait_ge(sem("ev_vn"), g + 1)
                    pe.wait_ge(sem("sgu_in"), 32)
                    for n in range(NT):
                        mm = nc.tensor.matmul(psf[:, 6 * 512 + n * P:6 * 512 + (n + 1) * P], E["vtok"][:, n, :],
                                              flat(E["sguw"][:, bass.ds(g, 1), :]), start=True, stop=True)
                    mm.then_inc(sem("ev_mix"), 1)

                    def scores(u):
                        if u == 0:
                            pe.wait_ge(sem("ev_rope"), g + 1)
                            pe.wait_ge(sem("ev_act"), g * 12 + 6)
                        else:
                            pe.wait_ge(sem("ev_exp"), g * 12 + 2 * u)
                        for half in range(2):
                            r = slice(half * HEAD, (half + 1) * HEAD)
                            lhs = E["q"][r, u * P:(u + 1) * P]
                            if u < QT:
                                nc.tensor.matmul(ps[:, 2 * half, :], lhs, E["k"][r, 0:LAT], start=True, stop=True)
                            mm = nc.tensor.matmul(ps[:, 2 * half + 1, 0:CTX], lhs, E["k"][r, LAT:T], start=True, stop=True)
                        mm.then_inc(sem("ev_sc"), 1)

                    def turn(u):
                        pe.wait_ge(sem("ev_p"), g * 6 + u + 1)
                        if u > 0:
                            pe.wait_ge(sem("ev_act"), g * 12 + 6 + u)
                        for n in range(0 if u < QT else QT, NT):
                            mm = nc.tensor.transpose(psf[:, 4 * 512 + n * P:4 * 512 + (n + 1) * P],
                                                     E["p"][:, 2 * (u % 2), n * P:(n + 1) * P], ident)
                        mm.then_inc(sem("ev_tr2"), 1)

                    scores(0)
                    for u in range(6):
                        if u < 5:
                            scores(u + 1)
                        turn(u)
                        if u == 4:
                            pe.wait_ge(sem("ev_cat"), g + 1)
                            pe.wait_ge(sem("ev_act"), g * 12 + 10)
                            for n in range(NT):
                                mm = nc.tensor.matmul(ps[:, 6, :], E["vvtok"][:, n, :], E["pT"][:, n, :],
                                                      start=n == 0, stop=n == NT - 1)
                    pe.wait_ge(sem("ev_act"), g * 12 + 12)
                    for n in range(2):
                        mm = nc.tensor.matmul(ps[:, 7, 0:CTX], E["vvtok"][:, QT + n, :], E["pTc"][:, n, :],
                                              start=n == 0, stop=n == 1)
                    mm.then_inc(sem("ev_pv"), 1)
                    pe.wait_ge(sem("ev_osq"), g + 1)
                    for t0, tn, half in pieces(T):
                        mm = nc.tensor.matmul(ps[:, 4 + half, 0:tn], ones, E["osq"][:, t0:t0 + tn], start=True, stop=True)
                    mm.then_inc(sem("ev_ms"), 1)
                pe.wait_ge(sem("cat_ready"), 1)

            def odd():
                name = "odd"
                a_wait(2)
                with pe.Fori(0, 4) as g:
                    for s, (bank, width) in enumerate(((0, LAT), (1, LAT), (2, T), (4, T))):
                        pe.wait_ge(landedA[s], landedA_at(name, g, s))
                        if s == 0:
                            pe.wait_ge(sem("od_free"), g + 1)
                        product(ringA, s, a, bank, width, m=HEAD if s == 3 else P).then_inc(readA, 1)
                    for i, src in enumerate((O["q"][:, 0, :], O["q"][:, 1, :], O["k"][:, 0:LAT])):
                        pe.wait_ge(sem("od_cp"), g * 5 + i + 1 + i // 2)
                        nc.tensor.matmul(ps[:, i, :], C("rot128"), src, start=True, stop=True).then_inc(sem("od_rot"), 1)
                    for n in range(NT):
                        mm = nc.tensor.transpose(ps[:, 4, n * HEAD:(n + 1) * HEAD], O["vT"][0:HEAD, n * P:(n + 1) * P],
                                                 ident[0:HEAD, 0:HEAD])
                    mm.then_inc(sem("od_vtr"), 1)

                    def scores(u):
                        hh, qt = divmod(u, QT)
                        r = slice((hh % 2) * HEAD, (hh % 2 + 1) * HEAD)
                        lo, hi = max(0, qt - 1) * P, min(QT, qt + 2) * P
                        b, w = 2 * (u % 2), hi - lo
                        lhs = O["q"][r, hh // 2, qt * P:(qt + 1) * P]
                        if u == 0:
                            pe.wait_ge(sem("od_rope"), g + 1)
                        if u >= 2:
                            pe.wait_ge(sem("od_exp"), g * 16 + u - 1)
                        nc.tensor.matmul(ps[:, b, 512 - w:512], lhs, O["k"][r, lo:hi], start=True, stop=False,
                                         skip_group_check=True)
                        if qt > 0:
                            nc.tensor.matmul(ps[:, b, 512 - w:512 - w + P], ident, C("maskl"), start=False, stop=qt == QT - 1,
                                             skip_group_check=True)
                        if qt < QT - 1:
                            nc.tensor.matmul(ps[:, b, 512 - P:512], ident, C("maskr"), start=False, stop=True,
                                             skip_group_check=True)
                        nc.tensor.matmul(ps[:, b + 1, 0:CTX], lhs, O["k"][r, LAT:T], start=True, stop=True) \
                            .then_inc(sem("od_sc"), 1)

                    def turn(u):
                        qt = u % QT
                        w = (min(QT, qt + 2) - max(0, qt - 1)) * P
                        pe.wait_ge(sem("od_p"), g * 16 + u + 1)
                        if u == 0:
                            pe.wait_ge(sem("od_cp"), g * 5 + 5)
                        else:
                            pe.wait_ge(sem("od_pt"), g * 16 + u)
                        for n in range((w + CTX) // P):
                            mm = nc.tensor.transpose(psf[:, 4 * 512 + n * P:4 * 512 + (n + 1) * P],
                                                     O["p"][:, u % 2, n * P:(n + 1) * P], ident)
                        mm.then_inc(sem("od_tr"), 1)

                    def values(u):
                        hh, qt = divmod(u, QT)
                        lo, hi = max(0, qt - 1), min(QT, qt + 2)
                        keys = list(range(lo, hi)) + [QT, QT + 1]
                        r = slice((hh % 2) * HEAD, (hh % 2 + 1) * HEAD)
                        pe.wait_ge(sem("od_pt"), g * 16 + u + 1)
                        for n, key in enumerate(keys):
                            mm = nc.tensor.matmul(ps[r, 6 + hh // 2, qt * P:(qt + 1) * P], O["vtok"][:, key, :],
                                                  O["pT"][:, u % 2, n * P:(n + 1) * P], start=n == 0,
                                                  stop=n == len(keys) - 1)
                        mm.then_inc(sem("od_pv"), 1)

                    scores(0)
                    for u in range(16):
                        if u < 15:
                            scores(u + 1)
                        turn(u)
                        if u > 0:
                            values(u - 1)
                    values(15)
                pe.wait_ge(sem("o_ready"), 1)

            def hgrn():
                name = "hg"
                a_wait(5)
                with pe.Fori(0, HEADS) as g:
                    for s, bank in enumerate((0, 2, 4, 6, 0)):
                        pe.wait_ge(landedB[s], landedB_at(name, g))
                        if s == 0:
                            pe.wait_ge(sem("hg_free"), g + 1)
                        if s == 4:
                            pe.wait_ge(sem("hg_act"), g * 10 + 1)
                        product(ringB, s, a, bank, T).then_inc(readB, 1)
                    pe.wait_ge(sem("hg_act"), g * 10 + 2)
                    for n in range(NT):
                        mm = nc.tensor.transpose(psf[:, 2 * 512 + n * P:2 * 512 + (n + 1) * P],
                                                 H["kl"][:, 2, n * P:(n + 1) * P], ident)
                    mm.then_inc(sem("hg_vtr"), 1)
                    pe.wait_ge(sem("hg_ksum"), g + 1)
                    for n in range(NT):
                        mm = nc.tensor.matmul(psf[:, 4 * 512 + n * P:4 * 512 + (n + 1) * P], H["kl"][:, 0, n * P:(n + 1) * P],
                                              H["q"][:, n * P:(n + 1) * P], start=True, stop=True)
                    mm.then_inc(sem("hg_diag"), 1)
                    for i in range(LEVELS):
                        if i == 0:
                            pe.wait_ge(sem("hg_act"), g * 10 + 8)
                        for d in range(2):
                            pe.wait_ge(sem("hg_lvl"), (g * LEVELS + i) * 2 + d + 1)
                            if i >= 2:
                                pe.wait_ge(sem("hg_sel"), (g * LEVELS + i - 2) * 2 + d + 1)
                            buf = 2 * d + i % 2
                            for n in range(NT):
                                keys = H["k"][:, d, n * P:(n + 1) * P] if i == 0 else H["kl"][:, buf, n * P:(n + 1) * P]
                                mm = nc.tensor.matmul(ps[:, buf, n * HEAD:(n + 1) * HEAD], keys,
                                                      H["ql"][:, buf, n * HEAD:(n + 1) * HEAD], start=True, stop=True)
                            mm.then_inc(sem("hg_A"), 1)
                    for d in range(2):
                        pe.wait_ge(sem("hg_kS"), g * 2 + d + 1)
                        if d == 1:
                            pe.wait_ge(sem("hg_act"), g * 10 + 9)
                        for n in range(NT):
                            mm = nc.tensor.transpose(psf[:, 4 * 512 + n * P:4 * 512 + (n + 1) * P],
                                                     H["kl"][:, 2 * d + 1, n * P:(n + 1) * P], ident)
                        mm.then_inc(sem("hg_ktr"), 1)
                    pe.wait_ge(sem("hg_sel"), (g + 1) * LEVELS * 2)
                    for n in range(NT):
                        nc.tensor.matmul(psf[:, 6 * 512 + n * P:6 * 512 + (n + 1) * P], H["v"][:, n, :], H["A"][:, n, :],
                                         start=n % 4 == 0, stop=False, skip_group_check=True)
                    for d in range(2):
                        pe.wait_ge(sem("hg_act"), g * 10 + 9 + d)
                        for n in range(NT):
                            mm = nc.tensor.matmul(psf[:, 2 * d * 512 + n * P:2 * d * 512 + (n + 1) * P],
                                                  ktok(d)[:, n, :], H["v"][:, n, :], start=True, stop=True)
                        mm.then_inc(sem("hg_add"), 1)
                    for d in range(2):
                        for i, n in enumerate(CHUNKS[d][1:]):
                            pe.wait_ge(sem("hg_state"), (g * 2 + d) * 5 + i + 1)
                            mm = nc.tensor.matmul(psf[:, 6 * 512 + n * P:6 * 512 + (n + 1) * P], state(d, i),
                                                  H["kl"][:, 2 * d, n * P:(n + 1) * P], start=False,
                                                  stop=d == 1 and n in (0, 4), skip_group_check=True)
                    mm.then_inc(sem("hg_o"), 1)
                    pe.wait_ge(sem("hg_osq"), g + 1)
                    for t0, tn, half in pieces(T):
                        mm = nc.tensor.matmul(ps[:, 4 + half, 0:tn], ones, H["kl"][:, 0, t0:t0 + tn], start=True, stop=True)
                    mm.then_inc(sem("hg_ms"), 1)
                pe.wait_ge(sem("og_ready"), 1)

            def mla():
                a_wait(7)
                name = "mla_low"
                for s, (bank, width) in enumerate(((0, LAT), (1, LAT), (2, T), (4, T))):
                    pe.wait_ge(landedA[s], landedA_at(name, 0, s))
                    product(ringA, s, a, bank, width, m=HEAD if s == 3 else P).then_inc(readA, 1)
                pe.wait_ge(sem("ml_low"), 1)
                for k in range(2):
                    nc.tensor.matmul(ps[:, 0, :], ones, M["qsq"][:, k, :], start=k == 0, stop=k == 1)
                for t0, tn, half in pieces(T):
                    nc.tensor.matmul(ps[:, 2 + half, 0:tn], ones, M["kvsq"][:, t0:t0 + tn], start=True, stop=True)
                nc.tensor.matmul(ps[:, 4, :], C("rot64")[0:HEAD, :], M["kpe"][0:HEAD, 0:LAT], start=True, stop=True) \
                    .then_inc(sem("ml_lowms"), 1)
                pe.wait_ge(sem("ml_lown"), 1)
                name = "mla"
                with pe.Fori(0, HEADS // 2) as g:
                    for e in range(2):
                        h = g * 2 + e
                        s = 2 * e
                        pe.wait_ge(landedA[s], landedA_at(name, g, s))
                        pe.wait_ge(sem("ml_free"), h + 1)
                        product(ringA, s, a, 0, LAT).then_inc(readA, 1)
                        s += 1
                        pe.wait_ge(landedA[s], landedA_at(name, g, s))
                        W = ringA[:, s, :]
                        for k in range(2):
                            nc.tensor.matmul(ps[:, 1, :], W[:, k * P:(k + 1) * P], M["qa"][:, k, :], start=k == 0, stop=k == 1)
                        for k in range(2):
                            nc.tensor.matmul(ps[0:HEAD, 2, :], W[:, 256 + k * HEAD:256 + (k + 1) * HEAD], M["qa"][:, k, :],
                                             start=k == 0, stop=k == 1)
                        for t0, tn, half in pieces(T):
                            nc.tensor.matmul(ps[:, 4 + half, 0:tn], W[:, 384:512], M["kva"][:, t0:t0 + tn], start=True, stop=True)
                        for n in range(NT):
                            mm = nc.tensor.matmul(psf[:, 6 * 512 + n * P:6 * 512 + (n + 1) * P], M["kva"][:, n * P:(n + 1) * P],
                                                  W[:, 512:640], start=True, stop=True)
                        mm.then_inc(readA, 1)
                        pe.wait_ge(sem("ml_cp"), h * 5 + 1)
                        nc.tensor.matmul(ps[:, 3, :], C("rot64")[0:HEAD, :], M["qp"][0:HEAD, :], start=True, stop=True) \
                            .then_inc(sem("ml_rot"), 1)

                        def scores(u):
                            b = 2 * (u % 2)
                            if u == 0:
                                pe.wait_ge(sem("ml_cp"), h * 5 + 5)
                            if u == 0:
                                pe.wait_ge(sem("ml_rope"), h + 1)
                            if u >= 2:
                                pe.wait_ge(sem("ml_exp"), h * 4 + u - 1)
                            for t0, tn, half in pieces(T):
                                nc.tensor.matmul(ps[:, b + half, 0:tn], M["qn"][:, u * P:(u + 1) * P], M["kn"][:, t0:t0 + tn],
                                                 start=True, stop=False)
                                mm = nc.tensor.matmul(ps[:, b + half, 0:tn], M["qp"][0:HEAD, u * P:(u + 1) * P],
                                                      M["kpe"][0:HEAD, t0:t0 + tn], start=False, stop=True)
                            mm.then_inc(sem("ml_sc"), 1)

                        def turn(u):
                            pe.wait_ge(sem("ml_p"), h * 4 + u + 1)
                            if u > 0:
                                pe.wait_ge(sem("ml_pt"), h * 4 + u)
                            for n in range(NT):
                                mm = nc.tensor.transpose(psf[:, 4 * 512 + n * P:4 * 512 + (n + 1) * P],
                                                         M["p"][:, u % 2, n * P:(n + 1) * P], ident)
                            mm.then_inc(sem("ml_tr"), 1)

                        scores(0)
                        for u in range(QT):
                            if u < QT - 1:
                                scores(u + 1)
                            turn(u)
                        pe.wait_ge(sem("ml_pt"), h * 4 + 4)
                        for n in range(NT):
                            mm = nc.tensor.matmul(ps[:, 6, :], M["v"][:, n, :], M["pT"][:, n, :], start=n == 0, stop=n == NT - 1)
                        mm.then_inc(sem("ml_pv"), 1)
                pe.wait_ge(sem("ml_og"), 1)

            pe.wait_ge(sem("svec_ready"), 1)
            ada("ada1", 0)
            ada("ada2", 16)
            pe.wait_ge(sem("consts_in"), 16)
            pe.wait_ge(sem("ada2_free"), RA + 48)
            norm_stats(0)
            even()
            out_product("even_out", E["cat"], T, 1)
            norm_stats(1)
            a_wait(1)
            ffn_in(0, T)
            pe.wait_ge(sem("hidden_ready"), 1)
            out_product("ffn_out0", hidden, T, 3)
            norm_stats(2)
            odd()
            out_product("odd_out", O["o"], LAT, 1)
            norm_stats(3)
            a_wait(3)
            ffn_in(1, LAT)
            pe.wait_ge(sem("hidden_ready"), 2)
            out_product("ffn_out1", hidden, LAT, 3)
            norm_stats(4)
            norm_stats(5)
            hgrn()
            out_product("hg_out", H["og"], T, 2)
            norm_stats(6)
            norm_stats(7)
            mla()
            out_product("mla_out", M["og"], LAT, 2)
            norm_stats(8)

        @block.scalar
        def _(act):
            def norm_squares(n):
                _, _, _, _, width = NORMS[n]
                post = n in (6, 8)
                if n == 0:
                    act.wait_ge(sem("x_in"), 16)
                elif post:
                    act.wait_ge(sem("y_ready"), 1 + (n == 8))
                else:
                    act.wait_ge(sem("x_ready"), X_READY[n])
                if n == 5:
                    act.dma_start(x[:, :, LAT:T], ctx2_in).then_inc(sem("ctx2_in"), 16)
                    act.wait_ge(sem("ctx2_in"), 16)
                for c in range(DC):
                    if DC * n + c >= 2:
                        act.wait_ge(sem("stat_done"), DC * n + c - 1)
                    nc.scalar.activation(sq[:, c % 2, 0:width], (a if post else x)[:, c, 0:width], ACT.Square) \
                        .then_inc(sem("sq_ready"), 1)

            def norm_root(n):
                width = NORMS[n][4]
                act.wait_ge(sem("inv_ready"), n + 1)
                nc.scalar.activation(rstd[:, 0:width], rstd[:, 0:width], ACT.Sqrt).then_inc(sem("rstd_ready"), 1)

            def norm(n):
                norm_squares(n)
                norm_root(n)
                if n in MODULATED:
                    m = MODULATED.index(n)
                    shift = MOD[NORMS[n][3], NORMS[n][1]]
                    for c in range(DC):
                        act.wait_ge(sem("scaled"), DC * m + c + 1)
                        for t0, tn, v in pieces(NORMS[n][4]):
                            last = nc.scalar.activation(a[:, c, t0:t0 + tn], a[:, c, t0:t0 + tn], ACT.Identity,
                                                        bias=mod[:, shift + c, v:v + 1])
                    last.then_inc(sem("a_ready"), 1)

            def ffn_in(l, width):
                name = f"ffn_in{l}"
                act.sem_inc(sem(f"ffn{l}_gate_free"), 2)
                with act.Fori(0, COUNT[name][0]) as g:
                    for j in range(2):
                        act.wait_ge(readA, readA_after(name, g, 2 * j))
                        act.wait_ge(sem(f"ffn{l}_up_free"), g * 2 + j + 1)
                        nc.scalar.activation(sg[:, j, 0:width], psf[:, 4 * j * 512:4 * j * 512 + width], ACT.Silu) \
                            .then_inc(sem(f"ffn{l}_gate_free"), 1)

            def even():
                with act.Fori(0, 4) as g:
                    for s, (bank, dst, fn) in enumerate(((0, "u", ACT.Gelu), (2, "q", ACT.Copy), (4, "k", ACT.Copy),
                                                         (6, "vT", ACT.Gelu), (0, "vvT", ACT.Copy))):
                        act.wait_ge(readB, readB_after("even", g, s))
                        nc.scalar.activation(E[dst], psf[:, bank * 512:bank * 512 + T], fn).then_inc(sem("ev_act"), 1)
                    act.wait_ge(sem("ev_tr"), g * 2 + 2)
                    nc.scalar.activation(E["vvtok"].rearrange("p a b -> p (a b)"), psf[:, 0:T], ACT.Copy) \
                        .then_inc(sem("ev_act"), 1)
                    act.wait_ge(sem("ev_vinv"), g + 1)
                    nc.scalar.activation(E["lstd"], E["lstd"], ACT.Sqrt).then_inc(sem("ev_vstd"), 1)

                    def exps(u):
                        act.wait_ge(sem("ev_mx"), g * 6 + u + 1)
                        if u >= 2:
                            act.wait_ge(sem("ev_tr2"), g * 6 + u - 1)
                        for half in range(2):
                            t0 = 0 if u < QT else LAT
                            c = 4 * (u % 2) + half
                            nc.scalar.activation(E["p"][:, 2 * (u % 2) + half, t0:T], psf[:, half * 1024 + t0:half * 1024 + T],
                                                 ACT.Exp, bias=st[:, 8 + c:9 + c], scale=SCALE,
                                                 accum_out=st[:, 16 + c:17 + c]).then_inc(sem("ev_exp"), 1)

                    def copy_p(u):
                        act.wait_ge(sem("ev_tr2"), g * 6 + u + 1)
                        if u < QT:
                            dst, src = E["pT"][:, :, u * P:(u + 1) * P], psf[:, 4 * 512:4 * 512 + T]
                        else:
                            dst, src = E["pTc"][:, :, (u - QT) * P:(u - QT + 1) * P], ps[:, 5, 0:CTX]
                        nc.scalar.activation(dst, src.rearrange("p (n t) -> p n t", t=P), ACT.Copy).then_inc(sem("ev_act"), 1)

                    exps(0)
                    for u in range(6):
                        if u < 5:
                            exps(u + 1)
                        copy_p(u)
                    act.wait_ge(sem("ev_pv"), g + 1)
                    nc.scalar.activation(E["osq"], psf[:, 6 * 512:6 * 512 + T], ACT.Square).then_inc(sem("ev_osq"), 1)
                    act.wait_ge(sem("ev_inv"), g + 1)
                    nc.scalar.activation(E["ro"], E["ro"], ACT.Sqrt).then_inc(sem("ev_ro"), 1)

            def odd():
                o_g = O["o"].rearrange("p (g j) t -> p g j t", j=2)
                act.sem_inc(sem("od_free"), 1)
                with act.Fori(0, 4) as g:
                    for s, (dst, src) in enumerate(((O["q"][:, 0, :], ps[:, 0, :]), (O["q"][:, 1, :], ps[:, 1, :]),
                                                    (O["k"], psf[:, 1024:1024 + T]),
                                                    (O["vT"][0:HEAD, :], psf[0:HEAD, 2048:2048 + T]))):
                        act.wait_ge(readA, readA_after("odd", g, s))
                        nc.scalar.activation(dst, src, ACT.Copy).then_inc(sem("od_cp"), 1)
                    act.wait_ge(sem("od_vtr"), g + 1)
                    nc.scalar.activation(O["vtok"].rearrange("p a b -> p (a b)"), ps[:, 4, 0:NT * HEAD], ACT.Copy) \
                        .then_inc(sem("od_cp"), 1)

                    def exps(u):
                        qt = u % QT
                        w = (min(QT, qt + 2) - max(0, qt - 1)) * P
                        c, at = u % 2, 1024 * (u % 2) + 512 - w
                        act.wait_ge(sem("od_mx"), g * 16 + u + 1)
                        if u >= 2:
                            act.wait_ge(sem("od_tr"), g * 16 + u - 1)
                        nc.scalar.activation(O["p"][:, c, 0:w + CTX], psf[:, at:at + w + CTX], ACT.Exp,
                                             bias=st[:, 8 + c:9 + c], scale=SCALE, accum_out=st[:, 16 + c:17 + c])
                        nc.scalar.activation(st[:, 18 + c:19 + c], one_col(SM("sink"), g, u // QT), ACT.Exp,
                                             bias=st[:, 8 + c:9 + c]).then_inc(sem("od_exp"), 1)

                    def copy_p(u):
                        qt = u % QT
                        n = (min(QT, qt + 2) - max(0, qt - 1)) * P + CTX
                        act.wait_ge(sem("od_tr"), g * 16 + u + 1)
                        if u >= 2:
                            act.wait_ge(sem("od_pv"), g * 16 + u - 1)
                        nc.scalar.activation(O["pT"][:, u % 2, 0:n], psf[:, 2048:2048 + n], ACT.Copy).then_inc(sem("od_pt"), 1)

                    exps(0)
                    for u in range(16):
                        if u < 15:
                            exps(u + 1)
                        copy_p(u)
                    act.wait_ge(sem("od_pv"), g * 16 + 16)
                    nc.scalar.activation(one(o_g, g, 0), ps[:, 6, :], ACT.Copy)
                    nc.scalar.activation(one(o_g, g, 1), ps[:, 7, :], ACT.Copy).then_inc(sem("od_free"), 1)
                act.wait_ge(sem("od_free"), 5)
                act.sem_inc(sem("o_ready"), 1)

            def copy_out(name, width, n):
                iters, per = COUNT[name]
                a_g = a[:].rearrange("p (g j) t -> p g j t", j=2)
                act.sem_inc(sem(name + "_free"), 2)
                with act.Fori(0, iters) as g:
                    for j in range(2):
                        act.wait_ge(readA, readA_after(name, g, 2 * j + 1))
                        nc.scalar.activation(one(a_g[:, :, :, 0:width], g, j), psf[:, 1024 * j:1024 * j + width], ACT.Copy) \
                            .then_inc(sem(name + "_free"), 1)
                act.wait_ge(sem(name + "_free"), 2 + DC)
                act.sem_inc(sem("y_ready"), 1)

            def hgrn():
                with act.Fori(0, HEADS) as g:
                    act.wait_ge(readB, readB_after("hg", g, 0))
                    nc.scalar.activation(H["q"], psf[:, 0:T], ACT.Silu).then_inc(sem("hg_act"), 1)
                    act.wait_ge(readB, readB_after("hg", g, 1))
                    nc.scalar.activation(H["kl"][:, 2, :], psf[:, 1024:1024 + T], ACT.Copy).then_inc(sem("hg_act"), 1)
                    for d in range(2):
                        gate = psf[:, 2048 + 1024 * d:2048 + 1024 * d + T]
                        act.wait_ge(readB, readB_after("hg", g, 2 + d))
                        nc.scalar.activation(H["P"][:, d, :], gate, ACT.Sigmoid).then_inc(sem("hg_act"), 1)
                        nc.scalar.activation(H["k"][:, d, :], gate, ACT.Sigmoid, scale=-1.0).then_inc(sem("hg_act"), 1)
                    act.wait_ge(readB, readB_after("hg", g, 4))
                    nc.scalar.activation(H["z"], psf[:, 0:T], ACT.Silu).then_inc(sem("hg_act"), 1)
                    act.wait_ge(sem("hg_vtr"), g + 1)
                    nc.scalar.activation(H["v"].rearrange("p a b -> p (a b)"), psf[:, 1024:1024 + T], ACT.Copy) \
                        .then_inc(sem("hg_act"), 1)
                    for d in range(2):
                        act.wait_ge(sem("hg_ktr"), g * 2 + d + 1)
                        nc.scalar.activation(flat(ktok(d)), psf[:, 2048:2048 + T], ACT.Copy).then_inc(sem("hg_act"), 1)
                    act.wait_ge(sem("hg_o"), g + 1)
                    nc.scalar.activation(H["kl"][:, 0, :], psf[:, 6 * 512:6 * 512 + T], ACT.Square).then_inc(sem("hg_osq"), 1)
                    act.wait_ge(sem("hg_inv"), g + 1)
                    nc.scalar.activation(rstd[:], rstd[:], ACT.Sqrt).then_inc(sem("hg_ro"), 1)

            def mla():
                act.wait_ge(readA, readA_after("mla_low", 0, 3))
                nc.scalar.activation(M["qa"].rearrange("p a b -> p (a b)"), psf[:, 0:1024], ACT.Copy)
                nc.scalar.activation(M["qsq"].rearrange("p a b -> p (a b)"), psf[:, 0:1024], ACT.Square)
                nc.scalar.activation(M["kva"], psf[:, 1024:1024 + T], ACT.Copy)
                nc.scalar.activation(M["kvsq"], psf[:, 1024:1024 + T], ACT.Square)
                nc.scalar.activation(M["kpe"][0:HEAD, :], psf[0:HEAD, 2048:2048 + T], ACT.Copy).then_inc(sem("ml_low"), 1)
                act.wait_ge(sem("ml_inv"), 1)
                nc.scalar.activation(M["rq"], M["rq"], ACT.Sqrt)
                nc.scalar.activation(M["rk"], M["rk"], ACT.Sqrt).then_inc(sem("ml_rlow"), 1)
                with act.Fori(0, HEADS // 2) as g:
                    for e in range(2):
                        h = g * 2 + e
                        act.wait_ge(readA, readA_after("mla", g, 2 * e + 1))
                        for dst, src, fn in ((M["qp"][0:HEAD, :], ps[0:HEAD, 2, :], ACT.Copy), (M["qn"], ps[:, 1, :], ACT.Copy),
                                             (M["kn"], psf[:, 2048:2048 + T], ACT.Copy),
                                             (M["v"].rearrange("p a b -> p (a b)"), psf[:, 3072:3072 + T], ACT.Copy),
                                             (M["z"], ps[:, 0, :], ACT.Silu)):
                            nc.scalar.activation(dst, src, fn).then_inc(sem("ml_cp"), 1)

                        def exps(u):
                            c = u % 2
                            act.wait_ge(sem("ml_mx"), h * 4 + u + 1)
                            if u >= 2:
                                act.wait_ge(sem("ml_tr"), h * 4 + u - 1)
                            nc.scalar.activation(M["p"][:, c, :], psf[:, 1024 * c:1024 * c + T], ACT.Exp, bias=st[:, 8 + c:9 + c],
                                                 scale=MLA_SCALE, accum_out=st[:, 16 + c:17 + c]).then_inc(sem("ml_exp"), 1)

                        def copy_p(u):
                            act.wait_ge(sem("ml_tr"), h * 4 + u + 1)
                            nc.scalar.activation(M["pT"][:, :, u * P:(u + 1) * P],
                                                 psf[:, 2048:2048 + T].rearrange("p (n t) -> p n t", t=P), ACT.Copy) \
                                .then_inc(sem("ml_pt"), 1)

                        exps(0)
                        for u in range(QT):
                            if u < QT - 1:
                                exps(u + 1)
                            copy_p(u)

            act.wait_ge(sem("smalls_in"), 16)
            nc.scalar.activation(svec[:], smalls[:, 0:32], ACT.Silu).then_inc(sem("svec_ready"), 1)
            act.wait_ge(sem("lb_diff"), 1)
            nc.scalar.activation(lbs[:, 0, :], lbs[:, 0, :], ACT.Exp).then_inc(sem("lb_exp"), 1)
            norm(0)
            act.wait_ge(sem("lam_sum"), 1)
            nc.scalar.activation(E["lam"][:, 2:4], ps[:, 2, 0:2], ACT.Exp).then_inc(sem("lam_exp"), 1)
            even()
            norm(1)
            ffn_in(0, T)
            norm(2)
            odd()
            norm(3)
            ffn_in(1, LAT)
            norm(4)
            norm(5)
            hgrn()
            copy_out("hg_out", T, 6)
            norm(6)
            norm(7)
            mla()
            copy_out("mla_out", LAT, 8)
            norm(8)

        @block.vector
        def _(dve):
            TT, TS, STT = nc.vector.tensor_tensor, nc.vector.tensor_scalar, nc.vector.scalar_tensor_tensor

            def norm(n):
                gains, l, scale, shift, width = NORMS[n]
                gain = SM(gains)[:, 16 * l:16 * l + 16].rearrange("p (c v) -> p c v", v=2) if scale or shift else None
                if scale:
                    m = MOD[scale, l]
                    STT(coef[:], mod[:, m:m + DC, :], 1.0, gain, ALU.add, ALU.mult)
                elif shift:
                    m = MOD[shift, l]
                    TT(coef[:], mod[:, m:m + DC, :], gain, ALU.mult)
                dve.wait_ge(sem("stat_done"), DC * (n + 1))
                TS(rstd[:, 0:width], psf[:, 0:width], 1.0 / D, EPS, ALU.mult, ALU.add)
                dve.drain()
                nc.vector.reciprocal(rstd[:, 0:width], rstd[:, 0:width]).then_inc(sem("inv_ready"), 1)
                dve.wait_ge(sem("rstd_ready"), n + 1)
                for c in range(DC):
                    for t0, tn, v in pieces(width):
                        t = slice(t0, t0 + tn)
                        if scale:
                            last = STT(a[:, c, t], x[:, c, t], coef[:, c, v:v + 1], rstd[:, t], ALU.mult, ALU.mult)
                        elif shift:
                            STT(a[:, c, t], a[:, c, t], coef[:, c, v:v + 1], rstd[:, t], ALU.mult, ALU.mult)
                        else:
                            STT(x[:, c, t], x[:, c, t], SM(gains)[:, c:c + 1], rstd[:, t], ALU.mult, ALU.mult)
                    if scale:
                        last.then_inc(sem("scaled"), 1)
                if not scale:
                    dve.drain()
                    if shift:
                        TT(x[:, :, 0:width], x[:, :, 0:width], a[:, :, 0:width], ALU.add)
                        dve.drain()
                    dve.sem_inc(sem("x_ready"), 1)

            def ada(name, first):
                iters, _ = COUNT[name]
                mod_g = mod[:, first:first + 4 * iters, :].rearrange("p (g s) v -> p g s v", s=RA)
                bias_g = SM("ada_b")[:, 2 * first:2 * (first + 4 * iters)].rearrange("p (g s v) -> p g s v", s=RA, v=2)
                dve.drain()
                dve.sem_inc(sem(name + "_free"), RA)
                with dve.Fori(0, iters) as g:
                    for s in range(RA):
                        dve.wait_ge(readA, readA_after(name, g, s))
                        TT(one(mod_g, g, s), ps[:, s, 0:2], one(bias_g, g, s), ALU.add).then_inc(sem(name + "_free"), 1)

            def residual(name, gate, width, per_n):
                iters, per = COUNT[name]
                J = per // per_n
                x_g = x[:].rearrange("p (g j) t -> p g j t", j=J)
                gate_g = mod[:, gate:gate + DC, :].rearrange("p (g j) v -> p g j v", j=J)
                dve.drain()
                dve.sem_inc(sem(name + "_free"), J)
                with dve.Fori(0, iters) as g:
                    for j in range(J):
                        dve.wait_ge(readA, readA_after(name, g, (j + 1) * per_n - 1))
                        for t0, tn, v in pieces(width):
                            xs = one(x_g[:, :, :, t0:t0 + tn], g, j)
                            last = STT(xs, psf[:, 1024 * j + t0:1024 * j + t0 + tn], one(gate_g[:, :, :, v:v + 1], g, j),
                                       xs, ALU.mult, ALU.add)
                        last.then_inc(sem(name + "_free"), 1)
                dve.drain()
                dve.sem_inc(sem("x_ready"), 1)

            def ffn_in(l, width):
                name = f"ffn_in{l}"
                dve.drain()
                dve.sem_inc(sem(f"ffn{l}_up_free"), 2)
                with dve.Fori(0, COUNT[name][0]) as g:
                    for j in range(2):
                        dve.wait_ge(readA, readA_after(name, g, 2 * j + 1))
                        dve.wait_ge(sem(f"ffn{l}_gate_free"), g * 2 + j + 3)
                        TT(one(hidden_g[:, :, :, 0:width], g, j), sg[:, j, 0:width],
                           psf[:, (4 * j + 2) * 512:(4 * j + 2) * 512 + width], ALU.mult).then_inc(sem(f"ffn{l}_up_free"), 1)
                dve.drain()
                dve.sem_inc(sem("hidden_ready"), 1)

            def rope(dst, rotated, tmp, cos, sin):
                TT(tmp, rotated, sin, ALU.mult)
                TT(dst, dst, cos, ALU.mult)

            def even():
                cos, sin = C("cos128"), C("sin128")
                cat_a, cat_b = E["cat"][:, 0:4, :], E["cat"][:, 4:8, :]
                lam = E["lam"]
                dve.sem_inc(sem("ev_free"), 1)
                with dve.Fori(0, 4) as g:
                    for i, (bank, dst) in enumerate(((2, "q"), (4, "k"))):
                        dve.wait_ge(sem("ev_rot"), g * 2 + i + 1)
                        rope(E[dst][:, 0:LAT], ps[:, bank, :], E["tmp"][:, i, :], cos, sin)
                    dve.drain()
                    for i, dst in enumerate("qk"):
                        last = TT(E[dst][:, 0:LAT], E[dst][:, 0:LAT], E["tmp"][:, i, :], ALU.add)
                    last.then_inc(sem("ev_rope"), 1)
                    dve.wait_ge(sem("ev_tr"), g * 2 + 1)
                    vps = psf[:, 6 * 512:6 * 512 + T].rearrange("p (n c) -> p n c", c=P)
                    for n in range(NT):
                        nc.vector.bn_stats(E["bst"][:, n, :], vps[:, n, :])
                    dve.drain()
                    for n in range(NT):
                        nc.vector.bn_aggr(E["mv"][:, n, :], E["bst"][:, n, :])
                    dve.drain()
                    TS(E["lstd"], E["mv"][:, :, 1], EPS, None, ALU.add)
                    dve.drain()
                    nc.vector.reciprocal(E["lstd"], E["lstd"]).then_inc(sem("ev_vinv"), 1)
                    dve.wait_ge(sem("ev_vstd"), g + 1)
                    for n in range(NT):
                        last = TS(E["vtok"][:, n, :], vps[:, n, :], E["mv"][:, n, 0:1], E["lstd"][:, n:n + 1],
                                  ALU.subtract, ALU.mult)
                    last.then_inc(sem("ev_vn"), 1)

                    def maxima(u):
                        dve.wait_ge(sem("ev_sc"), g * 6 + u + 1)
                        c, t0 = 4 * (u % 2), 0 if u < QT else LAT
                        for half in range(2):
                            nc.vector.reduce_max(st[:, c + half:c + half + 1], psf[:, half * 1024 + t0:half * 1024 + T], AX_X)
                        dve.drain()
                        TS(st[:, 8 + c:10 + c], st[:, c:c + 2], -SCALE, None, ALU.mult).then_inc(sem("ev_mx"), 1)

                    def difference(u):
                        c, t = 4 * (u % 2), slice(0 if u < QT else LAT, T)
                        p0, p1 = (E["p"][:, 2 * (u % 2) + half, t] for half in range(2))
                        dve.wait_ge(sem("ev_exp"), g * 12 + 2 * u + 2)
                        nc.vector.reciprocal(st[:, 24 + c:26 + c], st[:, 16 + c:18 + c])
                        dve.drain()
                        TT(st[:, 25 + c:26 + c], st[:, 25 + c:26 + c], lam[:, 5:6], ALU.mult)
                        TS(p0, p0, st[:, 24 + c:25 + c], None, ALU.mult)
                        dve.drain()
                        STT(p0, p1, st[:, 25 + c:26 + c], p0, ALU.mult, ALU.add).then_inc(sem("ev_p"), 1)

                    maxima(0)
                    dve.wait_ge(sem("ev_mix"), g + 1)
                    bias = E["sgub"][:, bass.ds(g, 1), :].broadcast_to([P, NT, P])
                    TT(E["mix"].rearrange("p (n c) -> p n c", c=P), vps, bias, ALU.add)
                    dve.drain()
                    TT(flat(cat_a[:, bass.ds(g, 1), :]), E["mix"], E["u"], ALU.mult).then_inc(sem("ev_cat"), 1)
                    for u in range(6):
                        if u < 5:
                            maxima(u + 1)
                        difference(u)
                    dve.wait_ge(sem("ev_ms"), g + 1)
                    TS(E["ro"], psf[:, 4 * 512:4 * 512 + T], 1.0 / P, EPS, ALU.mult, ALU.add)
                    dve.drain()
                    nc.vector.reciprocal(E["ro"], E["ro"]).then_inc(sem("ev_inv"), 1)
                    dve.wait_ge(sem("ev_ro"), g + 1)
                    STT(flat(cat_b[:, bass.ds(g, 1), :]), psf[:, 6 * 512:6 * 512 + T], lam[:, 6:7], E["ro"],
                        ALU.mult, ALU.mult).then_inc(sem("ev_free"), 1)
                dve.drain()
                dve.sem_inc(sem("cat_ready"), 1)

            def odd():
                with dve.Fori(0, 4) as g:
                    for i, dst in enumerate((O["q"][:, 0, :], O["q"][:, 1, :], O["k"][:, 0:LAT])):
                        dve.wait_ge(sem("od_rot"), g * 3 + i + 1)
                        rope(dst, ps[:, i, :], O["tmp"][:, i, :], C("cos128"), C("sin128"))
                        dve.drain()
                        last = TT(dst, dst, O["tmp"][:, i, :], ALU.add)
                    last.then_inc(sem("od_rope"), 1)

                    def maxima(u):
                        qt, c = u % QT, u % 2
                        w = (min(QT, qt + 2) - max(0, qt - 1)) * P
                        dve.wait_ge(sem("od_sc"), g * 16 + u + 1)
                        nc.vector.reduce_max(st[:, c:c + 1], psf[:, 1024 * c + 512 - w:1024 * c + 512 + CTX], AX_X)
                        dve.drain()
                        TS(st[:, 2 + c:3 + c], st[:, c:c + 1], SCALE, one_col(SM("sink"), g, u // QT), ALU.mult, ALU.max)
                        dve.drain()
                        TS(st[:, 8 + c:9 + c], st[:, 2 + c:3 + c], -1.0, None, ALU.mult).then_inc(sem("od_mx"), 1)

                    def normalise(u):
                        qt, c = u % QT, u % 2
                        n = (min(QT, qt + 2) - max(0, qt - 1)) * P + CTX
                        dve.wait_ge(sem("od_exp"), g * 16 + u + 1)
                        TT(st[:, 20 + c:21 + c], st[:, 16 + c:17 + c], st[:, 18 + c:19 + c], ALU.add)
                        dve.drain()
                        nc.vector.reciprocal(st[:, 24 + c:25 + c], st[:, 20 + c:21 + c])
                        dve.drain()
                        TS(O["p"][:, c, 0:n], O["p"][:, c, 0:n], st[:, 24 + c:25 + c], None, ALU.mult).then_inc(sem("od_p"), 1)

                    maxima(0)
                    for u in range(16):
                        if u < 15:
                            maxima(u + 1)
                        normalise(u)

            def hgrn():
                oml = lbs[:, 3, :].rearrange("p (d h) -> p d h", d=2)
                low = lbs[:, 2, :].rearrange("p (d h) -> p d h", d=2)
                dve.wait_ge(sem("lvl_ready"), NT)
                for buf in (1, 3):
                    nc.vector.memset(H["kl"][:, buf, :], 0.0)
                dve.drain()
                dve.sem_inc(sem("hg_free"), 1)
                with dve.Fori(0, HEADS) as g:
                    for d in range(2):
                        dve.wait_ge(sem("hg_act"), g * 10 + 4 + 2 * d)
                        TS(H["P"][:, d, :], H["P"][:, d, :], oml[:, d, bass.ds(g, 1)], low[:, d, bass.ds(g, 1)],
                           ALU.mult, ALU.add)
                        TS(H["k"][:, d, :], H["k"][:, d, :], oml[:, d, bass.ds(g, 1)], None, ALU.mult)
                    dve.drain()
                    TT(H["kl"][:, 0, :], H["k"][:, 0, :], H["k"][:, 1, :], ALU.add).then_inc(sem("hg_ksum"), 1)

                    def half(ap, h, i):
                        return ap.rearrange("p (b two h) -> p b two h", two=2, h=h)[:, :, i, :]

                    def end(ap, h, i, d):
                        r = h - 1 if d == 0 else 0
                        v = ap.rearrange("p (b two h) -> p b two h", two=2, h=h)[:, :, i, r:r + 1]
                        return v if h == 1 else v.broadcast_to([P, T // (2 * h), h])

                    def level(i):
                        h = 1 << i
                        for d in range(2):
                            buf, qh, kh = 2 * d + i % 2, 1 - d, d
                            if i >= 2:
                                dve.wait_ge(sem("hg_A"), (g * LEVELS + i - 2) * 2 + d + 1)
                            Pd, Sd = H["P"][:, d, :], H["S"][:, d, :]
                            last = TT(H["ql"][:, buf, :].rearrange("p (b h) -> p b h", h=h), half(H["q"], h, qh),
                                      half(Pd, h, qh), ALU.mult)
                            if i > 0:
                                last = TT(half(H["kl"][:, buf, :], h, kh), half(H["k"][:, d, :], h, kh), half(Sd, h, kh), ALU.mult)
                            last.then_inc(sem("hg_lvl"), 1)
                        for d in range(2):
                            qh, kh = 1 - d, d
                            Pd, Sd = H["P"][:, d, :], H["S"][:, d, :]
                            if i == 0:
                                nc.vector.tensor_copy(half(Sd, h, kh), half(Pd, h, qh))
                                nc.vector.memset(half(Sd, h, qh), 1.0)
                            else:
                                TT(half(Sd, h, kh), half(Sd, h, kh), end(Pd, h, qh, d), ALU.mult)
                        dve.drain()
                        for d in range(2):
                            qh, kh = 1 - d, d
                            Pd = H["P"][:, d, :]
                            if d == 1 and i > 0:
                                dve.wait_ge(sem("hg_A"), (g * LEVELS + i) * 2)
                            TT(half(Pd, h, qh), half(Pd, h, qh), end(Pd, h, kh, d), ALU.mult)
                        dve.drain()

                    def select(i):
                        h = 1 << i
                        for d in range(2):
                            nc.vector.copy_predicated(
                                half(flat(H["A"]), h, 1 - d),
                                lvl[:, d * LEVELS + i, :].rearrange("p (b h) -> p b h", h=h),
                                ps[:, 2 * d + i % 2, 0:T // 2].rearrange("p (b h) -> p b h", h=h)).then_inc(sem("hg_sel"), 1)

                    dve.wait_ge(sem("hg_act"), g * 10 + 8)
                    level(0)
                    dve.wait_ge(sem("hg_diag"), g + 1)
                    TT(H["A"], psf[:, 2048:2048 + T].rearrange("p (n c) -> p n c", c=P),
                       ident.unsqueeze(1).broadcast_to([P, NT, P]), ALU.mult)
                    for i in range(1, LEVELS):
                        level(i)
                        select(i - 1)
                    dve.wait_ge(sem("hg_A"), (g + 1) * LEVELS * 2)
                    for d in range(2):
                        TT(H["kl"][:, 2 * d, :], H["q"], H["P"][:, d, :], ALU.mult)
                        TT(H["kl"][:, 2 * d + 1, :], H["k"][:, d, :], H["S"][:, d, :], ALU.mult).then_inc(sem("hg_kS"), 1)
                    dve.drain()
                    select(LEVELS - 1)
                    for d in range(2):
                        dve.wait_ge(sem("hg_add"), g * 2 + d + 1)
                        for i, n in enumerate(CHUNKS[d][:5]):
                            add = psf[:, 2 * d * 512 + n * P:2 * d * 512 + (n + 1) * P]
                            at = n * P + (P - 1 if d == 0 else 0)
                            if i == 0:
                                nc.vector.tensor_copy(state(d, i), add).then_inc(sem("hg_state"), 1)
                            else:
                                dve.wait_ge(sem("hg_state"), (g * 2 + d) * 5 + i)
                                STT(state(d, i), state(d, i - 1), H["P"][:, d, at:at + 1], add, ALU.mult, ALU.add) \
                                    .then_inc(sem("hg_state"), 1)
                    dve.wait_ge(sem("hg_ms"), g + 1)
                    TS(rstd[:], psf[:, 2048:2048 + T], 1.0 / P, EPS, ALU.mult, ALU.add)
                    dve.drain()
                    nc.vector.reciprocal(rstd[:], rstd[:]).then_inc(sem("hg_inv"), 1)
                    dve.wait_ge(sem("hg_ro"), g + 1)
                    og = flat(H["og"][:, bass.ds(g, 1), :])
                    STT(H["S"][:, 0, :], psf[:, 6 * 512:6 * 512 + T], SM("o_norm"), rstd[:], ALU.mult, ALU.mult)
                    dve.drain()
                    TT(og, H["S"][:, 0, :], H["z"], ALU.mult).then_inc(sem("hg_free"), 1)
                dve.drain()
                dve.sem_inc(sem("og_ready"), 1)

            def mla():
                cos, sin = C("cos64")[0:HEAD, :], C("sin64")[0:HEAD, :]
                dve.wait_ge(sem("ml_lowms"), 1)
                TS(M["rq"], ps[:, 0, :], 1.0 / (2 * P), EPS, ALU.mult, ALU.add)
                TS(M["rk"], psf[:, 1024:1024 + T], 1.0 / P, EPS, ALU.mult, ALU.add)
                rope(M["kpe"][0:HEAD, 0:LAT], ps[0:HEAD, 4, :], M["tmp"][0:HEAD, :], cos, sin)
                dve.drain()
                TT(M["kpe"][0:HEAD, 0:LAT], M["kpe"][0:HEAD, 0:LAT], M["tmp"][0:HEAD, :], ALU.add)
                nc.vector.reciprocal(M["rq"], M["rq"])
                nc.vector.reciprocal(M["rk"], M["rk"]).then_inc(sem("ml_inv"), 1)
                dve.wait_ge(sem("ml_rlow"), 1)
                for k in range(2):
                    STT(M["qa"][:, k, :], M["qa"][:, k, :], SM("qa_norm")[:, k:k + 1], M["rq"], ALU.mult, ALU.mult)
                STT(M["kva"], M["kva"], SM("kva_norm"), M["rk"], ALU.mult, ALU.mult).then_inc(sem("ml_lown"), 1)
                dve.sem_inc(sem("ml_free"), 1)
                og_g = M["og"].rearrange("p (g e) t -> p g e t", e=2)
                with dve.Fori(0, HEADS // 2) as g:
                    for e in range(2):
                        h = g * 2 + e
                        dve.wait_ge(sem("ml_rot"), h + 1)
                        rope(M["qp"][0:HEAD, :], ps[0:HEAD, 3, :], M["tmp"][0:HEAD, :], cos, sin)
                        dve.drain()
                        TT(M["qp"][0:HEAD, :], M["qp"][0:HEAD, :], M["tmp"][0:HEAD, :], ALU.add).then_inc(sem("ml_rope"), 1)

                        def maxima(u):
                            c = u % 2
                            dve.wait_ge(sem("ml_sc"), h * 4 + u + 1)
                            nc.vector.reduce_max(st[:, c:c + 1], psf[:, 1024 * c:1024 * c + T], AX_X)
                            dve.drain()
                            TS(st[:, 8 + c:9 + c], st[:, c:c + 1], -MLA_SCALE, None, ALU.mult).then_inc(sem("ml_mx"), 1)

                        def normalise(u):
                            c = u % 2
                            dve.wait_ge(sem("ml_exp"), h * 4 + u + 1)
                            nc.vector.reciprocal(st[:, 24 + c:25 + c], st[:, 16 + c:17 + c])
                            dve.drain()
                            TS(M["p"][:, c, :], M["p"][:, c, :], st[:, 24 + c:25 + c], None, ALU.mult).then_inc(sem("ml_p"), 1)

                        maxima(0)
                        for u in range(QT):
                            if u < QT - 1:
                                maxima(u + 1)
                            normalise(u)
                        dve.wait_ge(sem("ml_pv"), h + 1)
                        TT(one(og_g, g, e), ps[:, 6, :], M["z"], ALU.mult).then_inc(sem("ml_free"), 1)
                dve.drain()
                dve.sem_inc(sem("ml_og"), 1)

            dve.wait_ge(sem("smalls_in"), 16)
            TT(lbs[:, 0, :], SM("lbl"), SM("lbl"), ALU.subtract).then_inc(sem("lb_diff"), 1)
            TT(E["lam"][:, 0:2], SM("lamv")[:, 0:2], SM("lamv")[:, 2:4], ALU.mult).then_inc(sem("lam_prod"), 1)
            TS(E["lam"][:, 6:7], SM("subln"), 1.0 - LAM_INIT, None, ALU.mult)
            dve.wait_ge(sem("lb_exp"), 1)
            nc.vector.reciprocal(lbs[:, 1, :], lbs[:, 0, :])
            dve.drain()
            TT(lbs[:, 1, :], lbs[:, 0, :], lbs[:, 1, :], ALU.mult)
            dve.drain()
            TT(lbs[:, 2, :], lbs[:, 1, :], lbs[:, 1, :], ALU.subtract)
            dve.drain()
            TS(lbs[:, 3, :], lbs[:, 2, :], -1.0, 1.0, ALU.mult, ALU.add)
            ada("ada1", 0)
            ada("ada2", 96)
            dve.drain()
            norm(0)
            dve.wait_ge(sem("lam_exp"), 1)
            TT(E["lam"][:, 4:5], E["lam"][:, 3:4], E["lam"][:, 2:3], ALU.subtract)
            dve.drain()
            TS(E["lam"][:, 5:6], E["lam"][:, 4:5], LAM_INIT, None, ALU.subtract)
            dve.drain()
            even()
            residual("even_out", MOD["g1", 0], T, 1)
            norm(1)
            ffn_in(0, T)
            residual("ffn_out0", MOD["g2", 0], T, 3)
            norm(2)
            odd()
            residual("odd_out", MOD["g1", 1], LAT, 1)
            norm(3)
            ffn_in(1, LAT)
            residual("ffn_out1", MOD["g2", 1], LAT, 3)
            norm(4)
            norm(5)
            hgrn()
            norm(6)
            norm(7)
            mla()
            norm(8)


def make_consts(np):
    c = np.zeros((P, N_CONST), np.float32)

    def put(name, v):
        c[:v.shape[0], CONST[name][0]:CONST[name][0] + v.shape[1]] = v

    put("ident", np.eye(P, dtype=np.float32))
    put("ones", np.ones((P, P), np.float32))
    rot = np.zeros((P, P), np.float32)
    for m in range(P):
        if m % 32 < 16:
            rot[m + 16, m] = -1
        else:
            rot[m - 16, m] = 1
    put("rot128", rot)
    rot = np.zeros((HEAD, P), np.float32)
    for m in range(HEAD):
        if m < 32:
            rot[m + 32, m] = -1
        else:
            rot[m - 32, m] = 1
    put("rot64", rot)
    inv = np.float32(10000.0) ** (-np.arange(16, dtype=np.float32) / np.float32(16))
    t = np.arange(LAT)
    pos = np.stack([t // 64, t % 64]).astype(np.float32)
    d = np.arange(P) % HEAD
    ang = pos[d // 32] * inv[d % 16][:, None]
    put("cos128", np.cos(ang))
    put("sin128", np.sin(ang))
    d = np.arange(HEAD) % 32
    ang = pos[d // 16] * inv[d % 16][:, None]
    put("cos64", np.cos(ang))
    put("sin64", np.sin(ang))
    q, k = np.arange(P)[:, None], np.arange(P)[None, :]
    put("maskl", np.where(k >= q, 0, NEG).astype(np.float32))
    put("maskr", np.where(k <= q, 0, NEG).astype(np.float32))
    lv = np.zeros((P, 2 * LEVELS, 64), np.float32)
    s = np.arange(P)
    for dd in range(2):
        for i in range(LEVELS):
            h = 1 << i
            for j in range(64):
                lv[:, dd * LEVELS + i, j] = (s // (2 * h) == j // h) & ((s // h) % 2 == dd)
    return c, lv


def chunked(np, v):
    return v.reshape(-1, P).T


def blocks(np, w):
    k, n = w.shape
    return w.reshape(k // P, P, n // P, P).transpose(2, 1, 0, 3)


def tiles(np, w):
    k, n = w.shape
    kp, np_ = -(-k // D) * D, -(-n // P) * P
    if (kp, np_) != (k, n):
        full = np.zeros((kp, np_), w.dtype)
        full[:k, :n] = w
        w = full
    b = blocks(np, w)
    nb = b.shape[0]
    return b.reshape(nb, P, kp // D, D).transpose(0, 2, 1, 3).reshape(-1, P, D)


def kernel(**inputs):
    import numpy as np
    import concourse.bacc as bacc
    from concourse.bass_utils import run_bass_kernel_spmd

    i = {k: np.asarray(v) for k, v in inputs.items()}

    def interleave(*ts):
        return np.stack(ts, axis=1).reshape(-1, P, D)

    w = i["even_w_in"][0]
    A_, Q_ = 512, 512
    parts = [tiles(np, w[:, at:at + 512]) for at in (0, 1024, 1536, 512, 2048)]
    even = interleave(*parts)

    def ffn(l):
        f = i["ffn_w_in"][l]
        return interleave(tiles(np, f[:, :HID]), tiles(np, f[:, HID:])), tiles(np, i["ffn_w_out"][l])

    f_in0, f_out0 = ffn(0)
    f_in1, f_out1 = ffn(1)
    w = i["odd_w_qkv"][0]
    odd = []
    for g in range(4):
        kg = w[:, 1024 + g * HEAD:1024 + (g + 1) * HEAD]
        odd += [tiles(np, w[:, g * 256:(g + 1) * 256]), tiles(np, np.concatenate([kg, kg], axis=1)),
                tiles(np, w[:, 1280 + g * HEAD:1280 + (g + 1) * HEAD])]
    odd = np.concatenate(odd)
    w = i["hg_w_in_2"][0]
    W2 = 2 * D
    hg = interleave(*[tiles(np, w[:, W2 * n:W2 * (n + 1)]) for n in range(5)])
    w = i["mla_w_in_2"][0]
    low = np.concatenate([tiles(np, w[:, 0:256]), tiles(np, w[:, 256:384]), tiles(np, w[:, 384:448])])
    qb = i["mla_w_qb_2"][0].reshape(2, P, HEADS, 192)
    kvb = i["mla_w_kvb_2"][0].reshape(P, HEADS, 256)
    wb = np.zeros((HEADS, P, D), np.float32)
    for k in range(2):
        wb[:, :, k * P:(k + 1) * P] = qb[k, :, :, 0:P].transpose(1, 0, 2)
        wb[:, :, 256 + k * HEAD:256 + (k + 1) * HEAD] = qb[k, :, :, P:].transpose(1, 0, 2)
    wb[:, :, 384:640] = kvb.transpose(1, 0, 2)
    mla = interleave(tiles(np, w[:, 448:]), wb)
    streamA = np.concatenate(
        [tiles(np, i["ada_w"][0]), tiles(np, i["ada_w"][1]), tiles(np, i["ada_w_2"][0]), tiles(np, i["ada_w_2"][1]),
         tiles(np, i["even_w_out"][0]), f_in0, f_out0, odd, tiles(np, i["odd_w_out"][0]), f_in1, f_out1,
         tiles(np, i["hg_w_out_2"][0]), low, mla, tiles(np, i["mla_w_out_2"][0])])
    streamB = np.concatenate([even, hg])
    assert len(streamA) == N_A and len(streamB) == N_B

    smalls = np.zeros((P, N_SMALL), np.float32)

    def put(name, v):
        v = v.reshape(v.shape[0], -1)
        assert v.shape[1] == SMALL[name][1] - SMALL[name][0], name
        smalls[:v.shape[0], SMALL[name][0]:SMALL[name][1]] = v

    def twice(v):
        return np.repeat(chunked(np, v)[:, :, None], 2, axis=2)

    for tag, name in (("", "cvec"), ("_2", "cvec2")):
        put(name, np.stack([chunked(np, i["c" + tag][0]), chunked(np, i["c_ctx" + tag])], axis=2))
    put("ada_b", twice(np.concatenate([i["ada_b"].ravel(), i["ada_b_2"].ravel()])))
    for name, src in (("norm1_g", "norm1_g"), ("norm2_g", "norm2_g"), ("norm_pre", "norm_pre_2"), ("norm_post", "norm_post_2")):
        put(name, twice(i[src].ravel()))
    put("final_g", chunked(np, i["final_g"]))
    put("subln", i["diff_subln_g"][0][:, None])
    put("lamv", np.stack([i["diff_lq1"][0], i["diff_lq2"][0], i["diff_lk1"][0], i["diff_lk2"][0]], axis=1))
    put("sink", np.broadcast_to(i["odd_sink"][0][None, :], (P, 16)))
    put("lbl", chunked(np, i["hg_lb_logits_2"][0].ravel()))
    put("o_norm", i["hg_o_norm_2"][0][:, None])
    put("qa_norm", chunked(np, i["mla_qa_norm_2"][0]))
    put("kva_norm", i["mla_kva_norm_2"][0][:, None])
    sgu = np.concatenate([i["sgu_w"][0].transpose(2, 0, 1).reshape(P, 512),
                          np.broadcast_to(i["sgu_b"][0].reshape(1, 512), (P, 512))], axis=1)

    def tokens(v):
        return v.T.reshape(DC, P, -1).transpose(1, 0, 2)

    x_in = np.concatenate([tokens(i["x"][0]), tokens(i["ctx"][0])], axis=2)
    consts, lv = make_consts(np)
    arrays = {"streamA": streamA, "streamB": streamB, "x_in": x_in, "ctx2_in": tokens(i["ctx_2"][0]), "smalls_in": smalls,
              "consts_in": consts, "lvl_in": lv, "sgu_in": sgu}
    arrays = {k: np.ascontiguousarray(v) for k, v in arrays.items()}
    nc = bacc.Bacc("TRN2", target_bir_lowering=False, num_devices=1)
    args = [nc.dram_tensor(k, v.shape, mybir.dt.from_np(v.dtype), kind="ExternalInput").ap() for k, v in arrays.items()]
    out = nc.dram_tensor("out", (P, DC, LAT), F32, kind="ExternalOutput").ap()
    build(nc, *args, out)
    r = run_bass_kernel_spmd(nc, [arrays], core_ids=[0])
    y = r.results[0]["out"]
    return y.transpose(2, 1, 0).reshape(1, LAT, D)
```

```python
from contextlib import ExitStack
import math

import concourse.bass as bass
from concourse import mybir

F32 = mybir.dt.float32
F32R = mybir.dt.float32r
U8 = mybir.dt.uint8
ALU = mybir.AluOpType
ACT = mybir.ActivationFunctionType
AX_X = mybir.AxisListType.X

P = 128
D = 1024
DC = D // P
LAT, CTX = 512, 256
T = LAT + CTX
NT = T // P
QT = LAT // P
HID = 2816
HC = HID // P
EPS = 1e-6
HEAD = 64
SCALE = HEAD ** -0.5
LAM_INIT = 0.8 - 0.6 * math.exp(0.0)
HEADS = 16
MLA_SCALE = (128 + 64) ** -0.5
LEVELS = 7
NEG = -1e30
RA, RB, RC = 4, 5, 2
GROUPS = 36

SMALL = {}
_at = 0
for _name, _n in (("cvec", 16), ("cvec2", 16), ("ada_b", 288), ("norm1_g", 32), ("norm2_g", 32), ("final_g", 8),
                  ("norm_pre", 32), ("norm_post", 32), ("subln", 1), ("lamv", 4), ("sink", 16), ("lbl", 32),
                  ("o_norm", 1), ("qa_norm", 2), ("kva_norm", 1)):
    SMALL[_name] = (_at, _at + _n)
    _at += _n
N_SMALL = _at
CONST = {}
_at = 0
for _name, _n in (("ident", 128), ("ones", 128), ("rot128", 128), ("rot64", 128), ("cos128", LAT), ("sin128", LAT),
                  ("cos64", LAT), ("sin64", LAT), ("maskl", 128), ("maskr", 128)):
    CONST[_name] = (_at, _at + _n)
    _at += _n
N_CONST = _at

PLAN_A = [("even_out", 2, 4), ("ffn_in0", 11, 4), ("ffn_out0", 2, 12),
          ("odd", 4, 4), ("odd_out", 2, 4), ("ffn_in1", 11, 4), ("ffn_out1", 2, 12),
          ("hg_out", 4, 4), ("mla_low", 1, 4), ("mla", 8, 4), ("mla_out", 4, 4)]
PLAN_B = [("even", 4, 5), ("hg", 16, 5)]
ORDER = ["even", "even_out", "ffn_in0", "ffn_out0", "odd", "odd_out", "ffn_in1", "ffn_out1",
         "hg", "hg_out", "mla_low", "mla", "mla_out"]


SPLIT_STAGES = ("even", "ffn_in0", "odd", "ffn_in1", "hg")
RH = 3


def starts(plan):
    at, out = 0, {}
    for name, iters, per in plan:
        out[name] = at
        at += iters * per
    return out, at


START_A, N_A = starts(PLAN_A)
START_B, N_B = starts(PLAN_B)
SPLIT_A, _ = starts([s for s in PLAN_A if s[0] in SPLIT_STAGES])
COUNT = {name: (iters, per) for name, iters, per in PLAN_A + PLAN_B}

MOD = {}
for _l in range(2):
    for _i, _name in enumerate(("sh1", "sc1", "g1", "sh2", "sc2", "g2")):
        MOD[_name, _l] = 48 * _l + 8 * _i
    for _i, _name in enumerate(("sh", "sc", "gt")):
        MOD[_name, _l] = 96 + 24 * _l + 8 * _i


def build(nc, streamA, streamB, streamC, x_in, ctx2_in, smalls_in, consts_in, lvl_in, sgu_in, out):
    with ExitStack() as ctx:
        def sb(name, shape, dt=F32):
            return ctx.enter_context(nc.sbuf_tensor(name, shape, dt))

        sems = {}

        def sem(name):
            if name not in sems:
                sems[name] = ctx.enter_context(nc.semaphore(name))
            return sems[name]

        def both(name, shape):
            with nc.sbuf_tensor(name, shape, F32) as v:
                pass
            return v, sb(name + "_r", shape, F32R)

        x, x_r = both("x", [P, DC, T])
        x_dram = nc.dram_tensor("x_scratch", (P, DC, T), F32).ap()
        og_dram = nc.dram_tensor("og_scratch", (P, HEADS // 2, T), F32).ap()
        a, a_r = both("a", [P, DC, T])
        ringA, ringA_r = both("ringA", [P, RA, D])
        ringB, ringB_r = both("ringB", [P, RB, D])
        sq = sb("sq", [P, 2, T])
        rstd = sb("rstd", [P, T])
        consts = sb("consts", [P, N_CONST])
        smalls = sb("smalls", [P, N_SMALL])
        mod = sb("mod", [P, 144, 2])
        coef = sb("coef", [P, DC, 2])
        svec = sb("svec", [P, 32])
        st = sb("st", [P, 64])
        esm = sb("esm", [P, 64])
        lvl = sb("lvl", [P, 2 * LEVELS, NT * 64], U8)
        FREE = 23808
        arena = sb("arena", [P, FREE])
        ps = ctx.enter_context(nc.psum_tensor("ps", [P, 8, 512], F32))
        psf = ps[:].rearrange("p b n -> p (b n)")

        def C(name):
            return consts[:, CONST[name][0]:CONST[name][1]]

        def SM(name):
            return smalls[:, SMALL[name][0]:SMALL[name][1]]

        ident, ones = C("ident"), C("ones")

        def carve():
            at = [0]

            def take(*shape):
                n = math.prod(shape)
                v = arena[:, at[0]:at[0] + n]
                at[0] += n
                assert at[0] <= FREE, at[0]
                if len(shape) == 2:
                    v = v.rearrange("p (a b) -> p a b", b=shape[1])
                elif len(shape) == 3:
                    v = v.rearrange("p (a b c) -> p a b c", b=shape[1], c=shape[2])
                return v
            return take

        def flat(ap):
            return ap.rearrange("p a t -> p (a t)")

        def one(ap, g, j):
            return ap[:, bass.ds(g, 1), j, :].rearrange("p a t -> p (a t)")

        landedA = [sem(f"landedA{s}") for s in range(RA)]
        landedB = [sem(f"landedB{s}") for s in range(RB)]
        readA, readB = sem("readA"), sem("readB")

        def readA_after(name, g, k):
            return RA + START_A[name] + g * COUNT[name][1] + k + 1

        def mla_landed(h, e):
            return 16 * (START_A["mla"] // RA + 1) + (h - e) * 8

        def mla_read(h, k):
            return RA + START_A["mla"] + h * 2 + k + 1

        def readB_after(name, g, k):
            return RB + START_B[name] + g * RB + k + 1

        def landedA_at(name, g, k):
            return 16 * ((START_A[name] + k) // RA + 1) + g * (16 * COUNT[name][1] // RA)

        def splitA_after(name, g, k):
            return SPLIT_A[name] + g * COUNT[name][1] + k + 1

        def splitB_after(name, g, k):
            return START_B[name] + g * RB + k + 1

        def landedB_at(name, g):
            return 16 * (START_B[name] // RB + 1) + g * 16

        tk = carve()
        hidden, sg = tk(HC, T), tk(2, T)
        ADA = (RC * D + 4 * LAT)
        ringC = arena[:, FREE - ADA:FREE - ADA + RC * D].rearrange("p (s k n) -> p s k n", s=RC, k=2)
        acc = arena[:, FREE - 4 * LAT:FREE].rearrange("p (i v n) -> p i v n", i=2, v=2)
        hidden_g = hidden.rearrange("p (g j) t -> p g j t", j=2)
        assert FREE - ADA >= HC * T + 2 * T
        tk = carve()
        E = dict(cat=tk(DC, T), u=tk(T), q=tk(T), k=tk(T), vT=tk(T), vvT=tk(T), vtok=tk(NT, P), vvtok=tk(NT, P),
                 tmp=tk(2, LAT), p=tk(4, T), pT=tk(NT, LAT), sguw=tk(4, P), sgub=tk(4, P))
        assert sum(math.prod(v.shape[1:]) for v in E.values()) <= FREE - ADA
        E.update(mix=E["vT"], pTc=E["vvT"][:, 0:2 * CTX].rearrange("p (a b) -> p a b", b=CTX), osq=sq[:, 0, :], ro=sq[:, 1, :],
                 lam=esm[:, 0:8], lstd=esm[:, 8:14], mv=esm[:, 14:26].rearrange("p (a b) -> p a b", b=2),
                 bst=esm[:, 26:62].rearrange("p (a b) -> p a b", b=6))
        lvl_f = a[:].rearrange("p c t -> p (c t)")[:, 0:2 * LEVELS * 64].rearrange("p (l j) -> p l j", j=64)
        tk = carve()
        O = dict(q=tk(2, LAT), k=tk(T), vT=tk(T), vtok=tk(NT, HEAD), p=tk(2, 640), pT=tk(2, 5 * P), o=tk(DC, LAT),
                 tmp=tk(3, LAT))
        tk = carve()
        H = dict(og=tk(HEADS // 2, T), S=tk(2, T), ql=tk(4, T // 2), kl=tk(4, T))
        HP = [dict(q=tk(T), z=tk(T), P=tk(2, T), k=tk(2, T), v=tk(NT, P)) for _ in range(2)]
        H.update(vT=tk(T), A=rstd[:].rearrange("p (n c) -> p n c", c=P))
        og_stage = ringA[:, RA - 1, 0:T]
        tk = carve()
        M = dict(og=tk(HEADS, LAT), qa=tk(2, LAT), kva=tk(T), kpe=tk(T), p=tk(2, T), pT=tk(NT, LAT), tmp=tk(LAT))
        MP = [dict(qn=tk(LAT), qp=tk(LAT), kn=tk(T), v=tk(NT, P), z=tk(LAT)) for _ in range(2)]
        pTf = M["pT"].rearrange("p a b -> p (a b)")
        M.update(qsq=pTf[:, 0:2 * LAT].rearrange("p (a b) -> p a b", b=LAT), kvsq=pTf[:, 1024:1024 + T],
                 rq=pTf[:, 1792:1792 + LAT], rk=pTf[:, 2304:2304 + T])
        lbs = sb("lbs", [P, 4, 32])

        def pieces(width):
            return [(0, LAT, 0)] + ([(LAT, CTX, 1)] if width == T else [])

        NORMS = [("norm1_g", 0, "sc1", "sh1", T), ("norm2_g", 0, "sc2", "sh2", T),
                 ("norm1_g", 1, "sc1", "sh1", T), ("norm2_g", 1, "sc2", "sh2", LAT),
                 ("final_g", 0, None, None, LAT),
                 ("norm_pre", 0, "sc", "sh", T), ("norm_post", 0, None, "gt", T),
                 ("norm_pre", 1, "sc", "sh", T), ("norm_post", 1, None, "gt", LAT)]
        MODULATED = [0, 1, 2, 3, 5, 7]
        SPLIT = [0, 1, 2, 3, 5]
        SPILL = {1: T, 2: LAT, 3: LAT, 5: LAT}
        SPILLS = list(SPILL)
        X_READY = {1: 1, 2: 2, 3: 3, 4: 4, 5: 5, 7: 6}
        CHUNKS = [[4, 5, 0, 1, 2, 3], [5, 4, 3, 2, 1, 0]]

        def ktok(d):
            return H["ql"][:, 2 * d:2 * d + 2, :].rearrange("p a (b c) -> p (a b) c", c=P)

        def state(d, i):
            at = (d * 5 + i) * P
            return sq[:].rearrange("p a t -> p (a t)")[:, at:at + P]

        def one_col(ap, g, j):
            return ap.rearrange("p (g j) -> p g j", j=4)[:, bass.ds(g, 1), j]

        block = ctx.enter_context(nc.Block())

        @block.sync
        def _(sp):
            sp.dma_start(smalls[:], smalls_in).then_inc(sem("smalls_in"), 16)
            sp.dma_start(x[:], x_in).then_inc(sem("x_in"), 16)
            sp.dma_start(consts[:], consts_in).then_inc(sem("consts_in"), 16)
            sp.dma_start(lvl_f, lvl_in).then_inc(sem("lvl_in"), 16)
            sp.dma_start(E["sguw"].rearrange("p a b -> p (a b)"), sgu_in[:, 0:512]).then_inc(sem("sgu_in"), 16)
            sp.dma_start(E["sgub"].rearrange("p a b -> p (a b)"), sgu_in[:, 512:1024]).then_inc(sem("sgu_in"), 16)
            groupsA = streamA.rearrange("(g s) p n -> g s p n", s=RA)
            groupsB = streamB.rearrange("(g s) p n -> g s p n", s=RB)
            groupsC = streamC.rearrange("(g s) p n -> g s p n", s=RC)

            def load_A(g, s):
                sp.wait_ge(readA, g * RA + s + 1)
                sp.dma_start(ringA[:, s, :], groupsA[bass.ds(g, 1), s].rearrange("a p n -> (a p) n")) \
                    .then_inc(landedA[s], 16)

            def load_B(g, s):
                sp.wait_ge(readB, g * RB + s + 1)
                sp.dma_start(ringB[:, s, :], groupsB[bass.ds(g, 1), s].rearrange("a p n -> (a p) n")) \
                    .then_inc(landedB[s], 16)

            def load_C(g, n):
                sp.wait_ge(sem("readC"), (g + n // RC) * RC + n % RC + 1)
                sp.dma_start(ringC[:, n % RC].rearrange("p k n -> p (k n)"),
                             groupsC[bass.ds(g + n // RC, 1), n % RC].rearrange("a p n -> (a p) n")) \
                    .then_inc(sem(f"landedC{n % RC}"), 16)

            def stream_A(name):
                first = START_A[name] // RA
                with sp.Fori(first, first + COUNT[name][0] * COUNT[name][1] // RA) as g:
                    for s in range(RA):
                        load_A(g, s)

            for s in range(RB):
                load_B(0, s)
            with sp.Fori(1, COUNT["even"][0]) as g:
                for s in range(3):
                    load_B(g, s)
                for n in range(8):
                    load_C(8 + (g - 1) * 4, n)
                for s in range(3, RB):
                    load_B(g, s)
            for n in range(8):
                load_C(8 + (COUNT["even"][0] - 1) * 4, n)
            sp.wait_ge(readB, RB + START_B["hg"])
            stream_A("even_out")
            first = START_A["ffn_in0"] // RA
            at_c = 24
            for s in range(RA):
                load_A(first, s)
            with sp.Fori(1, COUNT["ffn_in0"][0]) as g:
                for s in range(RA):
                    load_A(g + first, s)
                    for n in range(3 * s, min(3 * s + 3, 8)):
                        load_C(at_c + (g - 1) * 4, n)
            for n in range(8):
                load_C(at_c + (COUNT["ffn_in0"][0] - 1) * 4, n)
            at_c += COUNT["ffn_in0"][0] * 4
            first = START_A["ffn_out0"] // RA
            with sp.Fori(first, first + 3) as g:
                for s in range(RA):
                    load_A(g, s)
            for k in range(12):
                load_A(first + 3 + k // RA, k % RA)
                if k < 8:
                    load_C(at_c, k)
            for name in ("odd", "odd_out", "ffn_in1", "ffn_out1"):
                stream_A(name)
            first = START_B["hg"] // RB
            for lo, hi, store in ((0, 2, False), (2, 2 + HEADS // 2, True), (2 + HEADS // 2, HEADS, False)):
                with sp.Fori(first + lo, first + hi) as g:
                    for s in range(RB):
                        load_B(g, s)
                    if store:
                        sp.wait_ge(sem("hg_free"), g - first)
                        sp.dma_start(og_dram[:, bass.ds(g - first - 2, 1), :].rearrange("p a t -> p (a t)"), og_stage) \
                            .then_inc(sem("og_out"), 16)
            sp.wait_ge(readB, RB + N_B)
            for name in ("hg_out", "mla_low", "mla", "mla_out"):
                stream_A(name)
            sp.wait_ge(sem("x_ready"), 7)
            sp.dma_start(out, x[:, :, 0:LAT]).then_inc(sem("stored"), 16)
            sp.wait_ge(sem("stored"), 16)

        @block.gpsimd
        def _(pool):
            pool.wait_ge(sem("lvl_in"), 16)
            for n in range(NT):
                nc.gpsimd.tensor_copy(lvl[:].rearrange("p l (n j) -> p l n j", j=64)[:, :, n, :], lvl_f) \
                    .then_inc(sem("lvl_ready"), 1)
            groupsC = streamC.rearrange("(g s) p n -> g s p n", s=RC)
            with pool.Fori(0, 8) as g:
                for s in range(RC):
                    pool.wait_ge(sem("readC"), g * RC + s + 1)
                    pool.sem_inc(sem("ada_begun"), 1)
                    pool.dma_start(ringC[:, s].rearrange("p k n -> p (k n)"),
                                   groupsC[bass.ds(g, 1), s].rearrange("a p n -> (a p) n")).then_inc(sem(f"firstC{s}"), 16)

            def split(ring, ring_r, slot, high_r, high_slot, done):
                high = high_r[:, high_slot, :]
                nc.gpsimd.tensor_tensor(high, ring[:, slot, :], ones[:, 0:1].broadcast_to([P, D]), ALU.mult)
                pool.drain()
                nc.gpsimd.tensor_tensor(ring_r[:, slot, :], ring[:, slot, :], high.bitcast(F32), ALU.subtract) \
                    .then_inc(sem(done), 1)

            def split_A(name):
                with pool.Fori(0, COUNT[name][0]) as g:
                    for s in range(RA):
                        pool.wait_ge(landedA[s], landedA_at(name, g, s))
                        pool.sem_inc(sem("split_begun"), 1)
                        split(ringA, ringA_r, s, ringB_r, s, "splitA")

            def split_B(name):
                with pool.Fori(0, COUNT[name][0]) as g:
                    for s in range(RB):
                        pool.wait_ge(landedB[s], landedB_at(name, g))
                        pool.wait_ge(readB, readB_after(name, g, s - 2))
                        pool.sem_inc(sem("split_begun"), 1)
                        split(ringB, ringB_r, s, ringA_r, s % RH, "splitB")

            pool.wait_ge(sem("consts_in"), 16)
            split_B("even")
            split_A("ffn_in0")
            split_A("odd")
            split_A("ffn_in1")
            pool.wait_ge(readA, readA_after("ffn_out1", 1, 11))
            split_B("hg")

        @block.tensor
        def _(pe):
            pe.sem_inc(readA, RA)
            pe.sem_inc(readB, RB)

            def product(ring, slot, src, bank, width, kc=DC, k0=0, start=True, stop=True, m=P, w0=0):
                for k in range(kc):
                    for t0, tn, half in pieces(width):
                        mm = nc.tensor.matmul(ps[0:m, bank + half, 0:tn], ring[:, slot, w0 + k * P:w0 + k * P + m],
                                              src[:, k0 + k, t0:t0 + tn], start=start and k == 0,
                                              stop=stop and k == kc - 1)
                return mm

            def split_product(ring_r, slot, high_r, high_slot, bank, width):
                for k in range(DC):
                    w = slice(k * P, (k + 1) * P)
                    for t0, tn, half in pieces(width):
                        t = slice(t0, t0 + tn)
                        for i, (wk, src) in enumerate(((high_r[:, high_slot, w], x_r), (high_r[:, high_slot, w], a_r),
                                                       (ring_r[:, slot, w], x_r))):
                            mm = nc.tensor.matmul(ps[:, bank + half, 0:tn], wk, src[:, k, t], start=k == 0 and i == 0,
                                                  stop=k == DC - 1 and i == 2)
                return mm

            def split_product_A(name, g, s, bank, width):
                pe.wait_ge(sem("splitA"), splitA_after(name, g, s))
                split_product(ringA_r, s, ringB_r, s, bank, width).then_inc(readA, 1)

            def split_product_B(name, g, s, bank):
                pe.wait_ge(sem("splitB"), splitB_after(name, g, s))
                split_product(ringB_r, s, ringA_r, s % RH, bank, T).then_inc(readB, 1)

            def norm_stats(n):
                for c in range(DC):
                    pe.wait_ge(sem("sq_ready"), DC * n + c + 1)
                    for t0, tn, half in pieces(NORMS[n][4]):
                        mm = nc.tensor.matmul(ps[:, half, 0:tn], ones, sq[:, c % 2, t0:t0 + tn],
                                              start=c == 0, stop=c == DC - 1)
                    mm.then_inc(sem("stat_done"), 1)

            def a_wait(n):
                pe.wait_ge(sem("a_ready"), MODULATED.index(n) + 1)

            def ada_sum(done, bank, col):
                pe.wait_ge(sem("ada_acc"), done + 1)
                for i in range(2):
                    for c in range(4):
                        for v in range(2):
                            at = col + 8 * i + 2 * c + v
                            mm = nc.tensor.matmul(ps[:, bank, at:at + 1], acc[:, i, v, c * P:(c + 1) * P], ones[:, 0:1],
                                                  start=True, stop=True)
                mm.then_inc(sem("ada_sum"), 1)

            def out_product(name, src, width, per_n, low=None):
                iters, per = COUNT[name]
                J = per // per_n
                kall = src.shape[1] + (DC if low is not None else 0)
                with pe.Fori(0, iters) as g:
                    for j in range(J):
                        pe.wait_ge(sem(name + "_free"), g * J + j + 1)
                        for i in range(per_n):
                            k = j * per_n + i
                            kc = min(DC, kall - i * DC)
                            pe.wait_ge(landedA[k % RA], landedA_at(name, g, k))
                            part, k0 = (src, i * DC) if low is None else ((low, src)[i], 0)
                            product(ringA, k % RA, part, 2 * j, width, kc=kc, k0=k0, start=i == 0,
                                    stop=i == per_n - 1).then_inc(readA, 1)

            def ffn_in(l, width):
                name = f"ffn_in{l}"
                with pe.Fori(0, COUNT[name][0]) as g:
                    for s in range(RA):
                        pe.wait_ge(sem(f"ffn{l}_" + ("up_free" if s % 2 else "gate_free")), g * 2 + s // 2 + 1)
                        if l == 0 and s == RA - 1:
                            ada_sum(g + 6, 7, 256)
                        split_product_A(name, g, s, 2 * s, width)

            def even():
                name = "even"
                pe.wait_ge(sem("consts_in"), 16)
                pe.wait_ge(sem("lam_prod"), 1)
                nc.tensor.matmul(ps[:, 5, 0:2], ones, E["lam"][:, 0:2], start=True, stop=True).then_inc(sem("lam_sum"), 1)
                a_wait(0)
                with pe.Fori(0, 4) as g:
                    def tile(s, bank):
                        split_product_B(name, g, s, bank)

                    def scores(u):
                        if u > 0:
                            pe.wait_ge(sem("ev_exp"), g * 12 + 2 * u)
                        for half in range(2):
                            r = slice(half * HEAD, (half + 1) * HEAD)
                            lhs = E["q"][r, u * P:(u + 1) * P]
                            if u < QT:
                                nc.tensor.matmul(ps[:, 2 * half, :], lhs, E["k"][r, 0:LAT], start=True, stop=True)
                            mm = nc.tensor.matmul(ps[:, 2 * half + 1, 0:CTX], lhs, E["k"][r, LAT:T], start=True, stop=True)
                        mm.then_inc(sem("ev_sc"), 1)

                    def turn(u):
                        pe.wait_ge(sem("ev_p"), g * 6 + u + 1)
                        if u > 0:
                            pe.wait_ge(sem("ev_pt"), g * 6 + u)
                        for n in range(0 if u < QT else QT, NT):
                            mm = nc.tensor.transpose(psf[:, 4 * 512 + n * P:4 * 512 + (n + 1) * P],
                                                     E["p"][:, 2 * (u % 2), n * P:(n + 1) * P], ident)
                        mm.then_inc(sem("ev_tr2"), 1)

                    def to_tokens(src):
                        for n in range(NT):
                            mm = nc.tensor.transpose(psf[:, 6 * 512 + n * P:6 * 512 + (n + 1) * P],
                                                     E[src][:, n * P:(n + 1) * P], ident)
                        return mm

                    pe.wait_ge(sem("ev_free"), g + 1)
                    tile(0, 6)
                    tile(1, 4)
                    pe.wait_ge(sem("ev_q"), g + 1)
                    nc.tensor.matmul(ps[:, 6, :], C("rot128"), E["q"][:, 0:LAT], start=True, stop=True).then_inc(sem("ev_rot"), 1)
                    pe.wait_ge(sem("ev_k"), g + 1)
                    nc.tensor.matmul(ps[:, 4, :], C("rot128"), E["k"][:, 0:LAT], start=True, stop=True).then_inc(sem("ev_rot"), 1)
                    tile(2, 0)
                    pe.wait_ge(sem("ev_rope"), g + 1)
                    pe.wait_ge(sem("ev_vv"), g + 1)
                    scores(0)
                    tile(3, 6)
                    scores(1)
                    pe.wait_ge(sem("ev_v"), g + 1)
                    tile(4, 6)
                    turn(0)
                    scores(2)
                    pe.wait_ge(sem("ev_u"), g + 1)
                    to_tokens("vvT").then_inc(sem("ev_vvtr"), 1)
                    turn(1)
                    scores(3)
                    pe.wait_ge(sem("ev_vvtok"), g + 1)
                    to_tokens("vT").then_inc(sem("ev_vtr"), 1)
                    turn(2)
                    scores(4)
                    turn(3)
                    pe.wait_ge(sem("sgu_in"), 32)
                    pe.wait_ge(sem("ev_vn"), g + 1)
                    for n in range(NT):
                        mm = nc.tensor.matmul(psf[:, 6 * 512 + n * P:6 * 512 + (n + 1) * P], E["vtok"][:, n, :],
                                              flat(E["sguw"][:, bass.ds(g, 1), :]), start=True, stop=True)
                    mm.then_inc(sem("ev_mix"), 1)
                    scores(5)
                    turn(4)
                    pe.wait_ge(sem("ev_cat"), g + 1)
                    for n in range(NT):
                        nc.tensor.matmul(ps[:, 6, :], E["vvtok"][:, n, :], E["pT"][:, n, :], start=n == 0, stop=n == NT - 1)
                    turn(5)
                    ada_sum(g + 2, 0, 0)
                    pe.wait_ge(sem("ev_pt"), g * 6 + 6)
                    for n in range(2):
                        mm = nc.tensor.matmul(ps[:, 7, 0:CTX], E["vvtok"][:, QT + n, :], E["pTc"][:, n, :],
                                              start=n == 0, stop=n == 1)
                    mm.then_inc(sem("ev_pv"), 1)
                    pe.wait_ge(sem("ev_osq"), g + 1)
                    for t0, tn, half in pieces(T):
                        mm = nc.tensor.matmul(ps[:, 4 + half, 0:tn], ones, E["osq"][:, t0:t0 + tn], start=True, stop=True)
                    mm.then_inc(sem("ev_ms"), 1)
                pe.wait_ge(sem("cat_ready"), 1)

            def odd():
                name = "odd"
                a_wait(2)
                with pe.Fori(0, 4) as g:
                    for s, (bank, width) in enumerate(((0, LAT), (1, LAT), (2, T), (4, T))):
                        if s == 0:
                            pe.wait_ge(sem("od_free"), g + 1)
                        split_product_A(name, g, s, bank, width)
                    for i, src in enumerate((O["q"][:, 0, :], O["q"][:, 1, :], O["k"][:, 0:LAT])):
                        pe.wait_ge(sem("od_cp"), g * 5 + i + 1 + i // 2)
                        nc.tensor.matmul(ps[:, i, :], C("rot128"), src, start=True, stop=True).then_inc(sem("od_rot"), 1)
                    for n in range(NT):
                        mm = nc.tensor.transpose(ps[:, 4, n * HEAD:(n + 1) * HEAD], O["vT"][0:HEAD, n * P:(n + 1) * P],
                                                 ident[0:HEAD, 0:HEAD])
                    mm.then_inc(sem("od_vtr"), 1)

                    def scores(u):
                        hh, qt = divmod(u, QT)
                        r = slice((hh % 2) * HEAD, (hh % 2 + 1) * HEAD)
                        lo, hi = max(0, qt - 1) * P, min(QT, qt + 2) * P
                        b, w = 2 * (u % 2), hi - lo
                        lhs = O["q"][r, hh // 2, qt * P:(qt + 1) * P]
                        if u == 0:
                            pe.wait_ge(sem("od_rope"), g + 1)
                        if u >= 2:
                            pe.wait_ge(sem("od_exp"), g * 16 + u - 1)
                        nc.tensor.matmul(ps[:, b, 512 - w:512], lhs, O["k"][r, lo:hi], start=True, stop=False,
                                         skip_group_check=True)
                        if qt > 0:
                            nc.tensor.matmul(ps[:, b, 512 - w:512 - w + P], ident, C("maskl"), start=False, stop=qt == QT - 1,
                                             skip_group_check=True)
                        if qt < QT - 1:
                            nc.tensor.matmul(ps[:, b, 512 - P:512], ident, C("maskr"), start=False, stop=True,
                                             skip_group_check=True)
                        nc.tensor.matmul(ps[:, b + 1, 0:CTX], lhs, O["k"][r, LAT:T], start=True, stop=True) \
                            .then_inc(sem("od_sc"), 1)

                    def turn(u):
                        qt = u % QT
                        w = (min(QT, qt + 2) - max(0, qt - 1)) * P
                        pe.wait_ge(sem("od_p"), g * 16 + u + 1)
                        if u == 0:
                            pe.wait_ge(sem("od_cp"), g * 5 + 5)
                        else:
                            pe.wait_ge(sem("od_pt"), g * 16 + u)
                        for n in range((w + CTX) // P):
                            mm = nc.tensor.transpose(psf[:, 4 * 512 + n * P:4 * 512 + (n + 1) * P],
                                                     O["p"][:, u % 2, n * P:(n + 1) * P], ident)
                        mm.then_inc(sem("od_tr"), 1)

                    def values(u):
                        hh, qt = divmod(u, QT)
                        lo, hi = max(0, qt - 1), min(QT, qt + 2)
                        keys = list(range(lo, hi)) + [QT, QT + 1]
                        r = slice((hh % 2) * HEAD, (hh % 2 + 1) * HEAD)
                        pe.wait_ge(sem("od_pt"), g * 16 + u + 1)
                        for n, key in enumerate(keys):
                            mm = nc.tensor.matmul(ps[r, 6 + hh // 2, qt * P:(qt + 1) * P], O["vtok"][:, key, :],
                                                  O["pT"][:, u % 2, n * P:(n + 1) * P], start=n == 0,
                                                  stop=n == len(keys) - 1)
                        mm.then_inc(sem("od_pv"), 1)

                    scores(0)
                    for u in range(16):
                        if u < 15:
                            scores(u + 1)
                        turn(u)
                        if u > 0:
                            values(u - 1)
                    values(15)
                pe.wait_ge(sem("o_ready"), 1)
                ada_sum(17, 0, 0)

            def hgrn():
                a_wait(5)

                def tile(h, s, bank):
                    split_product_B("hg", h, s, bank)

                def values_to_tokens(h):
                    pe.wait_ge(sem("hg_vT"), h + 1)
                    for n in range(NT):
                        mm = nc.tensor.transpose(psf[:, 1024 + n * P:1024 + (n + 1) * P], H["vT"][:, n * P:(n + 1) * P], ident)
                    mm.then_inc(sem("hg_vtr"), 1)

                def pairs(h, e, i):
                    for d in range(2):
                        buf = 2 * d + i % 2
                        pe.wait_ge(sem("hg_lvl"), (h * LEVELS + i) * 2 + d + 1)
                        if i >= 2:
                            pe.wait_ge(sem("hg_sel"), (h * LEVELS + i - 2) * 2 + d + 1)
                        for n in range(NT):
                            keys = HP[e]["k"][:, d, n * P:(n + 1) * P] if i == 0 else H["kl"][:, buf, n * P:(n + 1) * P]
                            mm = nc.tensor.matmul(ps[:, 4 + buf, n * HEAD:(n + 1) * HEAD], keys,
                                                  H["ql"][:, buf, n * HEAD:(n + 1) * HEAD], start=True, stop=True)
                        mm.then_inc(sem("hg_A"), 1)

                def step(h, e, follow):
                    nxt = h + 1
                    pe.wait_ge(sem("hg_inv"), h + 1)
                    if follow:
                        tile(nxt, 0, 0)
                    pe.wait_ge(sem("hg_ksum"), h + 1)
                    for n in range(NT):
                        mm = nc.tensor.matmul(psf[:, 2048 + n * P:2048 + (n + 1) * P], H["kl"][:, 0, n * P:(n + 1) * P],
                                              HP[e]["q"][:, n * P:(n + 1) * P], start=True, stop=True)
                    mm.then_inc(sem("hg_diag"), 1)
                    if follow:
                        tile(nxt, 1, 2)
                    pe.wait_ge(sem("hg_init"), h + 1)
                    pe.wait_ge(sem("hg_free"), h + 1)
                    pairs(h, e, 0)
                    pairs(h, e, 1)
                    if follow:
                        pe.wait_ge(sem("hg_q"), nxt + 1)
                        tile(nxt, 2, 0)
                        values_to_tokens(nxt)
                    pairs(h, e, 2)
                    pairs(h, e, 3)
                    if follow:
                        pe.wait_ge(sem("hg_v"), nxt + 1)
                        tile(nxt, 3, 2)
                    pairs(h, e, 4)
                    pairs(h, e, 5)
                    pairs(h, e, 6)
                    pe.wait_ge(sem("hg_sel"), (h + 1) * LEVELS * 2)
                    for d in range(2):
                        pe.wait_ge(sem("hg_kS"), h * 2 + d + 1)
                        for n in range(NT):
                            at = 2048 + 1024 * d + n * P
                            mm = nc.tensor.transpose(psf[:, at:at + P], H["kl"][:, 2 * d + 1, n * P:(n + 1) * P], ident)
                        mm.then_inc(sem("hg_ktr"), 1)
                    if follow:
                        pe.wait_ge(sem("hg_gate"), nxt * 2 + 1)
                        tile(nxt, 4, 0)
                    for d in range(2):
                        pe.wait_ge(sem("hg_kt"), h * 2 + d + 1)
                        if d == 1 and follow:
                            pe.wait_ge(sem("hg_gate"), nxt * 2 + 2)
                        bank = 4 - 2 * d
                        for n in range(NT):
                            mm = nc.tensor.matmul(psf[:, bank * 512 + n * P:bank * 512 + (n + 1) * P], ktok(d)[:, n, :],
                                                  HP[e]["v"][:, n, :], start=True, stop=True)
                        mm.then_inc(sem("hg_add"), 1)
                    for n in range(NT):
                        nc.tensor.matmul(psf[:, 3072 + n * P:3072 + (n + 1) * P], HP[e]["v"][:, n, :], H["A"][:, n, :],
                                         start=n % 4 == 0, stop=False, skip_group_check=True)
                    for d in range(2):
                        for i, n in enumerate(CHUNKS[d][1:]):
                            pe.wait_ge(sem(f"hg_state{d}"), h * 5 + i + 1)
                            mm = nc.tensor.matmul(psf[:, 3072 + n * P:3072 + (n + 1) * P], state(d, i),
                                                  H["kl"][:, 2 * d, n * P:(n + 1) * P], start=False,
                                                  stop=d == 1 and n in (0, 4), skip_group_check=True)
                    mm.then_inc(sem("hg_o"), 1)
                    if follow:
                        pe.wait_ge(sem("hg_z"), nxt + 1)
                    pe.wait_ge(sem("hg_osq"), h + 1)
                    for t0, tn, half in pieces(T):
                        mm = nc.tensor.matmul(ps[:, half, 0:tn], ones, H["kl"][:, 0, t0:t0 + tn], start=True, stop=True)
                    mm.then_inc(sem("hg_ms"), 1)

                tile(0, 0, 0)
                tile(0, 1, 2)
                tile(0, 2, 4)
                values_to_tokens(0)
                tile(0, 3, 6)
                pe.wait_ge(sem("hg_q"), 1)
                tile(0, 4, 0)
                pe.wait_ge(sem("hg_z"), 1)
                with pe.Fori(0, HEADS // 2 - 1) as g:
                    for e in range(2):
                        step(g * 2 + e, e, True)
                step(HEADS - 2, 0, True)
                step(HEADS - 1, 1, False)
                pe.wait_ge(sem("og_ready"), 1)

            def mla():
                a_wait(7)
                name = "mla_low"
                for s, (bank, width) in enumerate(((0, LAT), (1, LAT), (2, T), (4, T))):
                    pe.wait_ge(landedA[s], landedA_at(name, 0, s))
                    product(ringA, s, a, bank, width, m=HEAD if s == 3 else P).then_inc(readA, 1)
                pe.wait_ge(sem("ml_low"), 1)
                for k in range(2):
                    nc.tensor.matmul(ps[:, 0, :], ones, M["qsq"][:, k, :], start=k == 0, stop=k == 1)
                for t0, tn, half in pieces(T):
                    nc.tensor.matmul(ps[:, 2 + half, 0:tn], ones, M["kvsq"][:, t0:t0 + tn], start=True, stop=True)
                nc.tensor.matmul(ps[:, 4, :], C("rot64")[0:HEAD, :], M["kpe"][0:HEAD, 0:LAT], start=True, stop=True) \
                    .then_inc(sem("ml_lowms"), 1)
                pe.wait_ge(sem("ml_lown"), 1)

                def project(h, e, piece):
                    W = ringA[:, 2 * e + 1, :]
                    if piece == "z":
                        pe.wait_ge(landedA[2 * e], mla_landed(h, e))
                        if not first(h):
                            pe.wait_ge(sem("ml_vl"), h)
                        product(ringA, 2 * e, a, 7, LAT).then_inc(readA, 1)
                    elif piece == "qn":
                        pe.wait_ge(landedA[2 * e + 1], mla_landed(h, e))
                        if not first(h):
                            pe.wait_ge(sem("ml_free"), h)
                        for k in range(2):
                            mm = nc.tensor.matmul(ps[:, 6, :], W[:, k * P:(k + 1) * P], M["qa"][:, k, :], start=k == 0, stop=k == 1)
                        mm.then_inc(sem("ml_qn_done"), 1)
                    elif piece == "qp":
                        pe.wait_ge(sem("ml_z"), h + 1)
                        for k in range(2):
                            mm = nc.tensor.matmul(ps[0:HEAD, 7, :], W[:, 256 + k * HEAD:256 + (k + 1) * HEAD], M["qa"][:, k, :],
                                                  start=k == 0, stop=k == 1)
                        mm.then_inc(sem("ml_qp_done"), 1)
                    elif piece == "rot":
                        pe.wait_ge(sem("ml_qp"), h + 1)
                        nc.tensor.matmul(ps[:, 6, :], C("rot64")[0:HEAD, :], MP[e]["qp"][0:HEAD, :], start=True, stop=True) \
                            .then_inc(sem("ml_rot"), 1)
                    elif piece == "kl":
                        nc.tensor.matmul(ps[:, 7, :], W[:, 384:512], M["kva"][:, 0:LAT], start=True, stop=True) \
                            .then_inc(sem("ml_kl_done"), 1)
                    elif piece == "kc":
                        pe.wait_ge(sem("ml_rope"), h + 1)
                        nc.tensor.matmul(ps[:, 6, 0:CTX], W[:, 384:512], M["kva"][:, LAT:T], start=True, stop=True) \
                            .then_inc(sem("ml_kc_done"), 1)
                    elif piece == "vl":
                        pe.wait_ge(sem("ml_kl"), h + 1)
                        for n in range(QT):
                            mm = nc.tensor.matmul(ps[:, 7, n * P:(n + 1) * P], M["kva"][:, n * P:(n + 1) * P], W[:, 512:640],
                                                  start=True, stop=True)
                        mm.then_inc(sem("ml_vl_done"), 1)
                    elif piece == "vc":
                        pe.wait_ge(sem("ml_kc"), h + 1)
                        for n in range(2):
                            mm = nc.tensor.matmul(ps[:, 6, n * P:(n + 1) * P], M["kva"][:, (QT + n) * P:(QT + n + 1) * P],
                                                  W[:, 512:640], start=True, stop=True)
                        mm.then_inc(readA, 1)

                def first(h):
                    return isinstance(h, int) and h == 0

                def step(h, e, follow):
                    B = MP[e]

                    def nxt(*names):
                        if follow:
                            for n in names:
                                project(h + 1, 1 - e, n)

                    def scores(u):
                        b = 2 * (u % 2)
                        if u == 0:
                            pe.wait_ge(sem("ml_rope"), h + 1)
                            pe.wait_ge(sem("ml_kc"), h + 1)
                        if u >= 2:
                            pe.wait_ge(sem("ml_exp"), h * 4 + u - 1)
                        for t0, tn, half in pieces(T):
                            nc.tensor.matmul(ps[:, b + half, 0:tn], B["qn"][:, u * P:(u + 1) * P], B["kn"][:, t0:t0 + tn],
                                             start=True, stop=False)
                            mm = nc.tensor.matmul(ps[:, b + half, 0:tn], B["qp"][0:HEAD, u * P:(u + 1) * P],
                                                  M["kpe"][0:HEAD, t0:t0 + tn], start=False, stop=True)
                        mm.then_inc(sem("ml_sc"), 1)

                    def turn(u):
                        pe.wait_ge(sem("ml_p"), h * 4 + u + 1)
                        if u > 0:
                            pe.wait_ge(sem("ml_pt"), h * 4 + u)
                        for n in range(NT):
                            mm = nc.tensor.transpose(psf[:, 4 * 512 + n * P:4 * 512 + (n + 1) * P],
                                                     M["p"][:, u % 2, n * P:(n + 1) * P], ident)
                        mm.then_inc(sem("ml_tr"), 1)

                    scores(0)
                    scores(1)
                    nxt("z")
                    turn(0)
                    scores(2)
                    nxt("qn", "qp")
                    turn(1)
                    scores(3)
                    nxt("rot", "kl", "kc")
                    turn(2)
                    nxt("vl")
                    turn(3)
                    nxt("vc")
                    pe.wait_ge(sem("ml_pt"), h * 4 + 4)
                    if follow:
                        pe.wait_ge(sem("ml_vc"), h + 2)
                    else:
                        pe.wait_ge(sem("ml_vc"), h + 1)
                    for n in range(NT):
                        mm = nc.tensor.matmul(ps[:, 6, :], B["v"][:, n, :], M["pT"][:, n, :], start=n == 0, stop=n == NT - 1)
                    mm.then_inc(sem("ml_pv"), 1)

                for n in ("z", "qn", "qp", "rot", "kl", "kc", "vl", "vc"):
                    project(0, 0, n)
                with pe.Fori(0, HEADS // 2 - 1) as g:
                    for e in range(2):
                        step(g * 2 + e, e, True)
                step(HEADS - 2, 0, True)
                step(HEADS - 1, 1, False)
                pe.wait_ge(sem("ml_og"), 1)

            pe.wait_ge(sem("consts_in"), 16)
            ada_sum(0, 2, 0)
            ada_sum(1, 3, 0)
            norm_stats(0)
            even()
            out_product("even_out", E["cat"], T, 1)
            norm_stats(1)
            a_wait(1)
            ffn_in(0, T)
            pe.wait_ge(sem("hidden_ready"), 1)
            out_product("ffn_out0", hidden, T, 3)
            norm_stats(2)
            odd()
            out_product("odd_out", O["o"], LAT, 1)
            norm_stats(3)
            a_wait(3)
            ffn_in(1, LAT)
            pe.wait_ge(sem("hidden_ready"), 2)
            out_product("ffn_out1", hidden, LAT, 3)
            norm_stats(4)
            norm_stats(5)
            hgrn()
            pe.wait_ge(sem("og_back"), 16)
            out_product("hg_out", H["og"], T, 2, low=x)
            norm_stats(6)
            norm_stats(7)
            mla()
            out_product("mla_out", M["og"], LAT, 2)
            norm_stats(8)

        @block.scalar
        def _(act):
            def norm_squares(n):
                _, _, _, _, width = NORMS[n]
                post = n in (6, 8)
                if n == 0:
                    act.wait_ge(sem("x_in"), 16)
                elif post:
                    act.wait_ge(sem("y_ready"), 1 + (n == 8))
                else:
                    act.wait_ge(sem("x_ready"), X_READY[n])
                if n in SPILL:
                    act.dma_start(x_dram[:, :, 0:SPILL[n]], x[:, :, 0:SPILL[n]]).then_inc(sem("x_out"), 16)
                if n == 5:
                    act.wait_ge(sem("ctx2_in"), 16)
                for c in range(DC):
                    if DC * n + c >= 2:
                        act.wait_ge(sem("stat_done"), DC * n + c - 1)
                    nc.scalar.activation(sq[:, c % 2, 0:width], (a if post else x)[:, c, 0:width], ACT.Square) \
                        .then_inc(sem("sq_ready"), 1)

            def norm_root(n):
                width = NORMS[n][4]
                act.wait_ge(sem("inv_ready"), n + 1)
                nc.scalar.activation(rstd[:, 0:width], rstd[:, 0:width], ACT.Sqrt).then_inc(sem("rstd_ready"), 1)

            def norm(n):
                norm_squares(n)
                norm_root(n)
                if n in MODULATED:
                    m = MODULATED.index(n)
                    shift = MOD[NORMS[n][3], NORMS[n][1]]
                    if n in SPILL:
                        act.wait_ge(sem("x_out"), 16 * (SPILLS.index(n) + 1))
                    for c in range(DC):
                        act.wait_ge(sem("scaled"), DC * m + c + 1)
                        for t0, tn, v in pieces(NORMS[n][4]):
                            t = slice(t0, t0 + tn)
                            last = nc.scalar.activation((x_r if n in SPLIT else a)[:, c, t], a[:, c, t], ACT.Identity,
                                                        bias=mod[:, shift + c, v:v + 1])
                        if n in SPLIT:
                            last.then_inc(sem("a_high"), 1)
                    if n not in SPLIT:
                        last.then_inc(sem("a_ready"), 1)

            def x_back(n):
                w = SPILL.get(n, T)
                act.dma_start(x[:, :, 0:w], x_dram[:, :, 0:w] if n else x_in).then_inc(sem("x_back"), 16)

            def ffn_in(l, width):
                name = f"ffn_in{l}"
                act.sem_inc(sem(f"ffn{l}_gate_free"), 2)
                with act.Fori(0, COUNT[name][0]) as g:
                    for j in range(2):
                        act.wait_ge(readA, readA_after(name, g, 2 * j))
                        act.wait_ge(sem(f"ffn{l}_up_free"), g * 2 + j + 1)
                        nc.scalar.activation(sg[:, j, 0:width], psf[:, 4 * j * 512:4 * j * 512 + width], ACT.Silu) \
                            .then_inc(sem(f"ffn{l}_gate_free"), 1)
                act.wait_ge(readA, readA_after(name, COUNT[name][0] - 1, RA - 1))
                x_back(1 + 2 * l)

            def even():
                with act.Fori(0, 4) as g:
                    def evacuate(s, bank, dst, fn):
                        act.wait_ge(readB, readB_after("even", g, s))
                        nc.scalar.activation(E[dst], psf[:, bank * 512:bank * 512 + T], fn).then_inc(sem("ev_" + dst.rstrip("T")), 1)

                    def exps(u):
                        act.wait_ge(sem("ev_mx"), g * 6 + u + 1)
                        if u >= 2:
                            act.wait_ge(sem("ev_tr2"), g * 6 + u - 1)
                        for half in range(2):
                            t0 = 0 if u < QT else LAT
                            c = 4 * (u % 2) + half
                            nc.scalar.activation(E["p"][:, 2 * (u % 2) + half, t0:T], psf[:, half * 1024 + t0:half * 1024 + T],
                                                 ACT.Exp, bias=st[:, 8 + c:9 + c], scale=SCALE,
                                                 accum_out=st[:, 16 + c:17 + c]).then_inc(sem("ev_exp"), 1)

                    def copy_p(u):
                        act.wait_ge(sem("ev_tr2"), g * 6 + u + 1)
                        if u < QT:
                            dst, src = E["pT"][:, :, u * P:(u + 1) * P], psf[:, 4 * 512:4 * 512 + T]
                        else:
                            dst, src = E["pTc"][:, :, (u - QT) * P:(u - QT + 1) * P], ps[:, 5, 0:CTX]
                        nc.scalar.activation(dst, src.rearrange("p (n t) -> p n t", t=P), ACT.Copy).then_inc(sem("ev_pt"), 1)

                    evacuate(0, 6, "q", ACT.Copy)
                    evacuate(1, 4, "k", ACT.Copy)
                    evacuate(2, 0, "vvT", ACT.Copy)
                    exps(0)
                    evacuate(3, 6, "vT", ACT.Gelu)
                    exps(1)
                    evacuate(4, 6, "u", ACT.Gelu)
                    copy_p(0)
                    exps(2)
                    act.wait_ge(sem("ev_vvtr"), g + 1)
                    nc.scalar.activation(E["vvtok"].rearrange("p a b -> p (a b)"), psf[:, 3072:3072 + T], ACT.Copy) \
                        .then_inc(sem("ev_vvtok"), 1)
                    copy_p(1)
                    exps(3)
                    copy_p(2)
                    act.wait_ge(sem("ev_vinv"), g + 1)
                    nc.scalar.activation(E["lstd"], E["lstd"], ACT.Sqrt).then_inc(sem("ev_vstd"), 1)
                    exps(4)
                    copy_p(3)
                    exps(5)
                    copy_p(4)
                    copy_p(5)
                    act.wait_ge(sem("ev_pv"), g + 1)
                    nc.scalar.activation(E["osq"], psf[:, 6 * 512:6 * 512 + T], ACT.Square).then_inc(sem("ev_osq"), 1)
                    act.wait_ge(sem("ev_inv"), g + 1)
                    nc.scalar.activation(E["ro"], E["ro"], ACT.Sqrt).then_inc(sem("ev_ro"), 1)
                x_back(0)

            def odd():
                o_g = O["o"].rearrange("p (g j) t -> p g j t", j=2)
                act.sem_inc(sem("od_free"), 1)
                with act.Fori(0, 4) as g:
                    for s, (dst, src) in enumerate(((O["q"][:, 0, :], ps[:, 0, :]), (O["q"][:, 1, :], ps[:, 1, :]),
                                                    (O["k"], psf[:, 1024:1024 + T]),
                                                    (O["vT"][0:HEAD, :], psf[0:HEAD, 2048:2048 + T]))):
                        act.wait_ge(readA, readA_after("odd", g, s))
                        nc.scalar.activation(dst, src, ACT.Copy).then_inc(sem("od_cp"), 1)
                    act.wait_ge(sem("od_vtr"), g + 1)
                    nc.scalar.activation(O["vtok"].rearrange("p a b -> p (a b)"), ps[:, 4, 0:NT * HEAD], ACT.Copy) \
                        .then_inc(sem("od_cp"), 1)

                    def exps(u):
                        qt = u % QT
                        w = (min(QT, qt + 2) - max(0, qt - 1)) * P
                        c, at = u % 2, 1024 * (u % 2) + 512 - w
                        act.wait_ge(sem("od_mx"), g * 16 + u + 1)
                        if u >= 2:
                            act.wait_ge(sem("od_tr"), g * 16 + u - 1)
                        nc.scalar.activation(O["p"][:, c, 0:w + CTX], psf[:, at:at + w + CTX], ACT.Exp,
                                             bias=st[:, 8 + c:9 + c], scale=SCALE, accum_out=st[:, 16 + c:17 + c])
                        nc.scalar.activation(st[:, 18 + c:19 + c], one_col(SM("sink"), g, u // QT), ACT.Exp,
                                             bias=st[:, 8 + c:9 + c]).then_inc(sem("od_exp"), 1)

                    def copy_p(u):
                        qt = u % QT
                        n = (min(QT, qt + 2) - max(0, qt - 1)) * P + CTX
                        act.wait_ge(sem("od_tr"), g * 16 + u + 1)
                        if u >= 2:
                            act.wait_ge(sem("od_pv"), g * 16 + u - 1)
                        nc.scalar.activation(O["pT"][:, u % 2, 0:n], psf[:, 2048:2048 + n], ACT.Copy).then_inc(sem("od_pt"), 1)

                    exps(0)
                    for u in range(16):
                        if u < 15:
                            exps(u + 1)
                        copy_p(u)
                    act.wait_ge(sem("od_pv"), g * 16 + 16)
                    nc.scalar.activation(one(o_g, g, 0), ps[:, 6, :], ACT.Copy)
                    nc.scalar.activation(one(o_g, g, 1), ps[:, 7, :], ACT.Copy).then_inc(sem("od_free"), 1)
                act.wait_ge(sem("od_free"), 5)
                act.sem_inc(sem("o_ready"), 1)
                x_back(2)
                act.dma_start(x[:, :, LAT:T], ctx2_in).then_inc(sem("ctx2_in"), 16)

            def copy_out(name, width, n):
                iters, per = COUNT[name]
                a_g = a[:].rearrange("p (g j) t -> p g j t", j=2)
                act.sem_inc(sem(name + "_free"), 2)
                with act.Fori(0, iters) as g:
                    for j in range(2):
                        act.wait_ge(readA, readA_after(name, g, 2 * j + 1))
                        nc.scalar.activation(one(a_g[:, :, :, 0:width], g, j), psf[:, 1024 * j:1024 * j + width], ACT.Copy) \
                            .then_inc(sem(name + "_free"), 1)
                act.wait_ge(sem(name + "_free"), 2 + DC)
                act.sem_inc(sem("y_ready"), 1)

            def hgrn():
                def evacuate(h, s, bank, dst, fn, done, **more):
                    act.wait_ge(readB, readB_after("hg", h, s))
                    return nc.scalar.activation(dst, psf[:, bank * 512:bank * 512 + T], fn, **more).then_inc(sem(done), 1)

                def gate(h, e, d, bank):
                    act.wait_ge(readB, readB_after("hg", h, 2 + d))
                    src = psf[:, bank * 512:bank * 512 + T]
                    nc.scalar.activation(HP[e]["P"][:, d, :], src, ACT.Sigmoid)
                    nc.scalar.activation(HP[e]["k"][:, d, :], src, ACT.Sigmoid, scale=-1.0).then_inc(sem("hg_gate"), 1)

                def values(h, e):
                    act.wait_ge(sem("hg_vtr"), h + 1)
                    nc.scalar.activation(HP[e]["v"].rearrange("p a b -> p (a b)"), psf[:, 1024:1024 + T], ACT.Copy) \
                        .then_inc(sem("hg_v"), 1)

                def step(h, e, follow):
                    nxt, B = h + 1, HP[1 - e]
                    if follow:
                        evacuate(nxt, 0, 0, B["q"], ACT.Silu, "hg_q")
                        evacuate(nxt, 1, 2, H["vT"], ACT.Copy, "hg_vT")
                        gate(nxt, 1 - e, 0, 0)
                        values(nxt, 1 - e)
                        gate(nxt, 1 - e, 1, 2)
                    for d in range(2):
                        act.wait_ge(sem("hg_ktr"), h * 2 + d + 1)
                        nc.scalar.activation(flat(ktok(d)), psf[:, 2048 + 1024 * d:2048 + 1024 * d + T], ACT.Copy) \
                            .then_inc(sem("hg_kt"), 1)
                    if follow:
                        evacuate(nxt, 4, 0, B["z"], ACT.Silu, "hg_z")
                        if isinstance(h, int):
                            act.wait_ge(sem("og_out"), 16 * (HEADS // 2 + 1))
                            act.dma_start(x[:], og_dram).then_inc(sem("og_back"), 16)
                    act.wait_ge(sem("hg_o"), h + 1)
                    nc.scalar.activation(H["kl"][:, 0, :], psf[:, 3072:3072 + T], ACT.Square).then_inc(sem("hg_osq"), 1)
                    act.wait_ge(sem("hg_inv"), h + 2)
                    nc.scalar.activation(rstd[:], rstd[:], ACT.Sqrt).then_inc(sem("hg_ro"), 1)

                evacuate(0, 0, 0, HP[0]["q"], ACT.Silu, "hg_q")
                evacuate(0, 1, 2, H["vT"], ACT.Copy, "hg_vT")
                gate(0, 0, 0, 4)
                values(0, 0)
                gate(0, 0, 1, 6)
                evacuate(0, 4, 0, HP[0]["z"], ACT.Silu, "hg_z")
                with act.Fori(0, HEADS // 2 - 1) as g:
                    for e in range(2):
                        step(g * 2 + e, e, True)
                step(HEADS - 2, 0, True)
                step(HEADS - 1, 1, False)

            def mla():
                act.wait_ge(readA, readA_after("mla_low", 0, 3))
                nc.scalar.activation(M["qa"].rearrange("p a b -> p (a b)"), psf[:, 0:1024], ACT.Copy)
                nc.scalar.activation(M["qsq"].rearrange("p a b -> p (a b)"), psf[:, 0:1024], ACT.Square)
                nc.scalar.activation(M["kva"], psf[:, 1024:1024 + T], ACT.Copy)
                nc.scalar.activation(M["kvsq"], psf[:, 1024:1024 + T], ACT.Square)
                nc.scalar.activation(M["kpe"][0:HEAD, :], psf[0:HEAD, 2048:2048 + T], ACT.Copy).then_inc(sem("ml_low"), 1)
                act.wait_ge(sem("ml_inv"), 1)
                nc.scalar.activation(M["rq"], M["rq"], ACT.Sqrt)
                nc.scalar.activation(M["rk"], M["rk"], ACT.Sqrt).then_inc(sem("ml_rlow"), 1)

                def evacuate(h, e, *names):
                    B = MP[e]
                    v = B["v"].rearrange("p a b -> p (a b)")
                    what = dict(z=(B["z"], ps[:, 7, :], ACT.Silu), qn=(B["qn"], ps[:, 6, :], ACT.Copy),
                                qp=(B["qp"][0:HEAD, :], ps[0:HEAD, 7, :], ACT.Copy), kl=(B["kn"][:, 0:LAT], ps[:, 7, :], ACT.Copy),
                                kc=(B["kn"][:, LAT:T], ps[:, 6, 0:CTX], ACT.Copy), vl=(v[:, 0:LAT], ps[:, 7, :], ACT.Copy),
                                vc=(v[:, LAT:T], ps[:, 6, 0:CTX], ACT.Copy))
                    for n in names:
                        if n in ("z", "vc"):
                            act.wait_ge(readA, mla_read(h, int(n == "vc")))
                        else:
                            act.wait_ge(sem(f"ml_{n}_done"), h + 1)
                        dst, src, fn = what[n]
                        nc.scalar.activation(dst, src, fn).then_inc(sem("ml_" + n), 1)

                def step(h, e, follow):
                    def nxt(*names):
                        if follow:
                            evacuate(h + 1, 1 - e, *names)

                    def exps(u):
                        c = u % 2
                        act.wait_ge(sem("ml_mx"), h * 4 + u + 1)
                        if u >= 2:
                            act.wait_ge(sem("ml_tr"), h * 4 + u - 1)
                        nc.scalar.activation(M["p"][:, c, :], psf[:, 1024 * c:1024 * c + T], ACT.Exp, bias=st[:, 8 + c:9 + c],
                                             scale=MLA_SCALE, accum_out=st[:, 16 + c:17 + c]).then_inc(sem("ml_exp"), 1)

                    def copy_p(u):
                        act.wait_ge(sem("ml_tr"), h * 4 + u + 1)
                        nc.scalar.activation(M["pT"][:, :, u * P:(u + 1) * P],
                                             psf[:, 2048:2048 + T].rearrange("p (n t) -> p n t", t=P), ACT.Copy) \
                            .then_inc(sem("ml_pt"), 1)

                    exps(0)
                    exps(1)
                    nxt("z")
                    copy_p(0)
                    exps(2)
                    nxt("qn", "qp")
                    copy_p(1)
                    exps(3)
                    nxt("kl", "kc")
                    copy_p(2)
                    nxt("vl")
                    copy_p(3)
                    nxt("vc")

                evacuate(0, 0, "z", "qn", "qp", "kl", "kc", "vl", "vc")
                with act.Fori(0, HEADS // 2 - 1) as g:
                    for e in range(2):
                        step(g * 2 + e, e, True)
                step(HEADS - 2, 0, True)
                step(HEADS - 1, 1, False)

            act.wait_ge(sem("smalls_in"), 16)
            nc.scalar.activation(svec[:], smalls[:, 0:32], ACT.Silu).then_inc(sem("svec_ready"), 1)
            act.wait_ge(sem("lb_diff"), 1)
            nc.scalar.activation(lbs[:, 0, :], lbs[:, 0, :], ACT.Exp).then_inc(sem("lb_exp"), 1)
            norm(0)
            act.wait_ge(sem("lam_sum"), 1)
            nc.scalar.activation(E["lam"][:, 2:4], ps[:, 5, 0:2], ACT.Exp).then_inc(sem("lam_exp"), 1)
            even()
            norm(1)
            ffn_in(0, T)
            norm(2)
            odd()
            norm(3)
            ffn_in(1, LAT)
            norm(4)
            norm(5)
            hgrn()
            copy_out("hg_out", T, 6)
            x_back(5)
            act.dma_start(x[:, :, LAT:T], ctx2_in).then_inc(sem("x_back"), 16)
            norm(6)
            norm(7)
            mla()
            copy_out("mla_out", LAT, 8)
            norm(8)

        @block.vector
        def _(dve):
            TT, TS, STT = nc.vector.tensor_tensor, nc.vector.tensor_scalar, nc.vector.scalar_tensor_tensor

            def norm(n):
                gains, l, scale, shift, width = NORMS[n]
                gain = SM(gains)[:, 16 * l:16 * l + 16].rearrange("p (c v) -> p c v", v=2) if scale or shift else None
                if scale:
                    m = MOD[scale, l]
                    STT(coef[:], mod[:, m:m + DC, :], 1.0, gain, ALU.add, ALU.mult)
                elif shift:
                    m = MOD[shift, l]
                    TT(coef[:], mod[:, m:m + DC, :], gain, ALU.mult)
                dve.wait_ge(sem("stat_done"), DC * (n + 1))
                TS(rstd[:, 0:width], psf[:, 0:width], 1.0 / D, EPS, ALU.mult, ALU.add)
                dve.drain()
                nc.vector.reciprocal(rstd[:, 0:width], rstd[:, 0:width]).then_inc(sem("inv_ready"), 1)
                dve.wait_ge(sem("rstd_ready"), n + 1)
                for c in range(DC):
                    for t0, tn, v in pieces(width):
                        t = slice(t0, t0 + tn)
                        if scale:
                            last = STT(a[:, c, t], x[:, c, t], coef[:, c, v:v + 1], rstd[:, t], ALU.mult, ALU.mult)
                        elif shift:
                            STT(a[:, c, t], a[:, c, t], coef[:, c, v:v + 1], rstd[:, t], ALU.mult, ALU.mult)
                        else:
                            STT(x[:, c, t], x[:, c, t], SM(gains)[:, c:c + 1], rstd[:, t], ALU.mult, ALU.mult)
                    if scale:
                        last.then_inc(sem("scaled"), 1)
                if n in SPLIT:
                    for c in range(DC):
                        dve.wait_ge(sem("a_high"), DC * SPLIT.index(n) + c + 1)
                        for t0, tn, v in pieces(width):
                            t, at = slice(t0, t0 + tn), MOD[shift, l] + c
                            last = STT(a_r[:, c, t], a[:, c, t], mod[:, at, v:v + 1], x_r[:, c, t].bitcast(F32),
                                       ALU.add, ALU.subtract)
                    last.then_inc(sem("a_ready"), 1)
                if not scale:
                    dve.drain()
                    if n == 6:
                        dve.wait_ge(sem("x_back"), 16 * 6)
                    if shift:
                        TT(x[:, :, 0:width], x[:, :, 0:width], a[:, :, 0:width], ALU.add)
                        dve.drain()
                    dve.sem_inc(sem("x_ready"), 1)

            def ada_group(group, i, vec):
                for t in range(4):
                    s = t % RC
                    if isinstance(group, int) and group < 4:
                        dve.wait_ge(sem(f"firstC{s}"), group * 32 + 16 * (t // RC + 1))
                    else:
                        dve.wait_ge(sem(f"landedC{s}"), (group - 4) * 32 + 16 * (t // RC + 1))
                    for k in range(2):
                        c = vec + 4 * t + 2 * k
                        for v in range(2):
                            if t == 0 and k == 0:
                                TS(acc[:, i, v, :], ringC[:, s, k, :], svec[:, c + v:c + v + 1], None, ALU.mult)
                            else:
                                last = STT(acc[:, i, v, :], ringC[:, s, k, :], svec[:, c + v:c + v + 1], acc[:, i, v, :],
                                           ALU.mult, ALU.add)
                        if k == 0:
                            dve.drain()
                    last.then_inc(sem("readC"), 1)
                    dve.drain()

            def ada_pair(pair, vec):
                dve.wait_ge(sem("ada_sum"), pair)
                ada_group(pair * 2, 0, vec)
                ada_group(pair * 2 + 1, 1, vec)
                dve.sem_inc(sem("ada_acc"), 1)

            def ada_mod(dst, bias, bank, col):
                TT(dst, ps[:, bank, col:col + 16], bias, ALU.add)

            def ada_places(first, n):
                m = mod[:, 8 * first:8 * (first + n), :].rearrange("p (g c) v -> p g (c v)", c=8)
                b = SM("ada_b")[:, 16 * first:16 * (first + n)].rearrange("p (g c) -> p g c", c=16)
                return m, b

            def residual(name, gate, width, per_n, back, between=None):
                iters, per = COUNT[name]
                J = per // per_n
                x_g = x[:].rearrange("p (g j) t -> p g j t", j=J)
                gate_g = mod[:, gate:gate + DC, :].rearrange("p (g j) v -> p g j v", j=J)
                dve.drain()
                dve.sem_inc(sem(name + "_free"), J)
                dve.wait_ge(sem("x_back"), 16 * back)

                def iteration(g):
                    for j in range(J):
                        dve.wait_ge(readA, readA_after(name, g, (j + 1) * per_n - 1))
                        for t0, tn, v in pieces(width):
                            xs = one(x_g[:, :, :, t0:t0 + tn], g, j)
                            last = STT(xs, psf[:, 1024 * j + t0:1024 * j + t0 + tn], one(gate_g[:, :, :, v:v + 1], g, j),
                                       xs, ALU.mult, ALU.add)
                        last.then_inc(sem(name + "_free"), 1)

                if between:
                    iteration(0)
                    between()
                    iteration(1)
                else:
                    with dve.Fori(0, iters) as g:
                        iteration(g)
                dve.drain()
                dve.sem_inc(sem("x_ready"), 1)

            def ffn_in(l, width):
                name = f"ffn_in{l}"
                dve.drain()
                dve.sem_inc(sem(f"ffn{l}_up_free"), 2)
                m, b = ada_places(6, 11)
                for lo, hi, vec in ((0, 6, 0), (6, 11, 16)):
                    with dve.Fori(lo, hi) as g:
                        if l == 0:
                            ada_pair(g + 6, vec)
                        for j in range(2):
                            dve.wait_ge(readA, readA_after(name, g, 2 * j + 1))
                            dve.wait_ge(sem(f"ffn{l}_gate_free"), g * 2 + j + 3)
                            TT(one(hidden_g[:, :, :, 0:width], g, j), sg[:, j, 0:width],
                               psf[:, (4 * j + 2) * 512:(4 * j + 2) * 512 + width], ALU.mult)
                            if l == 0 and j == 1:
                                ada_mod(flat(m[:, bass.ds(g, 1), :]), flat(b[:, bass.ds(g, 1), :]), 7, 256)
                            dve.drain()
                            dve.sem_inc(sem(f"ffn{l}_up_free"), 1)
                dve.sem_inc(sem("hidden_ready"), 1)

            def rope(dst, rotated, tmp, cos, sin):
                TT(tmp, rotated, sin, ALU.mult)
                TT(dst, dst, cos, ALU.mult)

            def even():
                cos, sin = C("cos128"), C("sin128")
                cat_a, cat_b = E["cat"][:, 0:4, :], E["cat"][:, 4:8, :]
                lam = E["lam"]
                mod_p, bias_p = ada_places(2, 4)
                dve.sem_inc(sem("ev_free"), 1)
                with dve.Fori(0, 4) as g:
                    vps = psf[:, 3072:3072 + T].rearrange("p (n c) -> p n c", c=P)

                    def maxima(u):
                        dve.wait_ge(sem("ev_sc"), g * 6 + u + 1)
                        c, t0 = 4 * (u % 2), 0 if u < QT else LAT
                        for half in range(2):
                            nc.vector.reduce_max(st[:, c + half:c + half + 1], psf[:, half * 1024 + t0:half * 1024 + T], AX_X)
                        dve.drain()
                        TS(st[:, 8 + c:10 + c], st[:, c:c + 2], -SCALE, None, ALU.mult).then_inc(sem("ev_mx"), 1)

                    def difference(u):
                        c, t = 4 * (u % 2), slice(0 if u < QT else LAT, T)
                        p0, p1 = (E["p"][:, 2 * (u % 2) + half, t] for half in range(2))
                        dve.wait_ge(sem("ev_exp"), g * 12 + 2 * u + 2)
                        nc.vector.reciprocal(st[:, 24 + c:26 + c], st[:, 16 + c:18 + c])
                        dve.drain()
                        TT(st[:, 25 + c:26 + c], st[:, 25 + c:26 + c], lam[:, 5:6], ALU.mult)
                        TS(p0, p0, st[:, 24 + c:25 + c], None, ALU.mult)
                        dve.drain()
                        STT(p0, p1, st[:, 25 + c:26 + c], p0, ALU.mult, ALU.add).then_inc(sem("ev_p"), 1)

                    for i, (bank, dst) in enumerate(((6, "q"), (4, "k"))):
                        dve.wait_ge(sem("ev_rot"), g * 2 + i + 1)
                        rope(E[dst][:, 0:LAT], ps[:, bank, :], E["tmp"][:, i, :], cos, sin)
                    dve.drain()
                    for i, dst in enumerate("qk"):
                        last = TT(E[dst][:, 0:LAT], E[dst][:, 0:LAT], E["tmp"][:, i, :], ALU.add)
                    last.then_inc(sem("ev_rope"), 1)
                    maxima(0)
                    difference(0)
                    dve.wait_ge(sem("ada_sum"), g + 2)
                    ada_group(g * 2 + 4, 0, 0)
                    maxima(1)
                    ada_group(g * 2 + 5, 1, 0)
                    dve.sem_inc(sem("ada_acc"), 1)
                    difference(1)
                    maxima(2)
                    difference(2)
                    maxima(3)
                    dve.wait_ge(sem("ev_vtr"), g + 1)
                    for n in range(NT):
                        nc.vector.bn_stats(E["bst"][:, n, :], vps[:, n, :])
                    dve.drain()
                    for n in range(NT):
                        nc.vector.bn_aggr(E["mv"][:, n, :], E["bst"][:, n, :])
                    dve.drain()
                    TS(E["lstd"], E["mv"][:, :, 1], EPS, None, ALU.add)
                    dve.drain()
                    nc.vector.reciprocal(E["lstd"], E["lstd"]).then_inc(sem("ev_vinv"), 1)
                    difference(3)
                    dve.wait_ge(sem("ev_vstd"), g + 1)
                    for n in range(NT):
                        last = TS(E["vtok"][:, n, :], vps[:, n, :], E["mv"][:, n, 0:1], E["lstd"][:, n:n + 1],
                                  ALU.subtract, ALU.mult)
                    last.then_inc(sem("ev_vn"), 1)
                    maxima(4)
                    difference(4)
                    dve.wait_ge(sem("ev_mix"), g + 1)
                    bias = E["sgub"][:, bass.ds(g, 1), :].broadcast_to([P, NT, P])
                    TT(E["mix"].rearrange("p (n c) -> p n c", c=P), vps, bias, ALU.add)
                    dve.drain()
                    TT(flat(cat_a[:, bass.ds(g, 1), :]), E["mix"], E["u"], ALU.mult).then_inc(sem("ev_cat"), 1)
                    maxima(5)
                    difference(5)
                    dve.wait_ge(sem("ada_sum"), g + 3)
                    ada_mod(flat(mod_p[:, bass.ds(g, 1), :]), flat(bias_p[:, bass.ds(g, 1), :]), 0, 0)
                    dve.wait_ge(sem("ev_ms"), g + 1)
                    TS(E["ro"], psf[:, 2048:2048 + T], 1.0 / P, EPS, ALU.mult, ALU.add)
                    dve.drain()
                    nc.vector.reciprocal(E["ro"], E["ro"]).then_inc(sem("ev_inv"), 1)
                    dve.wait_ge(sem("ev_ro"), g + 1)
                    STT(flat(cat_b[:, bass.ds(g, 1), :]), psf[:, 3072:3072 + T], lam[:, 6:7], E["ro"],
                        ALU.mult, ALU.mult).then_inc(sem("ev_free"), 1)
                dve.drain()
                dve.sem_inc(sem("cat_ready"), 1)

            def odd():
                with dve.Fori(0, 4) as g:
                    for i, dst in enumerate((O["q"][:, 0, :], O["q"][:, 1, :], O["k"][:, 0:LAT])):
                        dve.wait_ge(sem("od_rot"), g * 3 + i + 1)
                        rope(dst, ps[:, i, :], O["tmp"][:, i, :], C("cos128"), C("sin128"))
                        dve.drain()
                        last = TT(dst, dst, O["tmp"][:, i, :], ALU.add)
                    last.then_inc(sem("od_rope"), 1)

                    def maxima(u):
                        qt, c = u % QT, u % 2
                        w = (min(QT, qt + 2) - max(0, qt - 1)) * P
                        dve.wait_ge(sem("od_sc"), g * 16 + u + 1)
                        nc.vector.reduce_max(st[:, c:c + 1], psf[:, 1024 * c + 512 - w:1024 * c + 512 + CTX], AX_X)
                        dve.drain()
                        TS(st[:, 2 + c:3 + c], st[:, c:c + 1], SCALE, one_col(SM("sink"), g, u // QT), ALU.mult, ALU.max)
                        dve.drain()
                        TS(st[:, 8 + c:9 + c], st[:, 2 + c:3 + c], -1.0, None, ALU.mult).then_inc(sem("od_mx"), 1)

                    def normalise(u):
                        qt, c = u % QT, u % 2
                        n = (min(QT, qt + 2) - max(0, qt - 1)) * P + CTX
                        dve.wait_ge(sem("od_exp"), g * 16 + u + 1)
                        TT(st[:, 20 + c:21 + c], st[:, 16 + c:17 + c], st[:, 18 + c:19 + c], ALU.add)
                        dve.drain()
                        nc.vector.reciprocal(st[:, 24 + c:25 + c], st[:, 20 + c:21 + c])
                        dve.drain()
                        TS(O["p"][:, c, 0:n], O["p"][:, c, 0:n], st[:, 24 + c:25 + c], None, ALU.mult).then_inc(sem("od_p"), 1)

                    maxima(0)
                    for u in range(16):
                        if u < 15:
                            maxima(u + 1)
                        normalise(u)
                dve.wait_ge(sem("ada_sum"), 18)
                ada_mod(mod[:, 136:144, :].rearrange("p c v -> p (c v)"), SM("ada_b")[:, 272:288], 0, 0)
                dve.drain()

            def hgrn():
                low, oml = (lbs[:, i, :].rearrange("p (d g e) -> p d g e", d=2, e=2) for i in (2, 3))
                og_g = H["og"].rearrange("p (g e) t -> p g e t", e=2)
                G8 = HEADS // 4

                def half(ap, h, i):
                    return ap.rearrange("p (b two h) -> p b two h", two=2, h=h)[:, :, i, :]

                def end(ap, h, i, d):
                    r = h - 1 if d == 0 else 0
                    v = ap.rearrange("p (b two h) -> p b two h", two=2, h=h)[:, :, i, r:r + 1]
                    return v if h == 1 else v.broadcast_to([P, T // (2 * h), h])

                def step(g, e, store):
                    hd, B = g * 2 + e, HP[e]

                    def level(i):
                        h = 1 << i
                        for d in range(2):
                            buf, qh, kh = 2 * d + i % 2, 1 - d, d
                            if i >= 2:
                                dve.wait_ge(sem("hg_A"), (hd * LEVELS + i - 2) * 2 + d + 1)
                            Pd, Sd = B["P"][:, d, :], H["S"][:, d, :]
                            last = TT(H["ql"][:, buf, :].rearrange("p (b h) -> p b h", h=h), half(B["q"], h, qh),
                                      half(Pd, h, qh), ALU.mult)
                            if i > 0:
                                last = TT(half(H["kl"][:, buf, :], h, kh), half(B["k"][:, d, :], h, kh), half(Sd, h, kh), ALU.mult)
                            last.then_inc(sem("hg_lvl"), 1)
                        for d in range(2):
                            qh, kh = 1 - d, d
                            Pd, Sd = B["P"][:, d, :], H["S"][:, d, :]
                            if i == 0:
                                nc.vector.tensor_copy(half(Sd, h, kh), half(Pd, h, qh))
                                nc.vector.memset(half(Sd, h, qh), 1.0)
                            else:
                                TT(half(Sd, h, kh), half(Sd, h, kh), end(Pd, h, qh, d), ALU.mult)
                        dve.drain()
                        for d in range(2):
                            qh, kh = 1 - d, d
                            Pd = B["P"][:, d, :]
                            if d == 1 and i > 0:
                                dve.wait_ge(sem("hg_A"), (hd * LEVELS + i) * 2)
                            TT(half(Pd, h, qh), half(Pd, h, qh), end(Pd, h, kh, d), ALU.mult)
                        dve.drain()

                    def select(i):
                        h = 1 << i
                        for d in range(2):
                            nc.vector.copy_predicated(
                                half(flat(H["A"]), h, 1 - d),
                                lvl[:, d * LEVELS + i, :].rearrange("p (b h) -> p b h", h=h),
                                ps[:, 4 + 2 * d + i % 2, 0:T // 2].rearrange("p (b h) -> p b h", h=h)).then_inc(sem("hg_sel"), 1)

                    for d in range(2):
                        dve.wait_ge(sem("hg_gate"), hd * 2 + d + 1)
                        TS(B["P"][:, d, :], B["P"][:, d, :], oml[:, d, bass.ds(g, 1), e], low[:, d, bass.ds(g, 1), e],
                           ALU.mult, ALU.add)
                        TS(B["k"][:, d, :], B["k"][:, d, :], oml[:, d, bass.ds(g, 1), e], None, ALU.mult)
                    dve.drain()
                    TT(H["kl"][:, 0, :], B["k"][:, 0, :], B["k"][:, 1, :], ALU.add).then_inc(sem("hg_ksum"), 1)
                    dve.wait_ge(sem("hg_q"), hd + 1)
                    level(0)
                    dve.wait_ge(sem("hg_diag"), hd + 1)
                    TT(H["A"], psf[:, 2048:2048 + T].rearrange("p (n c) -> p n c", c=P),
                       ident.unsqueeze(1).broadcast_to([P, NT, P]), ALU.mult).then_inc(sem("hg_init"), 1)
                    for i in range(1, LEVELS):
                        level(i)
                        select(i - 1)
                    dve.wait_ge(sem("hg_A"), (hd + 1) * LEVELS * 2)
                    for d in range(2):
                        TT(H["kl"][:, 2 * d, :], B["q"], B["P"][:, d, :], ALU.mult)
                        TT(H["kl"][:, 2 * d + 1, :], B["k"][:, d, :], H["S"][:, d, :], ALU.mult).then_inc(sem("hg_kS"), 1)
                    dve.drain()
                    select(LEVELS - 1)
                    for i in range(5):
                        for d in range(2):
                            n = CHUNKS[d][i]
                            if i == 0:
                                dve.wait_ge(sem("hg_add"), hd * 2 + d + 1)
                            add = psf[:, (4 - 2 * d) * 512 + n * P:(4 - 2 * d) * 512 + (n + 1) * P]
                            at = n * P + (P - 1 if d == 0 else 0)
                            if i == 0:
                                nc.vector.tensor_copy(state(d, i), add).then_inc(sem(f"hg_state{d}"), 1)
                            else:
                                dve.wait_ge(sem(f"hg_state{d}"), hd * 5 + i)
                                STT(state(d, i), state(d, i - 1), B["P"][:, d, at:at + 1], add, ALU.mult, ALU.add) \
                                    .then_inc(sem(f"hg_state{d}"), 1)
                    dve.wait_ge(sem("hg_ms"), hd + 1)
                    TS(rstd[:], psf[:, 0:T], 1.0 / P, EPS, ALU.mult, ALU.add)
                    dve.drain()
                    nc.vector.reciprocal(rstd[:], rstd[:]).then_inc(sem("hg_inv"), 1)
                    dve.wait_ge(sem("hg_ro"), hd + 1)
                    STT(H["S"][:, 0, :], psf[:, 3072:3072 + T], SM("o_norm"), rstd[:], ALU.mult, ALU.mult)
                    dve.drain()
                    if store:
                        dve.wait_ge(sem("og_out"), 16 * (hd + 1))
                    TT(og_stage if store else one(og_g, g - G8, e), H["S"][:, 0, :], B["z"], ALU.mult) \
                        .then_inc(sem("hg_free"), 1)

                dve.wait_ge(sem("lvl_ready"), NT)
                for buf in (1, 3):
                    nc.vector.memset(H["kl"][:, buf, :], 0.0)
                dve.drain()
                dve.sem_inc(sem("hg_inv"), 1)
                dve.sem_inc(sem("hg_free"), 1)
                dve.sem_inc(sem("og_out"), 16)
                for lo, hi, store in ((0, G8, True), (G8, HEADS // 2 - 1, False)):
                    with dve.Fori(lo, hi) as g:
                        for e in range(2):
                            step(g, e, store)
                for e in range(2):
                    step(HEADS // 2 - 1, e, False)
                dve.drain()
                dve.sem_inc(sem("og_ready"), 1)

            def mla():
                cos, sin = C("cos64")[0:HEAD, :], C("sin64")[0:HEAD, :]
                dve.wait_ge(sem("ml_lowms"), 1)
                TS(M["rq"], ps[:, 0, :], 1.0 / (2 * P), EPS, ALU.mult, ALU.add)
                TS(M["rk"], psf[:, 1024:1024 + T], 1.0 / P, EPS, ALU.mult, ALU.add)
                rope(M["kpe"][0:HEAD, 0:LAT], ps[0:HEAD, 4, :], M["tmp"][0:HEAD, :], cos, sin)
                dve.drain()
                TT(M["kpe"][0:HEAD, 0:LAT], M["kpe"][0:HEAD, 0:LAT], M["tmp"][0:HEAD, :], ALU.add)
                nc.vector.reciprocal(M["rq"], M["rq"])
                nc.vector.reciprocal(M["rk"], M["rk"]).then_inc(sem("ml_inv"), 1)
                dve.wait_ge(sem("ml_rlow"), 1)
                for k in range(2):
                    STT(M["qa"][:, k, :], M["qa"][:, k, :], SM("qa_norm")[:, k:k + 1], M["rq"], ALU.mult, ALU.mult)
                STT(M["kva"], M["kva"], SM("kva_norm"), M["rk"], ALU.mult, ALU.mult).then_inc(sem("ml_lown"), 1)
                dve.sem_inc(sem("ml_free"), 1)
                og_g = M["og"].rearrange("p (g e) t -> p g e t", e=2)

                def rope_q(h, e):
                    q = MP[e]["qp"][0:HEAD, :]
                    dve.wait_ge(sem("ml_rot"), h + 1)
                    rope(q, ps[0:HEAD, 6, :], M["tmp"][0:HEAD, :], cos, sin)
                    dve.drain()
                    TT(q, q, M["tmp"][0:HEAD, :], ALU.add).then_inc(sem("ml_rope"), 1)

                def step(g, e, follow):
                    h = g * 2 + e

                    def maxima(u):
                        c = u % 2
                        dve.wait_ge(sem("ml_sc"), h * 4 + u + 1)
                        nc.vector.reduce_max(st[:, c:c + 1], psf[:, 1024 * c:1024 * c + T], AX_X)
                        dve.drain()
                        TS(st[:, 8 + c:9 + c], st[:, c:c + 1], -MLA_SCALE, None, ALU.mult).then_inc(sem("ml_mx"), 1)

                    def normalise(u):
                        c = u % 2
                        dve.wait_ge(sem("ml_exp"), h * 4 + u + 1)
                        nc.vector.reciprocal(st[:, 24 + c:25 + c], st[:, 16 + c:17 + c])
                        dve.drain()
                        TS(M["p"][:, c, :], M["p"][:, c, :], st[:, 24 + c:25 + c], None, ALU.mult).then_inc(sem("ml_p"), 1)

                    maxima(0)
                    maxima(1)
                    normalise(0)
                    maxima(2)
                    normalise(1)
                    maxima(3)
                    if follow:
                        rope_q(h + 1, 1 - e)
                    normalise(2)
                    normalise(3)
                    dve.wait_ge(sem("ml_pv"), h + 1)
                    TT(one(og_g, g, e), ps[:, 6, :], MP[e]["z"], ALU.mult).then_inc(sem("ml_free"), 1)

                rope_q(0, 0)
                with dve.Fori(0, HEADS // 2 - 1) as g:
                    for e in range(2):
                        step(g, e, True)
                step(HEADS // 2 - 1, 0, True)
                step(HEADS // 2 - 1, 1, False)
                dve.drain()
                dve.sem_inc(sem("ml_og"), 1)

            dve.wait_ge(sem("smalls_in"), 16)
            TT(lbs[:, 0, :], SM("lbl"), SM("lbl"), ALU.subtract).then_inc(sem("lb_diff"), 1)
            TT(E["lam"][:, 0:2], SM("lamv")[:, 0:2], SM("lamv")[:, 2:4], ALU.mult).then_inc(sem("lam_prod"), 1)
            TS(E["lam"][:, 6:7], SM("subln"), 1.0 - LAM_INIT, None, ALU.mult)
            dve.wait_ge(sem("lb_exp"), 1)
            nc.vector.reciprocal(lbs[:, 1, :], lbs[:, 0, :])
            dve.drain()
            TT(lbs[:, 1, :], lbs[:, 0, :], lbs[:, 1, :], ALU.mult)
            dve.drain()
            TT(lbs[:, 2, :], lbs[:, 1, :], lbs[:, 1, :], ALU.subtract)
            dve.drain()
            TS(lbs[:, 3, :], lbs[:, 2, :], -1.0, 1.0, ALU.mult, ALU.add)
            dve.sem_inc(sem("readC"), RC)
            dve.wait_ge(sem("svec_ready"), 1)
            m, b = ada_places(0, 2)
            for pair in range(2):
                if pair:
                    dve.wait_ge(sem("ada_sum"), pair)
                ada_group(2 * pair, 0, 0)
                ada_group(2 * pair + 1, 1, 0)
                dve.sem_inc(sem("ada_acc"), 1)
            for pair in range(2):
                dve.wait_ge(sem("ada_sum"), pair + 1)
                ada_mod(m[:, pair, :], b[:, pair, :], 2 + pair, 0)
            dve.wait_ge(sem("lvl_ready"), NT)
            dve.drain()
            norm(0)
            dve.wait_ge(sem("lam_exp"), 1)
            TT(E["lam"][:, 4:5], E["lam"][:, 3:4], E["lam"][:, 2:3], ALU.subtract)
            dve.drain()
            TS(E["lam"][:, 5:6], E["lam"][:, 4:5], LAM_INIT, None, ALU.subtract)
            dve.drain()
            even()
            residual("even_out", MOD["g1", 0], T, 1, 1)
            norm(1)
            ffn_in(0, T)
            residual("ffn_out0", MOD["g2", 0], T, 3, 2, lambda: ada_pair(17, 16))
            norm(2)
            odd()
            residual("odd_out", MOD["g1", 1], LAT, 1, 3)
            norm(3)
            ffn_in(1, LAT)
            residual("ffn_out1", MOD["g2", 1], LAT, 3, 4)
            norm(4)
            norm(5)
            hgrn()
            norm(6)
            norm(7)
            mla()
            norm(8)


def make_consts(np):
    c = np.zeros((P, N_CONST), np.float32)

    def put(name, v):
        c[:v.shape[0], CONST[name][0]:CONST[name][0] + v.shape[1]] = v

    put("ident", np.eye(P, dtype=np.float32))
    put("ones", np.ones((P, P), np.float32))
    rot = np.zeros((P, P), np.float32)
    for m in range(P):
        if m % 32 < 16:
            rot[m + 16, m] = -1
        else:
            rot[m - 16, m] = 1
    put("rot128", rot)
    rot = np.zeros((HEAD, P), np.float32)
    for m in range(HEAD):
        if m < 32:
            rot[m + 32, m] = -1
        else:
            rot[m - 32, m] = 1
    put("rot64", rot)
    inv = np.float32(10000.0) ** (-np.arange(16, dtype=np.float32) / np.float32(16))
    t = np.arange(LAT)
    pos = np.stack([t // 64, t % 64]).astype(np.float32)
    d = np.arange(P) % HEAD
    ang = pos[d // 32] * inv[d % 16][:, None]
    put("cos128", np.cos(ang))
    put("sin128", np.sin(ang))
    d = np.arange(HEAD) % 32
    ang = pos[d // 16] * inv[d % 16][:, None]
    put("cos64", np.cos(ang))
    put("sin64", np.sin(ang))
    q, k = np.arange(P)[:, None], np.arange(P)[None, :]
    put("maskl", np.where(k >= q, 0, NEG).astype(np.float32))
    put("maskr", np.where(k <= q, 0, NEG).astype(np.float32))
    lv = np.zeros((P, 2 * LEVELS, 64), np.float32)
    s = np.arange(P)
    for dd in range(2):
        for i in range(LEVELS):
            h = 1 << i
            for j in range(64):
                lv[:, dd * LEVELS + i, j] = (s // (2 * h) == j // h) & ((s // h) % 2 == dd)
    return c, lv


def chunked(np, v):
    return v.reshape(-1, P).T


def blocks(np, w):
    k, n = w.shape
    return w.reshape(k // P, P, n // P, P).transpose(2, 1, 0, 3)


def tiles(np, w):
    k, n = w.shape
    kp, np_ = -(-k // D) * D, -(-n // P) * P
    if (kp, np_) != (k, n):
        full = np.zeros((kp, np_), w.dtype)
        full[:k, :n] = w
        w = full
    b = blocks(np, w)
    nb = b.shape[0]
    return b.reshape(nb, P, kp // D, D).transpose(0, 2, 1, 3).reshape(-1, P, D)


def kernel(**inputs):
    import numpy as np
    import concourse.bacc as bacc
    from concourse.bass_utils import run_bass_kernel_spmd

    i = {k: np.asarray(v) for k, v in inputs.items()}

    def interleave(*ts):
        return np.stack(ts, axis=1).reshape(-1, P, D)

    w = i["even_w_in"][0]
    A_, Q_ = 512, 512
    parts = [tiles(np, w[:, at:at + 512]) for at in (1024, 1536, 2048, 512, 0)]
    even = interleave(*parts)

    def ffn(l):
        f = i["ffn_w_in"][l]
        return interleave(tiles(np, f[:, :HID]), tiles(np, f[:, HID:])), tiles(np, i["ffn_w_out"][l])

    f_in0, f_out0 = ffn(0)
    f_in1, f_out1 = ffn(1)
    w = i["odd_w_qkv"][0]
    odd = []
    for g in range(4):
        kg = w[:, 1024 + g * HEAD:1024 + (g + 1) * HEAD]
        odd += [tiles(np, w[:, g * 256:(g + 1) * 256]), tiles(np, np.concatenate([kg, kg], axis=1)),
                tiles(np, w[:, 1280 + g * HEAD:1280 + (g + 1) * HEAD])]
    odd = np.concatenate(odd)
    w = i["hg_w_in_2"][0]
    W2 = 2 * D
    hg = interleave(*[tiles(np, w[:, W2 * n:W2 * (n + 1)]) for n in range(5)])
    w = i["mla_w_in_2"][0]
    low = np.concatenate([tiles(np, w[:, 0:256]), tiles(np, w[:, 256:384]), tiles(np, w[:, 384:448])])
    qb = i["mla_w_qb_2"][0].reshape(2, P, HEADS, 192)
    kvb = i["mla_w_kvb_2"][0].reshape(P, HEADS, 256)
    wb = np.zeros((HEADS, P, D), np.float32)
    for k in range(2):
        wb[:, :, k * P:(k + 1) * P] = qb[k, :, :, 0:P].transpose(1, 0, 2)
        wb[:, :, 256 + k * HEAD:256 + (k + 1) * HEAD] = qb[k, :, :, P:].transpose(1, 0, 2)
    wb[:, :, 384:640] = kvb.transpose(1, 0, 2)
    mla = interleave(tiles(np, w[:, 448:]), wb)
    streamA = np.concatenate(
        [tiles(np, i["even_w_out"][0]), f_in0, f_out0, odd, tiles(np, i["odd_w_out"][0]), f_in1, f_out1,
         tiles(np, i["hg_w_out_2"][0]), low, mla, tiles(np, i["mla_w_out_2"][0])])
    streamB = np.concatenate([even, hg])
    streamC = np.concatenate([w.reshape(4, 2, P, -1, LAT).transpose(3, 0, 2, 1, 4).reshape(-1, P, D)
                              for w in (*i["ada_w"], *i["ada_w_2"])])
    assert len(streamA) == N_A and len(streamB) == N_B and len(streamC) == 4 * GROUPS

    smalls = np.zeros((P, N_SMALL), np.float32)

    def put(name, v):
        v = v.reshape(v.shape[0], -1)
        assert v.shape[1] == SMALL[name][1] - SMALL[name][0], name
        smalls[:v.shape[0], SMALL[name][0]:SMALL[name][1]] = v

    def twice(v):
        return np.repeat(chunked(np, v)[:, :, None], 2, axis=2)

    for tag, name in (("", "cvec"), ("_2", "cvec2")):
        put(name, np.stack([chunked(np, i["c" + tag][0]), chunked(np, i["c_ctx" + tag])], axis=2))
    put("ada_b", twice(np.concatenate([i["ada_b"].ravel(), i["ada_b_2"].ravel()])))
    for name, src in (("norm1_g", "norm1_g"), ("norm2_g", "norm2_g"), ("norm_pre", "norm_pre_2"), ("norm_post", "norm_post_2")):
        put(name, twice(i[src].ravel()))
    put("final_g", chunked(np, i["final_g"]))
    put("subln", i["diff_subln_g"][0][:, None])
    put("lamv", np.stack([i["diff_lq1"][0], i["diff_lq2"][0], i["diff_lk1"][0], i["diff_lk2"][0]], axis=1))
    put("sink", np.broadcast_to(i["odd_sink"][0][None, :], (P, 16)))
    put("lbl", chunked(np, i["hg_lb_logits_2"][0].ravel()))
    put("o_norm", i["hg_o_norm_2"][0][:, None])
    put("qa_norm", chunked(np, i["mla_qa_norm_2"][0]))
    put("kva_norm", i["mla_kva_norm_2"][0][:, None])
    sgu = np.concatenate([i["sgu_w"][0].transpose(2, 0, 1).reshape(P, 512),
                          np.broadcast_to(i["sgu_b"][0].reshape(1, 512), (P, 512))], axis=1)

    def tokens(v):
        return v.T.reshape(DC, P, -1).transpose(1, 0, 2)

    x_in = np.concatenate([tokens(i["x"][0]), tokens(i["ctx"][0])], axis=2)
    consts, lv = make_consts(np)
    arrays = {"streamA": streamA, "streamB": streamB, "streamC": streamC, "x_in": x_in, "ctx2_in": tokens(i["ctx_2"][0]), "smalls_in": smalls,
              "consts_in": consts, "lvl_in": lv, "sgu_in": sgu}
    arrays = {k: np.ascontiguousarray(v) for k, v in arrays.items()}
    nc = bacc.Bacc("TRN2", target_bir_lowering=False, num_devices=1)
    args = [nc.dram_tensor(k, v.shape, mybir.dt.from_np(v.dtype), kind="ExternalInput").ap() for k, v in arrays.items()]
    out = nc.dram_tensor("out", (P, DC, LAT), F32, kind="ExternalOutput").ap()
    build(nc, *args, out)
    r = run_bass_kernel_spmd(nc, [arrays], core_ids=[0])
    y = r.results[0]["out"]
    return y.transpose(2, 1, 0).reshape(1, LAT, D)
```

```python
from contextlib import ExitStack
import math

import concourse.bass as bass
from concourse import mybir

F32 = mybir.dt.float32
F32R = mybir.dt.float32r
U8 = mybir.dt.uint8
ALU = mybir.AluOpType
ACT = mybir.ActivationFunctionType
AX_X = mybir.AxisListType.X

P = 128
D = 1024
DC = D // P
LAT, CTX = 512, 256
T = LAT + CTX
NT = T // P
QT = LAT // P
HID = 2816
HC = HID // P
EPS = 1e-6
HEAD = 64
SCALE = HEAD ** -0.5
LAM_INIT = 0.8 - 0.6 * math.exp(0.0)
HEADS = 16
MLA_SCALE = (128 + 64) ** -0.5
LEVELS = 7
NEG = -1e30
RA, RB, RC = 4, 5, 2
GROUPS = 36

SMALL = {}
_at = 0
for _name, _n in (("cvec", 16), ("cvec2", 16), ("ada_b", 288), ("norm1_g", 32), ("norm2_g", 32), ("final_g", 8),
                  ("norm_pre", 32), ("norm_post", 32), ("subln", 1), ("lamv", 4), ("sink", 16), ("lbl", 32),
                  ("o_norm", 1), ("qa_norm", 2), ("kva_norm", 1)):
    SMALL[_name] = (_at, _at + _n)
    _at += _n
N_SMALL = _at
CONST = {}
_at = 0
for _name, _n in (("ident", 128), ("ones", 128), ("rot128", 128), ("rot64", 128), ("cos128", LAT), ("sin128", LAT),
                  ("cos64", LAT), ("sin64", LAT), ("maskl", 128), ("maskr", 128)):
    CONST[_name] = (_at, _at + _n)
    _at += _n
N_CONST = _at

PLAN_A = [("even_out", 2, 4), ("ffn_in0", 11, 4), ("ffn_out0", 2, 12),
          ("odd", 4, 4), ("odd_out", 2, 4), ("ffn_in1", 11, 4), ("ffn_out1", 2, 12),
          ("hg_out", 4, 4), ("mla_low", 1, 4), ("mla", 8, 4), ("mla_out", 4, 4)]
PLAN_B = [("even", 4, 5), ("hg", 16, 5)]
ORDER = ["even", "even_out", "ffn_in0", "ffn_out0", "odd", "odd_out", "ffn_in1", "ffn_out1",
         "hg", "hg_out", "mla_low", "mla", "mla_out"]


SPLIT_STAGES = ("even", "ffn_in0", "odd", "ffn_in1", "hg")
RH = 3


def starts(plan):
    at, out = 0, {}
    for name, iters, per in plan:
        out[name] = at
        at += iters * per
    return out, at


START_A, N_A = starts(PLAN_A)
START_B, N_B = starts(PLAN_B)
SPLIT_A, _ = starts([s for s in PLAN_A if s[0] in SPLIT_STAGES])
COUNT = {name: (iters, per) for name, iters, per in PLAN_A + PLAN_B}

MOD = {}
for _l in range(2):
    for _i, _name in enumerate(("sh1", "sc1", "g1", "sh2", "sc2", "g2")):
        MOD[_name, _l] = 48 * _l + 8 * _i
    for _i, _name in enumerate(("sh", "sc", "gt")):
        MOD[_name, _l] = 96 + 24 * _l + 8 * _i


def build(nc, streamA, streamB, streamC, x_in, ctx2_in, smalls_in, consts_in, lvl_in, sgu_in, out):
    with ExitStack() as ctx:
        def sb(name, shape, dt=F32):
            return ctx.enter_context(nc.sbuf_tensor(name, shape, dt))

        sems = {}

        def sem(name):
            if name not in sems:
                sems[name] = ctx.enter_context(nc.semaphore(name))
            return sems[name]

        def both(name, shape):
            with nc.sbuf_tensor(name, shape, F32) as v:
                pass
            return v, sb(name + "_r", shape, F32R)

        x, x_r = both("x", [P, DC, T])
        x_dram = nc.dram_tensor("x_scratch", (P, DC, T), F32).ap()
        og_dram = nc.dram_tensor("og_scratch", (P, HEADS // 2, T), F32).ap()
        a, a_r = both("a", [P, DC, T])
        ringA, ringA_r = both("ringA", [P, RA, D])
        ringB, ringB_r = both("ringB", [P, RB, D])
        sq = sb("sq", [P, 2, T])
        rstd = sb("rstd", [P, T])
        consts = sb("consts", [P, N_CONST])
        smalls = sb("smalls", [P, N_SMALL])
        mod = sb("mod", [P, 144, 2])
        coef = sb("coef", [P, DC, 2])
        svec = sb("svec", [P, 32])
        st = sb("st", [P, 64])
        esm = sb("esm", [P, 64])
        lvl = sb("lvl", [P, 2 * LEVELS, NT * 64], U8)
        FREE = 23808
        arena = sb("arena", [P, FREE])
        ps = ctx.enter_context(nc.psum_tensor("ps", [P, 8, 512], F32))
        psf = ps[:].rearrange("p b n -> p (b n)")

        def C(name):
            return consts[:, CONST[name][0]:CONST[name][1]]

        def SM(name):
            return smalls[:, SMALL[name][0]:SMALL[name][1]]

        ident, ones = C("ident"), C("ones")

        def carve():
            at = [0]

            def take(*shape):
                n = math.prod(shape)
                v = arena[:, at[0]:at[0] + n]
                at[0] += n
                assert at[0] <= FREE, at[0]
                if len(shape) == 2:
                    v = v.rearrange("p (a b) -> p a b", b=shape[1])
                elif len(shape) == 3:
                    v = v.rearrange("p (a b c) -> p a b c", b=shape[1], c=shape[2])
                return v
            return take

        def flat(ap):
            return ap.rearrange("p a t -> p (a t)")

        def one(ap, g, j):
            return ap[:, bass.ds(g, 1), j, :].rearrange("p a t -> p (a t)")

        landedA = [sem(f"landedA{s}") for s in range(RA)]
        landedB = [sem(f"landedB{s}") for s in range(RB)]
        readA, readB = sem("readA"), sem("readB")

        def readA_after(name, g, k):
            return RA + START_A[name] + g * COUNT[name][1] + k + 1

        def mla_landed(h, e):
            return 16 * (START_A["mla"] // RA + 1) + (h - e) * 8

        def mla_read(h, k):
            return RA + START_A["mla"] + h * 2 + k + 1

        def readB_after(name, g, k):
            return RB + START_B[name] + g * RB + k + 1

        def landedA_at(name, g, k):
            return 16 * ((START_A[name] + k) // RA + 1) + g * (16 * COUNT[name][1] // RA)

        def splitA_after(name, g, k):
            return SPLIT_A[name] + g * COUNT[name][1] + k + 1

        def splitB_after(name, g, k):
            return START_B[name] + g * RB + k + 1

        def landedB_at(name, g):
            return 16 * (START_B[name] // RB + 1) + g * 16

        tk = carve()
        hidden, sg = tk(HC, T), tk(2, T)
        ADA = (RC * D + 4 * LAT)
        ringC = arena[:, FREE - ADA:FREE - ADA + RC * D].rearrange("p (s k n) -> p s k n", s=RC, k=2)
        acc = arena[:, FREE - 4 * LAT:FREE].rearrange("p (i v n) -> p i v n", i=2, v=2)
        hidden_g = hidden.rearrange("p (g j) t -> p g j t", j=2)
        assert FREE - ADA >= HC * T + 2 * T
        tk = carve()
        E = dict(cat=tk(DC, T), u=tk(T), q=tk(T), k=tk(T), vT=tk(T), vvT=tk(T), vtok=tk(NT, P), vvtok=tk(NT, P),
                 tmp=tk(2, LAT), p=tk(4, T), pT=tk(NT, LAT), sguw=tk(4, P), sgub=tk(4, P))
        assert sum(math.prod(v.shape[1:]) for v in E.values()) <= FREE - ADA
        E.update(mix=E["vT"], pTc=E["vvT"][:, 0:2 * CTX].rearrange("p (a b) -> p a b", b=CTX), osq=sq[:, 0, :], ro=sq[:, 1, :],
                 lam=esm[:, 0:8], lstd=esm[:, 8:14], mv=esm[:, 14:26].rearrange("p (a b) -> p a b", b=2),
                 bst=esm[:, 26:62].rearrange("p (a b) -> p a b", b=6))
        lvl_f = a[:].rearrange("p c t -> p (c t)")[:, 0:2 * LEVELS * 64].rearrange("p (l j) -> p l j", j=64)
        tk = carve()
        O = dict(q=tk(2, LAT), k=tk(T), vT=tk(T), vtok=tk(NT, HEAD), p=tk(2, 640), pT=tk(2, 5 * P), o=tk(DC, LAT),
                 tmp=tk(3, LAT))
        tk = carve()
        H = dict(og=tk(HEADS // 2, T), S=tk(2, T), ql=tk(2, T), kl=tk(4, T))
        HP = [dict(q=tk(T), z=tk(T), P=tk(2, T), k=tk(2, T), v=tk(NT, P)) for _ in range(2)]
        H.update(vT=tk(T), A=rstd[:].rearrange("p (n c) -> p n c", c=P))
        og_stage = ringA[:, RA - 1, 0:T]
        tk = carve()
        M = dict(og=tk(HEADS, LAT), qa=tk(2, LAT), kva=tk(T), kpe=tk(T), p=tk(2, T), pT=tk(NT, LAT), tmp=tk(LAT))
        MP = [dict(qn=tk(LAT), qp=tk(LAT), kn=tk(T), v=tk(NT, P), z=tk(LAT)) for _ in range(2)]
        pTf = M["pT"].rearrange("p a b -> p (a b)")
        M.update(qsq=pTf[:, 0:2 * LAT].rearrange("p (a b) -> p a b", b=LAT), kvsq=pTf[:, 1024:1024 + T],
                 rq=pTf[:, 1792:1792 + LAT], rk=pTf[:, 2304:2304 + T])
        lbs = sb("lbs", [P, 4, 32])

        def pieces(width):
            return [(0, LAT, 0)] + ([(LAT, CTX, 1)] if width == T else [])

        NORMS = [("norm1_g", 0, "sc1", "sh1", T), ("norm2_g", 0, "sc2", "sh2", T),
                 ("norm1_g", 1, "sc1", "sh1", T), ("norm2_g", 1, "sc2", "sh2", LAT),
                 ("final_g", 0, None, None, LAT),
                 ("norm_pre", 0, "sc", "sh", T), ("norm_post", 0, None, "gt", T),
                 ("norm_pre", 1, "sc", "sh", T), ("norm_post", 1, None, "gt", LAT)]
        MODULATED = [0, 1, 2, 3, 5, 7]
        SPLIT = [0, 1, 2, 3, 5]
        SPILL = {1: T, 2: LAT, 3: LAT, 5: LAT}
        SPILLS = list(SPILL)
        X_READY = {1: 1, 2: 2, 3: 3, 4: 4, 5: 5, 7: 6}
        ADA_FFN = (5, 17)
        CHUNKS = [[4, 5, 0, 1, 2, 3], [5, 4, 3, 2, 1, 0]]

        def ktok(d):
            return H["ql"][:, d, :].rearrange("p (b c) -> p b c", c=P)

        def state(d, i):
            at = (d * 5 + i) * P
            return sq[:].rearrange("p a t -> p (a t)")[:, at:at + P]

        def one_col(ap, g, j):
            return ap.rearrange("p (g j) -> p g j", j=4)[:, bass.ds(g, 1), j]

        block = ctx.enter_context(nc.Block())

        @block.sync
        def _(sp):
            sp.dma_start(smalls[:], smalls_in).then_inc(sem("smalls_in"), 16)
            sp.dma_start(lvl_f, lvl_in).then_inc(sem("lvl_in"), 16)
            sp.wait_ge(sem("firstC1"), 16)
            sp.dma_start(x[:], x_in).then_inc(sem("x_in"), 16)
            sp.dma_start(consts[:], consts_in).then_inc(sem("consts_in"), 16)
            sp.dma_start(E["sguw"].rearrange("p a b -> p (a b)"), sgu_in[:, 0:512]).then_inc(sem("sgu_in"), 16)
            sp.dma_start(E["sgub"].rearrange("p a b -> p (a b)"), sgu_in[:, 512:1024]).then_inc(sem("sgu_in"), 16)
            groupsA = streamA.rearrange("(g s) p n -> g s p n", s=RA)
            groupsB = streamB.rearrange("(g s) p n -> g s p n", s=RB)
            groupsC = streamC.rearrange("(g s) p n -> g s p n", s=RC)

            def load_A(g, s):
                sp.wait_ge(readA, g * RA + s + 1)
                sp.dma_start(ringA[:, s, :], groupsA[bass.ds(g, 1), s].rearrange("a p n -> (a p) n")) \
                    .then_inc(landedA[s], 16)

            def load_B(g, s):
                sp.wait_ge(readB, g * RB + s + 1)
                sp.dma_start(ringB[:, s, :], groupsB[bass.ds(g, 1), s].rearrange("a p n -> (a p) n")) \
                    .then_inc(landedB[s], 16)

            def load_C(g, n):
                sp.wait_ge(sem("readC"), (g + n // RC) * RC + n % RC + 1)
                sp.dma_start(ringC[:, n % RC].rearrange("p k n -> p (k n)"),
                             groupsC[bass.ds(g + n // RC, 1), n % RC].rearrange("a p n -> (a p) n")) \
                    .then_inc(sem(f"landedC{n % RC}"), 16)

            def stream_A(name):
                first = START_A[name] // RA
                with sp.Fori(first, first + COUNT[name][0] * COUNT[name][1] // RA) as g:
                    for s in range(RA):
                        load_A(g, s)

            sp.wait_ge(sem("firstC1"), 16 * 5)
            for s in range(RB):
                load_B(0, s)
            with sp.Fori(1, COUNT["even"][0]) as g:
                for n in range(4):
                    load_C(8 + (g - 1) * 4, n)
                for s in range(3):
                    load_B(g, s)
                for n in range(4, 8):
                    load_C(8 + (g - 1) * 4, n)
                for s in range(3, RB):
                    load_B(g, s)
            for n in range(8):
                load_C(8 + (COUNT["even"][0] - 1) * 4, n)
            sp.wait_ge(readB, RB + START_B["hg"])
            stream_A("even_out")

            def stream_ffn(l):
                first, n = START_A[f"ffn_in{l}"] // RA, COUNT[f"ffn_in{l}"][0]
                at_c = 24 * (l + 1)
                for s in range(RA):
                    load_A(first, s)
                load_C(at_c, 0)
                load_C(at_c, 1)
                with sp.Fori(1, n) as g:
                    load_A(g + first, 0)
                    load_C(at_c + (g - 1) * 2, 2)
                    load_C(at_c + (g - 1) * 2, 3)
                    load_A(g + first, 1)
                    load_C(at_c + g * 2, 0)
                    load_C(at_c + g * 2, 1)
                    load_A(g + first, 2)
                    load_A(g + first, 3)
                load_C(at_c + (n - 1) * 2, 2)
                load_C(at_c + (n - 1) * 2, 3)
                first = START_A[f"ffn_out{l}"] // RA
                with sp.Fori(first, first + 3) as g:
                    for s in range(RA):
                        load_A(g, s)
                for k in range(12):
                    load_A(first + 3 + k // RA, k % RA)
                    if k < 4:
                        load_C(at_c + n * 2, k)

            stream_ffn(0)
            stream_A("odd")
            stream_A("odd_out")
            stream_ffn(1)
            first = START_B["hg"] // RB
            for lo, hi, store in ((0, 2, False), (2, 2 + HEADS // 2, True), (2 + HEADS // 2, HEADS, False)):
                with sp.Fori(first + lo, first + hi) as g:
                    for s in range(RB):
                        load_B(g, s)
                    if store:
                        sp.wait_ge(sem("hg_free"), g - first)
                        sp.dma_start(og_dram[:, bass.ds(g - first - 2, 1), :].rearrange("p a t -> p (a t)"), og_stage) \
                            .then_inc(sem("og_out"), 16)
            sp.wait_ge(readB, RB + N_B)
            for name in ("hg_out", "mla_low", "mla", "mla_out"):
                stream_A(name)
            sp.wait_ge(sem("x_ready"), 7)
            sp.dma_start(out, x[:, :, 0:LAT]).then_inc(sem("stored"), 16)
            sp.wait_ge(sem("stored"), 16)

        @block.gpsimd
        def _(pool):
            groupsC = streamC.rearrange("(g s) p n -> g s p n", s=RC)
            with pool.Fori(0, 8) as g:
                for s in range(RC):
                    pool.wait_ge(sem("readC"), g * RC + s + 1)
                    pool.sem_inc(sem("ada_begun"), 1)
                    pool.dma_start(ringC[:, s].rearrange("p k n -> p (k n)"),
                                   groupsC[bass.ds(g, 1), s].rearrange("a p n -> (a p) n")).then_inc(sem(f"firstC{s}"), 16)

            def split(ring, ring_r, slot, high_r, high_slot, done):
                high = high_r[:, high_slot, :]
                nc.gpsimd.tensor_tensor(high, ring[:, slot, :], ones[:, 0:1].broadcast_to([P, D]), ALU.mult)
                pool.drain()
                nc.gpsimd.tensor_tensor(ring_r[:, slot, :], ring[:, slot, :], high.bitcast(F32), ALU.subtract) \
                    .then_inc(sem(done), 1)

            def split_A(name):
                with pool.Fori(0, COUNT[name][0]) as g:
                    for s in range(RA):
                        pool.wait_ge(landedA[s], landedA_at(name, g, s))
                        pool.sem_inc(sem("split_begun"), 1)
                        split(ringA, ringA_r, s, ringB_r, s, "splitA")

            def split_B(name):
                with pool.Fori(0, COUNT[name][0]) as g:
                    for s in range(RB):
                        pool.wait_ge(landedB[s], landedB_at(name, g))
                        pool.wait_ge(readB, readB_after(name, g, s - (RB - RH if s < RB - RH else RH)))
                        pool.sem_inc(sem("split_begun"), 1)
                        split(ringB, ringB_r, s, ringA_r, s % RH, "splitB")

            pool.wait_ge(sem("consts_in"), 16)
            split_B("even")
            split_A("ffn_in0")
            split_A("odd")
            split_A("ffn_in1")
            pool.wait_ge(readA, readA_after("ffn_out1", 1, 11))
            split_B("hg")

        @block.tensor
        def _(pe):
            pe.sem_inc(readA, RA)
            pe.sem_inc(readB, RB)

            def product(ring, slot, src, bank, width, kc=DC, k0=0, start=True, stop=True, m=P, w0=0):
                for k in range(kc):
                    for t0, tn, half in pieces(width):
                        mm = nc.tensor.matmul(ps[0:m, bank + half, 0:tn], ring[:, slot, w0 + k * P:w0 + k * P + m],
                                              src[:, k0 + k, t0:t0 + tn], start=start and k == 0,
                                              stop=stop and k == kc - 1)
                return mm

            def split_product(ring_r, slot, high_r, high_slot, bank, width, ks=range(DC), ready=None):
                for k in ks:
                    w = slice(k * P, (k + 1) * P)
                    if ready is not None:
                        pe.wait_ge(sem("a_ready"), ready + k + 1)
                    for t0, tn, half in pieces(width):
                        t = slice(t0, t0 + tn)
                        for i, (wk, src) in enumerate(((high_r[:, high_slot, w], x_r), (high_r[:, high_slot, w], a_r),
                                                       (ring_r[:, slot, w], x_r))):
                            mm = nc.tensor.matmul(ps[:, bank + half, 0:tn], wk, src[:, k, t], start=k == 0 and i == 0,
                                                  stop=k == DC - 1 and i == 2)
                return mm

            def split_product_A(name, g, s, bank, width, n):
                pe.wait_ge(sem("splitA"), splitA_after(name, g, s))
                split_product(ringA_r, s, ringB_r, s, bank, width, ready=a_before(n) if s == 0 else None).then_inc(readA, 1)

            def split_product_B(name, g, s, bank, n, ks=range(DC)):
                if ks[0] == 0:
                    pe.wait_ge(sem("splitB"), splitB_after(name, g, s))
                mm = split_product(ringB_r, s, ringA_r, s % RH, bank, T, ks, a_before(n) if s == 0 else None)
                if ks[-1] == DC - 1:
                    mm.then_inc(readB, 1)

            def norm_stats(n):
                for c in range(DC):
                    pe.wait_ge(sem("sq_ready"), DC * n + c + 1)
                    for t0, tn, half in pieces(NORMS[n][4]):
                        mm = nc.tensor.matmul(ps[:, half, 0:tn], ones, sq[:, c % 2, t0:t0 + tn],
                                              start=c == 0, stop=c == DC - 1)
                    mm.then_inc(sem("stat_done"), 1)

            def a_before(n):
                return DC * MODULATED.index(n)

            def ada_sum(done, bank, col, groups=2):
                pe.wait_ge(sem("ada_acc"), done + 1)
                for i in range(groups):
                    for c in range(4):
                        for v in range(2):
                            at = col + 8 * i + 2 * c + v
                            mm = nc.tensor.matmul(ps[:, bank, at:at + 1], acc[:, i, v, c * P:(c + 1) * P], ones[:, 0:1],
                                                  start=True, stop=True)
                mm.then_inc(sem("ada_sum"), 1)

            def ada_direct(group):
                at = 2 * (group % 2)
                for t in range(4):
                    s = t % RC
                    pe.wait_ge(sem(f"firstC{s}"), group * 32 + 16 * (t // RC + 1))
                    for k in range(2):
                        for c in range(4):
                            mm = nc.tensor.matmul(ps[:, 4 + c, at:at + 2], ringC[:, s, k, c * P:(c + 1) * P],
                                                  svec[:, 4 * t + 2 * k:4 * t + 2 * k + 2], start=t == 0 and k == 0,
                                                  stop=t == 3 and k == 1)
                    mm.then_inc(sem("readC"), 1)

            def out_product(name, src, width, per_n, low=None):
                iters, per = COUNT[name]
                J = per // per_n
                kall = src.shape[1] + (DC if low is not None else 0)
                with pe.Fori(0, iters) as g:
                    for j in range(J):
                        pe.wait_ge(sem(name + "_free"), g * J + j + 1)
                        for i in range(per_n):
                            k = j * per_n + i
                            kc = min(DC, kall - i * DC)
                            pe.wait_ge(landedA[k % RA], landedA_at(name, g, k))
                            part, k0 = (src, i * DC) if low is None else ((low, src)[i], 0)
                            product(ringA, k % RA, part, 2 * j, width, kc=kc, k0=k0, start=i == 0,
                                    stop=i == per_n - 1).then_inc(readA, 1)

            def ffn_in(l, width):
                name = f"ffn_in{l}"
                with pe.Fori(0, COUNT[name][0]) as g:
                    for s in range(RA):
                        pe.wait_ge(sem(f"ffn{l}_" + ("up_free" if s % 2 else "gate_free")), g * 2 + s // 2 + 1)
                        if s == RA - 1:
                            ada_sum(g + ADA_FFN[l], 7, 256, 1)
                        split_product_A(name, g, s, 2 * s, width, 1 + 2 * l)

            def even():
                name = "even"
                pe.wait_ge(sem("consts_in"), 16)
                pe.wait_ge(sem("lam_prod"), 1)
                nc.tensor.matmul(ps[:, 3, 0:2], ones, E["lam"][:, 0:2], start=True, stop=True).then_inc(sem("lam_sum"), 1)
                with pe.Fori(0, 4) as g:
                    def tile(s, bank):
                        split_product_B(name, g, s, bank, 0)

                    def scores(u):
                        if u > 0:
                            pe.wait_ge(sem("ev_exp"), g * 12 + 2 * u)
                        for half in range(2):
                            r = slice(half * HEAD, (half + 1) * HEAD)
                            lhs = E["q"][r, u * P:(u + 1) * P]
                            if u < QT:
                                nc.tensor.matmul(ps[:, 2 * half, :], lhs, E["k"][r, 0:LAT], start=True, stop=True)
                            mm = nc.tensor.matmul(ps[:, 2 * half + 1, 0:CTX], lhs, E["k"][r, LAT:T], start=True, stop=True)
                        mm.then_inc(sem("ev_sc"), 1)

                    def turn(u):
                        pe.wait_ge(sem("ev_p"), g * 6 + u + 1)
                        if u > 0:
                            pe.wait_ge(sem("ev_pt"), g * 6 + u)
                        for n in range(0 if u < QT else QT, NT):
                            mm = nc.tensor.transpose(psf[:, 4 * 512 + n * P:4 * 512 + (n + 1) * P],
                                                     E["p"][:, 2 * (u % 2), n * P:(n + 1) * P], ident)
                        mm.then_inc(sem("ev_tr2"), 1)

                    def to_tokens(src):
                        for n in range(NT):
                            mm = nc.tensor.transpose(psf[:, 6 * 512 + n * P:6 * 512 + (n + 1) * P],
                                                     E[src][:, n * P:(n + 1) * P], ident)
                        return mm

                    pe.wait_ge(sem("ev_ms_out"), g + 1)
                    tile(0, 0)
                    tile(1, 2)
                    pe.wait_ge(sem("ev_q"), g + 1)
                    nc.tensor.matmul(ps[:, 0, :], C("rot128"), E["q"][:, 0:LAT], start=True, stop=True).then_inc(sem("ev_rot"), 1)
                    pe.wait_ge(sem("ev_k"), g + 1)
                    nc.tensor.matmul(ps[:, 2, :], C("rot128"), E["k"][:, 0:LAT], start=True, stop=True).then_inc(sem("ev_rot"), 1)
                    tile(2, 4)
                    pe.wait_ge(sem("ev_rope"), g + 1)
                    scores(0)
                    pe.wait_ge(sem("ev_free"), g + 1)
                    tile(3, 6)
                    scores(1)
                    pe.wait_ge(sem("ev_v"), g + 1)
                    tile(4, 6)
                    pe.wait_ge(sem("ev_vv"), g + 1)
                    turn(0)
                    scores(2)
                    pe.wait_ge(sem("ev_u"), g + 1)
                    to_tokens("vvT").then_inc(sem("ev_vvtr"), 1)
                    turn(1)
                    scores(3)
                    pe.wait_ge(sem("ev_vvtok"), g + 1)
                    to_tokens("vT").then_inc(sem("ev_vtr"), 1)
                    turn(2)
                    scores(4)
                    turn(3)
                    pe.wait_ge(sem("sgu_in"), 32)
                    pe.wait_ge(sem("ev_vn"), g + 1)
                    for n in range(NT):
                        mm = nc.tensor.matmul(psf[:, 6 * 512 + n * P:6 * 512 + (n + 1) * P], E["vtok"][:, n, :],
                                              flat(E["sguw"][:, bass.ds(g, 1), :]), start=True, stop=True)
                    mm.then_inc(sem("ev_mix"), 1)
                    scores(5)
                    turn(4)
                    pe.wait_ge(sem("ev_cat"), g + 1)
                    for n in range(NT):
                        nc.tensor.matmul(ps[:, 6, :], E["vvtok"][:, n, :], E["pT"][:, n, :], start=n == 0, stop=n == NT - 1)
                    turn(5)
                    ada_sum(g + 1, 0, 0)
                    pe.wait_ge(sem("ev_pt"), g * 6 + 6)
                    for n in range(2):
                        mm = nc.tensor.matmul(ps[:, 7, 0:CTX], E["vvtok"][:, QT + n, :], E["pTc"][:, n, :],
                                              start=n == 0, stop=n == 1)
                    mm.then_inc(sem("ev_pv"), 1)
                    pe.wait_ge(sem("ev_osq"), g + 1)
                    for t0, tn, half in pieces(T):
                        mm = nc.tensor.matmul(ps[:, 4 + half, 0:tn], ones, E["osq"][:, t0:t0 + tn], start=True, stop=True)
                    mm.then_inc(sem("ev_ms"), 1)
                pe.wait_ge(sem("cat_ready"), 1)

            def odd():
                name = "odd"
                with pe.Fori(0, 4) as g:
                    for s, (bank, width) in enumerate(((0, LAT), (1, LAT), (2, T), (4, T))):
                        if s == 0:
                            pe.wait_ge(sem("od_free"), g + 1)
                        split_product_A(name, g, s, bank, width, 2)
                    for i, src in enumerate((O["q"][:, 0, :], O["q"][:, 1, :], O["k"][:, 0:LAT])):
                        pe.wait_ge(sem("od_cp"), g * 5 + i + 1 + i // 2)
                        nc.tensor.matmul(ps[:, i, :], C("rot128"), src, start=True, stop=True).then_inc(sem("od_rot"), 1)
                    for n in range(NT):
                        mm = nc.tensor.transpose(ps[:, 4, n * HEAD:(n + 1) * HEAD], O["vT"][0:HEAD, n * P:(n + 1) * P],
                                                 ident[0:HEAD, 0:HEAD])
                    mm.then_inc(sem("od_vtr"), 1)

                    def scores(u):
                        hh, qt = divmod(u, QT)
                        r = slice((hh % 2) * HEAD, (hh % 2 + 1) * HEAD)
                        lo, hi = max(0, qt - 1) * P, min(QT, qt + 2) * P
                        b, w = 2 * (u % 2), hi - lo
                        lhs = O["q"][r, hh // 2, qt * P:(qt + 1) * P]
                        if u == 0:
                            pe.wait_ge(sem("od_rope"), g + 1)
                        if u >= 2:
                            pe.wait_ge(sem("od_exp"), g * 16 + u - 1)
                        nc.tensor.matmul(ps[:, b, 512 - w:512], lhs, O["k"][r, lo:hi], start=True, stop=False,
                                         skip_group_check=True)
                        if qt > 0:
                            nc.tensor.matmul(ps[:, b, 512 - w:512 - w + P], ident, C("maskl"), start=False, stop=qt == QT - 1,
                                             skip_group_check=True)
                        if qt < QT - 1:
                            nc.tensor.matmul(ps[:, b, 512 - P:512], ident, C("maskr"), start=False, stop=True,
                                             skip_group_check=True)
                        nc.tensor.matmul(ps[:, b + 1, 0:CTX], lhs, O["k"][r, LAT:T], start=True, stop=True) \
                            .then_inc(sem("od_sc"), 1)

                    def turn(u):
                        qt = u % QT
                        w = (min(QT, qt + 2) - max(0, qt - 1)) * P
                        pe.wait_ge(sem("od_p"), g * 16 + u + 1)
                        if u == 0:
                            pe.wait_ge(sem("od_cp"), g * 5 + 5)
                        else:
                            pe.wait_ge(sem("od_pt"), g * 16 + u)
                        for n in range((w + CTX) // P):
                            mm = nc.tensor.transpose(psf[:, 4 * 512 + n * P:4 * 512 + (n + 1) * P],
                                                     O["p"][:, u % 2, n * P:(n + 1) * P], ident)
                        mm.then_inc(sem("od_tr"), 1)

                    def values(u):
                        hh, qt = divmod(u, QT)
                        lo, hi = max(0, qt - 1), min(QT, qt + 2)
                        keys = list(range(lo, hi)) + [QT, QT + 1]
                        r = slice((hh % 2) * HEAD, (hh % 2 + 1) * HEAD)
                        pe.wait_ge(sem("od_pt"), g * 16 + u + 1)
                        for n, key in enumerate(keys):
                            mm = nc.tensor.matmul(ps[r, 6 + hh // 2, qt * P:(qt + 1) * P], O["vtok"][:, key, :],
                                                  O["pT"][:, u % 2, n * P:(n + 1) * P], start=n == 0,
                                                  stop=n == len(keys) - 1)
                        mm.then_inc(sem("od_pv"), 1)

                    scores(0)
                    for u in range(16):
                        if u < 15:
                            scores(u + 1)
                        turn(u)
                        if u > 0:
                            values(u - 1)
                    values(15)
                pe.wait_ge(sem("o_ready"), 1)
                ada_sum(ADA_FFN[0] + 11, 0, 0, 1)

            def hgrn():
                def tile(h, s, bank, ks=range(DC)):
                    split_product_B("hg", h, s, bank, 5, ks)

                def values_to_tokens(h):
                    pe.wait_ge(sem("hg_vT"), h + 1)
                    for n in range(NT):
                        mm = nc.tensor.transpose(psf[:, 1024 + n * P:1024 + (n + 1) * P], H["vT"][:, n * P:(n + 1) * P], ident)
                    mm.then_inc(sem("hg_vtr"), 1)

                def pairs(h, i):
                    p = i % 2
                    pe.wait_ge(sem("hg_lvl"), h * LEVELS + i + 1)
                    if i >= 2:
                        pe.wait_ge(sem("hg_sel"), h * LEVELS + i - 1)
                    for n in range(NT):
                        at = 2048 + 1024 * p + n * P
                        mm = nc.tensor.matmul(psf[:, at:at + P], H["kl"][:, 2 + p, n * P:(n + 1) * P],
                                              H["ql"][:, p, n * P:(n + 1) * P], start=True, stop=True)
                    mm.then_inc(sem("hg_A"), 1)

                def step(h, e, follow, ahead):
                    nxt = h + 1
                    pe.wait_ge(sem("hg_ms_out"), h + 1)
                    pe.wait_ge(sem("hg_ksum"), h + 1)
                    for n in range(NT):
                        mm = nc.tensor.matmul(psf[:, 2048 + n * P:2048 + (n + 1) * P], H["kl"][:, 0, n * P:(n + 1) * P],
                                              HP[e]["q"][:, n * P:(n + 1) * P], start=True, stop=True)
                    mm.then_inc(sem("hg_diag"), 1)
                    if follow:
                        tile(nxt, 1, 2)
                    pe.wait_ge(sem("hg_init"), h + 1)
                    pe.wait_ge(sem("hg_free"), h + 1)
                    first, second = range(DC // 2), range(DC // 2, DC)
                    pairs(h, 0)
                    pairs(h, 1)
                    if follow:
                        pe.wait_ge(sem("hg_q"), nxt + 1)
                        tile(nxt, 2, 0, first)
                    pairs(h, 2)
                    if follow:
                        tile(nxt, 2, 0, second)
                        values_to_tokens(nxt)
                    pairs(h, 3)
                    if follow:
                        pe.wait_ge(sem("hg_v"), nxt + 1)
                        tile(nxt, 3, 2, first)
                    pairs(h, 4)
                    if follow:
                        tile(nxt, 3, 2, second)
                    pairs(h, 5)
                    if follow:
                        pe.wait_ge(sem("hg_gate"), nxt * 2 + 1)
                        tile(nxt, 4, 0, first)
                    pairs(h, 6)
                    if follow:
                        tile(nxt, 4, 0, second)
                    pe.wait_ge(sem("hg_sel"), (h + 1) * LEVELS)
                    for d in range(2):
                        pe.wait_ge(sem("hg_kS"), h * 2 + d + 1)
                        for n in range(NT):
                            at = 2048 + 1024 * d + n * P
                            mm = nc.tensor.transpose(psf[:, at:at + P], H["kl"][:, 2 * d + 1, n * P:(n + 1) * P], ident)
                        mm.then_inc(sem("hg_ktr"), 1)
                    for d in range(2):
                        pe.wait_ge(sem("hg_kt"), h * 2 + d + 1)
                        if d == 1 and follow:
                            pe.wait_ge(sem("hg_gate"), nxt * 2 + 2)
                        bank = 4 - 2 * d
                        for n in range(NT):
                            mm = nc.tensor.matmul(psf[:, bank * 512 + n * P:bank * 512 + (n + 1) * P], ktok(d)[:, n, :],
                                                  HP[e]["v"][:, n, :], start=True, stop=True)
                        mm.then_inc(sem("hg_add"), 1)
                    for n in range(NT):
                        nc.tensor.matmul(psf[:, 3072 + n * P:3072 + (n + 1) * P], HP[e]["v"][:, n, :], H["A"][:, n, :],
                                         start=n % 4 == 0, stop=False, skip_group_check=True)
                    for d in range(2):
                        for i, n in enumerate(CHUNKS[d][1:]):
                            pe.wait_ge(sem(f"hg_state{d}"), h * 5 + i + 1)
                            mm = nc.tensor.matmul(psf[:, 3072 + n * P:3072 + (n + 1) * P], state(d, i),
                                                  H["kl"][:, 2 * d, n * P:(n + 1) * P], start=False,
                                                  stop=d == 1 and n in (0, 4), skip_group_check=True)
                    mm.then_inc(sem("hg_o"), 1)
                    if follow:
                        pe.wait_ge(sem("hg_z"), nxt + 1)
                    if ahead:
                        tile(nxt + 1, 0, 0, first)
                    pe.wait_ge(sem("hg_osq"), h + 1)
                    for t0, tn, half in pieces(T):
                        mm = nc.tensor.matmul(ps[:, 4 + half, 0:tn], ones, H["kl"][:, 0, t0:t0 + tn], start=True, stop=True)
                    mm.then_inc(sem("hg_ms"), 1)
                    if ahead:
                        tile(nxt + 1, 0, 0, second)

                tile(0, 0, 0)
                tile(0, 1, 2)
                tile(0, 2, 4)
                values_to_tokens(0)
                tile(0, 3, 6)
                pe.wait_ge(sem("hg_q"), 1)
                tile(0, 4, 0)
                pe.wait_ge(sem("hg_z"), 1)
                tile(1, 0, 0)
                with pe.Fori(0, HEADS // 2 - 1) as g:
                    for e in range(2):
                        step(g * 2 + e, e, True, True)
                step(HEADS - 2, 0, True, False)
                step(HEADS - 1, 1, False, False)
                pe.wait_ge(sem("og_ready"), 1)

            def mla():
                pe.wait_ge(sem("a_ready"), a_before(7) + DC)
                name = "mla_low"
                for s, (bank, width) in enumerate(((0, LAT), (1, LAT), (2, T), (4, T))):
                    pe.wait_ge(landedA[s], landedA_at(name, 0, s))
                    product(ringA, s, a, bank, width, m=HEAD if s == 3 else P).then_inc(readA, 1)
                pe.wait_ge(sem("ml_low"), 1)
                for k in range(2):
                    nc.tensor.matmul(ps[:, 0, :], ones, M["qsq"][:, k, :], start=k == 0, stop=k == 1)
                for t0, tn, half in pieces(T):
                    nc.tensor.matmul(ps[:, 2 + half, 0:tn], ones, M["kvsq"][:, t0:t0 + tn], start=True, stop=True)
                nc.tensor.matmul(ps[:, 4, :], C("rot64")[0:HEAD, :], M["kpe"][0:HEAD, 0:LAT], start=True, stop=True) \
                    .then_inc(sem("ml_lowms"), 1)
                pe.wait_ge(sem("ml_lown"), 1)

                def project(h, e, piece):
                    W = ringA[:, 2 * e + 1, :]
                    if piece == "z":
                        pe.wait_ge(landedA[2 * e], mla_landed(h, e))
                        if not first(h):
                            pe.wait_ge(sem("ml_vl"), h)
                        product(ringA, 2 * e, a, 7, LAT).then_inc(readA, 1)
                    elif piece == "qn":
                        pe.wait_ge(landedA[2 * e + 1], mla_landed(h, e))
                        if not first(h):
                            pe.wait_ge(sem("ml_free"), h)
                        for k in range(2):
                            mm = nc.tensor.matmul(ps[:, 6, :], W[:, k * P:(k + 1) * P], M["qa"][:, k, :], start=k == 0, stop=k == 1)
                        mm.then_inc(sem("ml_qn_done"), 1)
                    elif piece == "qp":
                        pe.wait_ge(sem("ml_z"), h + 1)
                        for k in range(2):
                            mm = nc.tensor.matmul(ps[0:HEAD, 7, :], W[:, 256 + k * HEAD:256 + (k + 1) * HEAD], M["qa"][:, k, :],
                                                  start=k == 0, stop=k == 1)
                        mm.then_inc(sem("ml_qp_done"), 1)
                    elif piece == "rot":
                        pe.wait_ge(sem("ml_qp"), h + 1)
                        nc.tensor.matmul(ps[:, 6, :], C("rot64")[0:HEAD, :], MP[e]["qp"][0:HEAD, :], start=True, stop=True) \
                            .then_inc(sem("ml_rot"), 1)
                    elif piece == "kl":
                        nc.tensor.matmul(ps[:, 7, :], W[:, 384:512], M["kva"][:, 0:LAT], start=True, stop=True) \
                            .then_inc(sem("ml_kl_done"), 1)
                    elif piece == "kc":
                        pe.wait_ge(sem("ml_rope"), h + 1)
                        nc.tensor.matmul(ps[:, 6, 0:CTX], W[:, 384:512], M["kva"][:, LAT:T], start=True, stop=True) \
                            .then_inc(sem("ml_kc_done"), 1)
                    elif piece == "vl":
                        pe.wait_ge(sem("ml_kl"), h + 1)
                        for n in range(QT):
                            mm = nc.tensor.matmul(ps[:, 7, n * P:(n + 1) * P], M["kva"][:, n * P:(n + 1) * P], W[:, 512:640],
                                                  start=True, stop=True)
                        mm.then_inc(sem("ml_vl_done"), 1)
                    elif piece == "vc":
                        pe.wait_ge(sem("ml_kc"), h + 1)
                        for n in range(2):
                            mm = nc.tensor.matmul(ps[:, 6, n * P:(n + 1) * P], M["kva"][:, (QT + n) * P:(QT + n + 1) * P],
                                                  W[:, 512:640], start=True, stop=True)
                        mm.then_inc(readA, 1)

                def first(h):
                    return isinstance(h, int) and h == 0

                def step(h, e, follow):
                    B = MP[e]

                    def nxt(*names):
                        if follow:
                            for n in names:
                                project(h + 1, 1 - e, n)

                    def scores(u):
                        b = 2 * (u % 2)
                        if u == 0:
                            pe.wait_ge(sem("ml_rope"), h + 1)
                            pe.wait_ge(sem("ml_kc"), h + 1)
                        if u >= 2:
                            pe.wait_ge(sem("ml_exp"), h * 4 + u - 1)
                        for t0, tn, half in pieces(T):
                            nc.tensor.matmul(ps[:, b + half, 0:tn], B["qn"][:, u * P:(u + 1) * P], B["kn"][:, t0:t0 + tn],
                                             start=True, stop=False)
                            mm = nc.tensor.matmul(ps[:, b + half, 0:tn], B["qp"][0:HEAD, u * P:(u + 1) * P],
                                                  M["kpe"][0:HEAD, t0:t0 + tn], start=False, stop=True)
                        mm.then_inc(sem("ml_sc"), 1)

                    def turn(u):
                        pe.wait_ge(sem("ml_p"), h * 4 + u + 1)
                        if u > 0:
                            pe.wait_ge(sem("ml_pt"), h * 4 + u)
                        for n in range(NT):
                            mm = nc.tensor.transpose(psf[:, 4 * 512 + n * P:4 * 512 + (n + 1) * P],
                                                     M["p"][:, u % 2, n * P:(n + 1) * P], ident)
                        mm.then_inc(sem("ml_tr"), 1)

                    scores(0)
                    scores(1)
                    nxt("z")
                    turn(0)
                    scores(2)
                    nxt("qn", "qp")
                    turn(1)
                    scores(3)
                    nxt("rot", "kl")
                    turn(2)
                    nxt("kc", "vl")
                    turn(3)
                    nxt("vc")
                    pe.wait_ge(sem("ml_pt"), h * 4 + 4)
                    if follow:
                        pe.wait_ge(sem("ml_vc"), h + 2)
                    else:
                        pe.wait_ge(sem("ml_vc"), h + 1)
                    for n in range(NT):
                        mm = nc.tensor.matmul(ps[:, 6, :], B["v"][:, n, :], M["pT"][:, n, :], start=n == 0, stop=n == NT - 1)
                    mm.then_inc(sem("ml_pv"), 1)

                for n in ("z", "qn", "qp", "rot", "kl", "kc", "vl", "vc"):
                    project(0, 0, n)
                with pe.Fori(0, HEADS // 2 - 1) as g:
                    for e in range(2):
                        step(g * 2 + e, e, True)
                step(HEADS - 2, 0, True)
                step(HEADS - 1, 1, False)
                pe.wait_ge(sem("ml_og"), 1)

            pe.wait_ge(sem("consts_in"), 16)
            norm_stats(0)
            ada_sum(0, 2, 0)
            pe.wait_ge(sem("svec_ready"), 1)
            ada_direct(2)
            ada_direct(3)
            even()
            out_product("even_out", E["cat"], T, 1)
            norm_stats(1)
            ffn_in(0, T)
            pe.wait_ge(sem("hidden_ready"), 1)
            out_product("ffn_out0", hidden, T, 3)
            norm_stats(2)
            odd()
            out_product("odd_out", O["o"], LAT, 1)
            norm_stats(3)
            ffn_in(1, LAT)
            pe.wait_ge(sem("hidden_ready"), 2)
            out_product("ffn_out1", hidden, LAT, 3)
            ada_sum(ADA_FFN[1] + 11, 7, 256, 1)
            norm_stats(4)
            norm_stats(5)
            hgrn()
            pe.wait_ge(sem("og_back"), 16)
            out_product("hg_out", H["og"], T, 2, low=x)
            norm_stats(6)
            norm_stats(7)
            mla()
            out_product("mla_out", M["og"], LAT, 2)
            norm_stats(8)

        @block.scalar
        def _(act):
            def norm_squares(n):
                _, _, _, _, width = NORMS[n]
                post = n in (6, 8)
                if n == 0:
                    act.wait_ge(sem("x_in"), 16)
                elif post:
                    act.wait_ge(sem("y_ready"), 1 + (n == 8))
                else:
                    act.wait_ge(sem("x_ready"), X_READY[n])
                if n in SPILL:
                    act.dma_start(x_dram[:, :, 0:SPILL[n]], x[:, :, 0:SPILL[n]]).then_inc(sem("x_out"), 16)
                if n == 5:
                    act.wait_ge(sem("ctx2_in"), 16)
                for c in range(DC):
                    if DC * n + c >= 2:
                        act.wait_ge(sem("stat_done"), DC * n + c - 1)
                    nc.scalar.activation(sq[:, c % 2, 0:width], (a if post else x)[:, c, 0:width], ACT.Square) \
                        .then_inc(sem("sq_ready"), 1)

            def norm_root(n):
                width = NORMS[n][4]
                act.wait_ge(sem("inv_ready"), n + 1)
                nc.scalar.activation(rstd[:, 0:width], rstd[:, 0:width], ACT.Sqrt).then_inc(sem("rstd_ready"), 1)

            def norm(n):
                norm_squares(n)
                norm_root(n)
                if n in MODULATED:
                    m = MODULATED.index(n)
                    shift = MOD[NORMS[n][3], NORMS[n][1]]
                    if n in SPILL:
                        act.wait_ge(sem("x_out"), 16 * (SPILLS.index(n) + 1))
                    for c in range(DC):
                        act.wait_ge(sem("scaled"), DC * m + c + 1)
                        for t0, tn, v in pieces(NORMS[n][4]):
                            t = slice(t0, t0 + tn)
                            last = nc.scalar.activation((x_r if n in SPLIT else a)[:, c, t], a[:, c, t], ACT.Identity,
                                                        bias=mod[:, shift + c, v:v + 1])
                        last.then_inc(sem("a_high" if n in SPLIT else "a_ready"), 1)

            def x_back(n):
                w = SPILL.get(n, T)
                act.dma_start(x[:, :, 0:w], x_dram[:, :, 0:w] if n else x_in).then_inc(sem("x_back"), 16)

            def ffn_in(l, width):
                name = f"ffn_in{l}"
                act.sem_inc(sem(f"ffn{l}_gate_free"), 2)
                with act.Fori(0, COUNT[name][0]) as g:
                    for j in range(2):
                        act.wait_ge(readA, readA_after(name, g, 2 * j))
                        act.wait_ge(sem(f"ffn{l}_up_free"), g * 2 + j + 1)
                        nc.scalar.activation(sg[:, j, 0:width], psf[:, 4 * j * 512:4 * j * 512 + width], ACT.Silu) \
                            .then_inc(sem(f"ffn{l}_gate_free"), 1)
                act.wait_ge(readA, readA_after(name, COUNT[name][0] - 1, RA - 1))
                x_back(1 + 2 * l)

            def even():
                with act.Fori(0, 4) as g:
                    def evacuate(s, bank, dst, fn):
                        act.wait_ge(readB, readB_after("even", g, s))
                        nc.scalar.activation(E[dst], psf[:, bank * 512:bank * 512 + T], fn).then_inc(sem("ev_" + dst.rstrip("T")), 1)

                    def exps(u):
                        act.wait_ge(sem("ev_mx"), g * 6 + u + 1)
                        if u >= 2:
                            act.wait_ge(sem("ev_tr2"), g * 6 + u - 1)
                        for half in range(2):
                            t0 = 0 if u < QT else LAT
                            c = 4 * (u % 2) + half
                            nc.scalar.activation(E["p"][:, 2 * (u % 2) + half, t0:T], psf[:, half * 1024 + t0:half * 1024 + T],
                                                 ACT.Exp, bias=st[:, 8 + c:9 + c], scale=SCALE,
                                                 accum_out=st[:, 16 + c:17 + c]).then_inc(sem("ev_exp"), 1)

                    def copy_p(u):
                        act.wait_ge(sem("ev_tr2"), g * 6 + u + 1)
                        if u < QT:
                            dst, src = E["pT"][:, :, u * P:(u + 1) * P], psf[:, 4 * 512:4 * 512 + T]
                        else:
                            dst, src = E["pTc"][:, :, (u - QT) * P:(u - QT + 1) * P], ps[:, 5, 0:CTX]
                        nc.scalar.activation(dst, src.rearrange("p (n t) -> p n t", t=P), ACT.Copy).then_inc(sem("ev_pt"), 1)

                    evacuate(0, 0, "q", ACT.Copy)
                    evacuate(1, 2, "k", ACT.Copy)
                    evacuate(2, 4, "vvT", ACT.Copy)
                    exps(0)
                    evacuate(3, 6, "vT", ACT.Gelu)
                    exps(1)
                    evacuate(4, 6, "u", ACT.Gelu)
                    copy_p(0)
                    exps(2)
                    act.wait_ge(sem("ev_vvtr"), g + 1)
                    nc.scalar.activation(E["vvtok"].rearrange("p a b -> p (a b)"), psf[:, 3072:3072 + T], ACT.Copy) \
                        .then_inc(sem("ev_vvtok"), 1)
                    copy_p(1)
                    exps(3)
                    copy_p(2)
                    act.wait_ge(sem("ev_vinv"), g + 1)
                    nc.scalar.activation(E["lstd"], E["lstd"], ACT.Sqrt).then_inc(sem("ev_vstd"), 1)
                    exps(4)
                    copy_p(3)
                    exps(5)
                    copy_p(4)
                    copy_p(5)
                    act.wait_ge(sem("ev_pv"), g + 1)
                    nc.scalar.activation(E["osq"], psf[:, 6 * 512:6 * 512 + T], ACT.Square).then_inc(sem("ev_osq"), 1)
                    act.wait_ge(sem("ev_inv"), g + 1)
                    nc.scalar.activation(E["ro"], E["ro"], ACT.Sqrt).then_inc(sem("ev_ro"), 1)
                x_back(0)

            def odd():
                o_g = O["o"].rearrange("p (g j) t -> p g j t", j=2)
                act.sem_inc(sem("od_free"), 1)
                with act.Fori(0, 4) as g:
                    for s, (dst, src) in enumerate(((O["q"][:, 0, :], ps[:, 0, :]), (O["q"][:, 1, :], ps[:, 1, :]),
                                                    (O["k"], psf[:, 1024:1024 + T]),
                                                    (O["vT"][0:HEAD, :], psf[0:HEAD, 2048:2048 + T]))):
                        act.wait_ge(readA, readA_after("odd", g, s))
                        nc.scalar.activation(dst, src, ACT.Copy).then_inc(sem("od_cp"), 1)
                    act.wait_ge(sem("od_vtr"), g + 1)
                    nc.scalar.activation(O["vtok"].rearrange("p a b -> p (a b)"), ps[:, 4, 0:NT * HEAD], ACT.Copy) \
                        .then_inc(sem("od_cp"), 1)

                    def exps(u):
                        qt = u % QT
                        w = (min(QT, qt + 2) - max(0, qt - 1)) * P
                        c, at = u % 2, 1024 * (u % 2) + 512 - w
                        act.wait_ge(sem("od_mx"), g * 16 + u + 1)
                        if u >= 2:
                            act.wait_ge(sem("od_tr"), g * 16 + u - 1)
                        nc.scalar.activation(O["p"][:, c, 0:w + CTX], psf[:, at:at + w + CTX], ACT.Exp,
                                             bias=st[:, 8 + c:9 + c], scale=SCALE, accum_out=st[:, 16 + c:17 + c])
                        nc.scalar.activation(st[:, 18 + c:19 + c], one_col(SM("sink"), g, u // QT), ACT.Exp,
                                             bias=st[:, 8 + c:9 + c]).then_inc(sem("od_exp"), 1)

                    def copy_p(u):
                        qt = u % QT
                        n = (min(QT, qt + 2) - max(0, qt - 1)) * P + CTX
                        act.wait_ge(sem("od_tr"), g * 16 + u + 1)
                        if u >= 2:
                            act.wait_ge(sem("od_pv"), g * 16 + u - 1)
                        nc.scalar.activation(O["pT"][:, u % 2, 0:n], psf[:, 2048:2048 + n], ACT.Copy).then_inc(sem("od_pt"), 1)

                    exps(0)
                    for u in range(16):
                        if u < 15:
                            exps(u + 1)
                        copy_p(u)
                    act.wait_ge(sem("od_pv"), g * 16 + 16)
                    nc.scalar.activation(one(o_g, g, 0), ps[:, 6, :], ACT.Copy)
                    nc.scalar.activation(one(o_g, g, 1), ps[:, 7, :], ACT.Copy).then_inc(sem("od_free"), 1)
                act.wait_ge(sem("od_free"), 5)
                act.sem_inc(sem("o_ready"), 1)
                x_back(2)
                act.dma_start(x[:, :, LAT:T], ctx2_in).then_inc(sem("ctx2_in"), 16)

            def copy_out(name, width, n):
                iters, per = COUNT[name]
                a_g = a[:].rearrange("p (g j) t -> p g j t", j=2)
                act.sem_inc(sem(name + "_free"), 2)
                with act.Fori(0, iters) as g:
                    for j in range(2):
                        act.wait_ge(readA, readA_after(name, g, 2 * j + 1))
                        nc.scalar.activation(one(a_g[:, :, :, 0:width], g, j), psf[:, 1024 * j:1024 * j + width], ACT.Copy) \
                            .then_inc(sem(name + "_free"), 1)
                act.wait_ge(sem(name + "_free"), 2 + DC)
                act.sem_inc(sem("y_ready"), 1)

            def hgrn():
                def evacuate(h, s, bank, dst, fn, done, **more):
                    act.wait_ge(readB, readB_after("hg", h, s))
                    return nc.scalar.activation(dst, psf[:, bank * 512:bank * 512 + T], fn, **more).then_inc(sem(done), 1)

                low, oml = (lbs[:, i, :].rearrange("p (d g e) -> p d g e", d=2, e=2) for i in (2, 3))

                def gate(h, e, d, bank):
                    act.wait_ge(readB, readB_after("hg", h, 2 + d))
                    src = psf[:, bank * 512:bank * 512 + T]
                    nc.scalar.activation(HP[e]["P"][:, d, :], src, ACT.Sigmoid)
                    nc.scalar.activation(HP[e]["k"][:, d, :], src, ACT.Sigmoid, scale=-1.0).then_inc(sem("hg_gate"), 1)

                def bounded(g, e, d):
                    P_, k_ = HP[e]["P"][:, d, :], HP[e]["k"][:, d, :]
                    act.drain()
                    nc.scalar.activation(P_, P_, ACT.Identity, bias=low[:, d, bass.ds(g, 1), e], scale=oml[:, d, bass.ds(g, 1), e])
                    nc.scalar.activation(k_, k_, ACT.Copy, scale=oml[:, d, bass.ds(g, 1), e]).then_inc(sem("hg_k"), 1)

                def values(h, e):
                    act.wait_ge(sem("hg_vtr"), h + 1)
                    nc.scalar.activation(HP[e]["v"].rearrange("p a b -> p (a b)"), psf[:, 1024:1024 + T], ACT.Copy) \
                        .then_inc(sem("hg_v"), 1)

                def step(g, e, follow):
                    h, G = g * 2 + e, g + e
                    nxt, B = h + 1, HP[1 - e]
                    if follow:
                        evacuate(nxt, 0, 0, B["q"], ACT.Silu, "hg_q")
                        evacuate(nxt, 1, 2, H["vT"], ACT.Copy, "hg_vT")
                        gate(nxt, 1 - e, 0, 0)
                        values(nxt, 1 - e)
                        bounded(G, 1 - e, 0)
                        gate(nxt, 1 - e, 1, 2)
                        bounded(G, 1 - e, 1)
                    if follow:
                        evacuate(nxt, 4, 0, B["z"], ACT.Silu, "hg_z")
                        if isinstance(h, int):
                            act.wait_ge(sem("og_out"), 16 * (HEADS // 2 + 1))
                            act.dma_start(x[:], og_dram).then_inc(sem("og_back"), 16)
                    for d in range(2):
                        act.wait_ge(sem("hg_ktr"), h * 2 + d + 1)
                        nc.scalar.activation(flat(ktok(d)), psf[:, 2048 + 1024 * d:2048 + 1024 * d + T], ACT.Copy) \
                            .then_inc(sem("hg_kt"), 1)
                    act.wait_ge(sem("hg_o"), h + 1)
                    nc.scalar.activation(H["kl"][:, 0, :], psf[:, 3072:3072 + T], ACT.Square).then_inc(sem("hg_osq"), 1)
                    act.wait_ge(sem("hg_inv"), h + 1)
                    nc.scalar.activation(rstd[:], rstd[:], ACT.Sqrt).then_inc(sem("hg_ro"), 1)

                evacuate(0, 0, 0, HP[0]["q"], ACT.Silu, "hg_q")
                evacuate(0, 1, 2, H["vT"], ACT.Copy, "hg_vT")
                gate(0, 0, 0, 4)
                values(0, 0)
                gate(0, 0, 1, 6)
                for d in range(2):
                    bounded(0, 0, d)
                evacuate(0, 4, 0, HP[0]["z"], ACT.Silu, "hg_z")
                with act.Fori(0, HEADS // 2 - 1) as g:
                    for e in range(2):
                        step(g, e, True)
                step(HEADS // 2 - 1, 0, True)
                step(HEADS // 2 - 1, 1, False)

            def mla():
                act.wait_ge(readA, readA_after("mla_low", 0, 3))
                nc.scalar.activation(M["qa"].rearrange("p a b -> p (a b)"), psf[:, 0:1024], ACT.Copy)
                nc.scalar.activation(M["qsq"].rearrange("p a b -> p (a b)"), psf[:, 0:1024], ACT.Square)
                nc.scalar.activation(M["kva"], psf[:, 1024:1024 + T], ACT.Copy)
                nc.scalar.activation(M["kvsq"], psf[:, 1024:1024 + T], ACT.Square)
                nc.scalar.activation(M["kpe"][0:HEAD, :], psf[0:HEAD, 2048:2048 + T], ACT.Copy).then_inc(sem("ml_low"), 1)
                act.wait_ge(sem("ml_inv"), 1)
                nc.scalar.activation(M["rq"], M["rq"], ACT.Sqrt)
                nc.scalar.activation(M["rk"], M["rk"], ACT.Sqrt).then_inc(sem("ml_rlow"), 1)

                def evacuate(h, e, *names):
                    B = MP[e]
                    v = B["v"].rearrange("p a b -> p (a b)")
                    what = dict(z=(B["z"], ps[:, 7, :], ACT.Silu), qn=(B["qn"], ps[:, 6, :], ACT.Copy),
                                qp=(B["qp"][0:HEAD, :], ps[0:HEAD, 7, :], ACT.Copy), kl=(B["kn"][:, 0:LAT], ps[:, 7, :], ACT.Copy),
                                kc=(B["kn"][:, LAT:T], ps[:, 6, 0:CTX], ACT.Copy), vl=(v[:, 0:LAT], ps[:, 7, :], ACT.Copy),
                                vc=(v[:, LAT:T], ps[:, 6, 0:CTX], ACT.Copy))
                    for n in names:
                        if n in ("z", "vc"):
                            act.wait_ge(readA, mla_read(h, int(n == "vc")))
                        else:
                            act.wait_ge(sem(f"ml_{n}_done"), h + 1)
                        dst, src, fn = what[n]
                        nc.scalar.activation(dst, src, fn).then_inc(sem("ml_" + n), 1)

                def step(h, e, follow):
                    def nxt(*names):
                        if follow:
                            evacuate(h + 1, 1 - e, *names)

                    def exps(u):
                        c = u % 2
                        act.wait_ge(sem("ml_mx"), h * 4 + u + 1)
                        if u >= 2:
                            act.wait_ge(sem("ml_tr"), h * 4 + u - 1)
                        nc.scalar.activation(M["p"][:, c, :], psf[:, 1024 * c:1024 * c + T], ACT.Exp, bias=st[:, 8 + c:9 + c],
                                             scale=MLA_SCALE, accum_out=st[:, 16 + c:17 + c]).then_inc(sem("ml_exp"), 1)

                    def copy_p(u):
                        act.wait_ge(sem("ml_tr"), h * 4 + u + 1)
                        nc.scalar.activation(M["pT"][:, :, u * P:(u + 1) * P],
                                             psf[:, 2048:2048 + T].rearrange("p (n t) -> p n t", t=P), ACT.Copy) \
                            .then_inc(sem("ml_pt"), 1)

                    exps(0)
                    exps(1)
                    nxt("z")
                    copy_p(0)
                    exps(2)
                    nxt("qn", "qp")
                    copy_p(1)
                    exps(3)
                    nxt("kl")
                    copy_p(2)
                    nxt("kc", "vl")
                    copy_p(3)
                    nxt("vc")

                evacuate(0, 0, "z", "qn", "qp", "kl", "kc", "vl", "vc")
                with act.Fori(0, HEADS // 2 - 1) as g:
                    for e in range(2):
                        step(g * 2 + e, e, True)
                step(HEADS - 2, 0, True)
                step(HEADS - 1, 1, False)

            act.wait_ge(sem("smalls_in"), 16)
            nc.scalar.activation(svec[:], smalls[:, 0:32], ACT.Silu).then_inc(sem("svec_ready"), 1)
            act.wait_ge(sem("lb_diff"), 1)
            nc.scalar.activation(lbs[:, 0, :], lbs[:, 0, :], ACT.Exp).then_inc(sem("lb_exp"), 1)
            act.wait_ge(sem("lvl_in"), 16)
            for n in range(NT):
                nc.scalar.activation(lvl[:].rearrange("p l (n j) -> p l n j", j=64)[:, :, n, :], lvl_f, ACT.Copy) \
                    .then_inc(sem("lvl_ready"), 1)
            norm(0)
            act.wait_ge(sem("lam_sum"), 1)
            nc.scalar.activation(E["lam"][:, 2:4], ps[:, 3, 0:2], ACT.Exp).then_inc(sem("lam_exp"), 1)
            even()
            norm(1)
            ffn_in(0, T)
            norm(2)
            odd()
            norm(3)
            ffn_in(1, LAT)
            norm(4)
            norm(5)
            hgrn()
            copy_out("hg_out", T, 6)
            x_back(5)
            act.dma_start(x[:, :, LAT:T], ctx2_in).then_inc(sem("x_back"), 16)
            norm(6)
            norm(7)
            mla()
            copy_out("mla_out", LAT, 8)
            norm(8)

        @block.vector
        def _(dve):
            TT, TS, STT = nc.vector.tensor_tensor, nc.vector.tensor_scalar, nc.vector.scalar_tensor_tensor

            def norm(n):
                gains, l, scale, shift, width = NORMS[n]
                gain = SM(gains)[:, 16 * l:16 * l + 16].rearrange("p (c v) -> p c v", v=2) if scale or shift else None
                if scale:
                    m = MOD[scale, l]
                    STT(coef[:], mod[:, m:m + DC, :], 1.0, gain, ALU.add, ALU.mult)
                elif shift:
                    m = MOD[shift, l]
                    TT(coef[:], mod[:, m:m + DC, :], gain, ALU.mult)
                dve.wait_ge(sem("stat_done"), DC * (n + 1))
                TS(rstd[:, 0:width], psf[:, 0:width], 1.0 / D, EPS, ALU.mult, ALU.add)
                dve.drain()
                nc.vector.reciprocal(rstd[:, 0:width], rstd[:, 0:width]).then_inc(sem("inv_ready"), 1)
                dve.wait_ge(sem("rstd_ready"), n + 1)
                def low(c):
                    dve.wait_ge(sem("a_high"), DC * SPLIT.index(n) + c + 1)
                    for t0, tn, v in pieces(width):
                        t, at = slice(t0, t0 + tn), MOD[shift, l] + c
                        last = STT(a_r[:, c, t], a[:, c, t], mod[:, at, v:v + 1], x_r[:, c, t].bitcast(F32), ALU.add, ALU.subtract)
                    last.then_inc(sem("a_ready"), 1)

                for c in range(DC):
                    for t0, tn, v in pieces(width):
                        t = slice(t0, t0 + tn)
                        if scale:
                            last = STT(a[:, c, t], x[:, c, t], coef[:, c, v:v + 1], rstd[:, t], ALU.mult, ALU.mult)
                        elif shift:
                            STT(a[:, c, t], a[:, c, t], coef[:, c, v:v + 1], rstd[:, t], ALU.mult, ALU.mult)
                        else:
                            STT(x[:, c, t], x[:, c, t], SM(gains)[:, c:c + 1], rstd[:, t], ALU.mult, ALU.mult)
                    if scale:
                        last.then_inc(sem("scaled"), 1)
                    if n in SPLIT and c >= 2:
                        low(c - 2)
                if n in SPLIT:
                    low(DC - 2)
                    low(DC - 1)
                if not scale:
                    dve.drain()
                    if n == 6:
                        dve.wait_ge(sem("x_back"), 16 * 6)
                    if shift:
                        TT(x[:, :, 0:width], x[:, :, 0:width], a[:, :, 0:width], ALU.add)
                        dve.drain()
                    dve.sem_inc(sem("x_ready"), 1)

            def ada_group(group, i, vec):
                for t in range(4):
                    s = t % RC
                    if isinstance(group, int) and group < 4:
                        dve.wait_ge(sem(f"firstC{s}"), group * 32 + 16 * (t // RC + 1))
                    else:
                        dve.wait_ge(sem(f"landedC{s}"), (group - 4) * 32 + 16 * (t // RC + 1))
                    for k in range(2):
                        c = vec + 4 * t + 2 * k
                        for v in range(2):
                            if t == 0 and k == 0:
                                TS(acc[:, i, v, :], ringC[:, s, k, :], svec[:, c + v:c + v + 1], None, ALU.mult)
                            else:
                                last = STT(acc[:, i, v, :], ringC[:, s, k, :], svec[:, c + v:c + v + 1], acc[:, i, v, :],
                                           ALU.mult, ALU.add)
                        if k == 0:
                            dve.drain()
                    last.then_inc(sem("readC"), 1)
                    dve.drain()

            def ada_one(l, g):
                dve.wait_ge(sem("ada_sum"), g + ADA_FFN[l])
                ada_group(g + 12 * (l + 1), 0, 16 * l)
                dve.sem_inc(sem("ada_acc"), 1)

            def ada_mod(dst, bias, bank, col):
                TT(dst, ps[:, bank, col:col + dst.shape[1]], bias, ALU.add)

            def ada_last(l, bank, col):
                dve.wait_ge(sem("ada_sum"), ADA_FFN[l] + 12)
                m, b = ada_places(12 * (l + 1) + 11, 1, 4)
                ada_mod(m[:, 0, :], b[:, 0, :], bank, col)
                dve.drain()

            def ada_places(first, n, c=8):
                m = mod[:, c * first:c * (first + n), :].rearrange("p (g c) v -> p g (c v)", c=c)
                b = SM("ada_b")[:, 2 * c * first:2 * c * (first + n)].rearrange("p (g c) -> p g c", c=2 * c)
                return m, b

            def residual(name, gate, width, per_n, back, between=None):
                iters, per = COUNT[name]
                J = per // per_n
                x_g = x[:].rearrange("p (g j) t -> p g j t", j=J)
                gate_g = mod[:, gate:gate + DC, :].rearrange("p (g j) v -> p g j v", j=J)
                dve.drain()
                dve.sem_inc(sem(name + "_free"), J)
                dve.wait_ge(sem("x_back"), 16 * back)

                def iteration(g):
                    for j in range(J):
                        dve.wait_ge(readA, readA_after(name, g, (j + 1) * per_n - 1))
                        for t0, tn, v in pieces(width):
                            xs = one(x_g[:, :, :, t0:t0 + tn], g, j)
                            last = STT(xs, psf[:, 1024 * j + t0:1024 * j + t0 + tn], one(gate_g[:, :, :, v:v + 1], g, j),
                                       xs, ALU.mult, ALU.add)
                        last.then_inc(sem(name + "_free"), 1)

                if between:
                    iteration(0)
                    between()
                    iteration(1)
                else:
                    with dve.Fori(0, iters) as g:
                        iteration(g)
                dve.drain()
                dve.sem_inc(sem("x_ready"), 1)

            def ffn_in(l, width):
                name = f"ffn_in{l}"
                dve.drain()
                dve.sem_inc(sem(f"ffn{l}_up_free"), 2)
                m, b = ada_places(12 * (l + 1), 11, 4)
                with dve.Fori(0, COUNT[name][0]) as g:
                    ada_one(l, g)
                    for j in range(2):
                        dve.wait_ge(readA, readA_after(name, g, 2 * j + 1))
                        dve.wait_ge(sem(f"ffn{l}_gate_free"), g * 2 + j + 3)
                        TT(one(hidden_g[:, :, :, 0:width], g, j), sg[:, j, 0:width],
                           psf[:, (4 * j + 2) * 512:(4 * j + 2) * 512 + width], ALU.mult)
                        if j == 1:
                            ada_mod(flat(m[:, bass.ds(g, 1), :]), flat(b[:, bass.ds(g, 1), :]), 7, 256)
                        dve.drain()
                        dve.sem_inc(sem(f"ffn{l}_up_free"), 1)
                dve.sem_inc(sem("hidden_ready"), 1)

            def rope(dst, rotated, tmp, cos, sin):
                TT(tmp, rotated, sin, ALU.mult)
                TT(dst, dst, cos, ALU.mult)

            def even():
                cos, sin = C("cos128"), C("sin128")
                cat_a, cat_b = E["cat"][:, 0:4, :], E["cat"][:, 4:8, :]
                lam = E["lam"]
                mod_p, bias_p = ada_places(2, 4)
                dve.sem_inc(sem("ev_free"), 1)
                dve.sem_inc(sem("ev_ms_out"), 1)
                with dve.Fori(0, 4) as g:
                    vps = psf[:, 3072:3072 + T].rearrange("p (n c) -> p n c", c=P)

                    def maxima(u):
                        dve.wait_ge(sem("ev_sc"), g * 6 + u + 1)
                        c, t0 = 4 * (u % 2), 0 if u < QT else LAT
                        for half in range(2):
                            nc.vector.reduce_max(st[:, c + half:c + half + 1], psf[:, half * 1024 + t0:half * 1024 + T], AX_X)
                        dve.drain()
                        TS(st[:, 8 + c:10 + c], st[:, c:c + 2], -SCALE, None, ALU.mult).then_inc(sem("ev_mx"), 1)

                    def difference(u):
                        c, t = 4 * (u % 2), slice(0 if u < QT else LAT, T)
                        p0, p1 = (E["p"][:, 2 * (u % 2) + half, t] for half in range(2))
                        dve.wait_ge(sem("ev_exp"), g * 12 + 2 * u + 2)
                        nc.vector.reciprocal(st[:, 24 + c:26 + c], st[:, 16 + c:18 + c])
                        dve.drain()
                        TT(st[:, 25 + c:26 + c], st[:, 25 + c:26 + c], lam[:, 5:6], ALU.mult)
                        TS(p0, p0, st[:, 24 + c:25 + c], None, ALU.mult)
                        dve.drain()
                        STT(p0, p1, st[:, 25 + c:26 + c], p0, ALU.mult, ALU.add).then_inc(sem("ev_p"), 1)

                    dve.wait_ge(sem("ada_sum"), g + 1)
                    ada_group(g * 2 + 4, 0, 0)
                    for i, (bank, dst) in enumerate(((0, "q"), (2, "k"))):
                        dve.wait_ge(sem("ev_rot"), g * 2 + i + 1)
                        rope(E[dst][:, 0:LAT], ps[:, bank, :], E["tmp"][:, i, :], cos, sin)
                    dve.drain()
                    for i, dst in enumerate("qk"):
                        last = TT(E[dst][:, 0:LAT], E[dst][:, 0:LAT], E["tmp"][:, i, :], ALU.add)
                    last.then_inc(sem("ev_rope"), 1)
                    maxima(0)
                    difference(0)
                    ada_group(g * 2 + 5, 1, 0)
                    dve.sem_inc(sem("ada_acc"), 1)
                    maxima(1)
                    difference(1)
                    maxima(2)
                    difference(2)
                    maxima(3)
                    dve.wait_ge(sem("ev_vtr"), g + 1)
                    for n in range(NT):
                        nc.vector.bn_stats(E["bst"][:, n, :], vps[:, n, :])
                    dve.drain()
                    for n in range(NT):
                        nc.vector.bn_aggr(E["mv"][:, n, :], E["bst"][:, n, :])
                    dve.drain()
                    TS(E["lstd"], E["mv"][:, :, 1], EPS, None, ALU.add)
                    dve.drain()
                    nc.vector.reciprocal(E["lstd"], E["lstd"]).then_inc(sem("ev_vinv"), 1)
                    difference(3)
                    dve.wait_ge(sem("ev_vstd"), g + 1)
                    for n in range(NT):
                        last = TS(E["vtok"][:, n, :], vps[:, n, :], E["mv"][:, n, 0:1], E["lstd"][:, n:n + 1],
                                  ALU.subtract, ALU.mult)
                    last.then_inc(sem("ev_vn"), 1)
                    maxima(4)
                    difference(4)
                    dve.wait_ge(sem("ev_mix"), g + 1)
                    bias = E["sgub"][:, bass.ds(g, 1), :].broadcast_to([P, NT, P])
                    TT(E["mix"].rearrange("p (n c) -> p n c", c=P), vps, bias, ALU.add)
                    dve.drain()
                    TT(flat(cat_a[:, bass.ds(g, 1), :]), E["mix"], E["u"], ALU.mult).then_inc(sem("ev_cat"), 1)
                    maxima(5)
                    difference(5)
                    dve.wait_ge(sem("ada_sum"), g + 2)
                    ada_mod(flat(mod_p[:, bass.ds(g, 1), :]), flat(bias_p[:, bass.ds(g, 1), :]), 0, 0)
                    dve.wait_ge(sem("ev_ms"), g + 1)
                    TS(E["ro"], psf[:, 2048:2048 + T], 1.0 / P, EPS, ALU.mult, ALU.add).then_inc(sem("ev_ms_out"), 1)
                    dve.drain()
                    nc.vector.reciprocal(E["ro"], E["ro"]).then_inc(sem("ev_inv"), 1)
                    dve.wait_ge(sem("ev_ro"), g + 1)
                    STT(flat(cat_b[:, bass.ds(g, 1), :]), psf[:, 3072:3072 + T], lam[:, 6:7], E["ro"],
                        ALU.mult, ALU.mult).then_inc(sem("ev_free"), 1)
                dve.drain()
                dve.sem_inc(sem("cat_ready"), 1)

            def odd():
                with dve.Fori(0, 4) as g:
                    for i, dst in enumerate((O["q"][:, 0, :], O["q"][:, 1, :], O["k"][:, 0:LAT])):
                        dve.wait_ge(sem("od_rot"), g * 3 + i + 1)
                        rope(dst, ps[:, i, :], O["tmp"][:, i, :], C("cos128"), C("sin128"))
                        dve.drain()
                        last = TT(dst, dst, O["tmp"][:, i, :], ALU.add)
                    last.then_inc(sem("od_rope"), 1)

                    def maxima(u):
                        qt, c = u % QT, u % 2
                        w = (min(QT, qt + 2) - max(0, qt - 1)) * P
                        dve.wait_ge(sem("od_sc"), g * 16 + u + 1)
                        nc.vector.reduce_max(st[:, c:c + 1], psf[:, 1024 * c + 512 - w:1024 * c + 512 + CTX], AX_X)
                        dve.drain()
                        TS(st[:, 2 + c:3 + c], st[:, c:c + 1], SCALE, one_col(SM("sink"), g, u // QT), ALU.mult, ALU.max)
                        dve.drain()
                        TS(st[:, 8 + c:9 + c], st[:, 2 + c:3 + c], -1.0, None, ALU.mult).then_inc(sem("od_mx"), 1)

                    def normalise(u):
                        qt, c = u % QT, u % 2
                        n = (min(QT, qt + 2) - max(0, qt - 1)) * P + CTX
                        dve.wait_ge(sem("od_exp"), g * 16 + u + 1)
                        TT(st[:, 20 + c:21 + c], st[:, 16 + c:17 + c], st[:, 18 + c:19 + c], ALU.add)
                        dve.drain()
                        nc.vector.reciprocal(st[:, 24 + c:25 + c], st[:, 20 + c:21 + c])
                        dve.drain()
                        TS(O["p"][:, c, 0:n], O["p"][:, c, 0:n], st[:, 24 + c:25 + c], None, ALU.mult).then_inc(sem("od_p"), 1)

                    maxima(0)
                    for u in range(16):
                        normalise(u)
                        if u < 15:
                            maxima(u + 1)
                ada_last(0, 0, 0)

            def hgrn():
                og_g = H["og"].rearrange("p (g e) t -> p g e t", e=2)
                G8 = HEADS // 4

                def half(ap, h, i):
                    return ap.rearrange("p (n b two h) -> p n b two h", n=NT, two=2, h=h)[:, :, :, i, :]

                def side(ap, h, d):
                    return ap.rearrange("p (n d b h) -> p n d b h", n=NT, d=2, h=h)[:, :, d, :, :]

                def end(ap, h, i, d):
                    r = h - 1 if d == 0 else 0
                    v = half(ap, h, i)[:, :, :, r:r + 1]
                    return v if h == 1 else v.broadcast_to([P, NT, HEAD // h, h])

                def level(hd, e, i):
                    B, h, p = HP[e], 1 << i, i % 2
                    keys = H["kl"][:, 2 + p, :]
                    if i >= 2:
                        dve.wait_ge(sem("hg_A"), hd * LEVELS + i - 1)
                    for d in range(2):
                        qh, kh = 1 - d, d
                        Pd, Sd = B["P"][:, d, :], H["S"][:, d, :]
                        TT(side(H["ql"][:, p, :], h, d), half(B["q"], h, qh), half(Pd, h, qh), ALU.mult)
                        if i > 0:
                            last = TT(half(keys, h, kh), half(B["k"][:, d, :], h, kh), half(Sd, h, kh), ALU.mult)
                        else:
                            last = nc.vector.tensor_copy(half(keys, h, kh), half(B["k"][:, d, :], h, kh))
                    last.then_inc(sem("hg_lvl"), 1)
                    for d in range(2):
                        qh, kh = 1 - d, d
                        Pd, Sd = B["P"][:, d, :], H["S"][:, d, :]
                        if i == 0:
                            nc.vector.tensor_copy(half(Sd, h, kh), half(Pd, h, qh))
                            nc.vector.memset(half(Sd, h, qh), 1.0)
                        else:
                            TT(half(Sd, h, kh), half(Sd, h, kh), end(Pd, h, qh, d), ALU.mult)
                    dve.drain()
                    for d in range(2):
                        qh, kh = 1 - d, d
                        Pd = B["P"][:, d, :]
                        if d == 1 and i > 0:
                            dve.wait_ge(sem("hg_A"), hd * LEVELS + i)
                        TT(half(Pd, h, qh), half(Pd, h, qh), end(Pd, h, kh, d), ALU.mult)
                    dve.drain()

                def select(e, i):
                    h = 1 << i
                    at = 2048 + 1024 * (i % 2)
                    for d in range(2):
                        last = nc.vector.copy_predicated(
                            half(flat(H["A"]), h, 1 - d),
                            lvl[:, d * LEVELS + i, :].rearrange("p (n b h) -> p n b h", n=NT, h=h),
                            side(psf[:, at:at + T], h, d))
                    last.then_inc(sem("hg_sel"), 1)

                def prepare(g, e):
                    hd, B = g * 2 + e, HP[e]
                    dve.wait_ge(sem("hg_k"), hd * 2 + 2)
                    TT(H["kl"][:, 0, :], B["k"][:, 0, :], B["k"][:, 1, :], ALU.add).then_inc(sem("hg_ksum"), 1)

                def begin(g, e):
                    dve.wait_ge(sem("hg_q"), g * 2 + e + 1)
                    level(g * 2 + e, e, 0)

                def step(g, e, store, follow):
                    hd, B = g * 2 + e, HP[e]
                    dve.wait_ge(sem("hg_diag"), hd + 1)
                    TT(H["A"], psf[:, 2048:2048 + T].rearrange("p (n c) -> p n c", c=P),
                       ident.unsqueeze(1).broadcast_to([P, NT, P]), ALU.mult).then_inc(sem("hg_init"), 1)
                    for i in range(1, LEVELS):
                        level(hd, e, i)
                        select(e, i - 1)
                    dve.drain()
                    dve.wait_ge(sem("hg_A"), (hd + 1) * LEVELS)
                    for d in range(2):
                        TT(H["kl"][:, 2 * d + 1, :], B["k"][:, d, :], H["S"][:, d, :], ALU.mult).then_inc(sem("hg_kS"), 1)
                        if d == 0:
                            select(e, LEVELS - 1)
                    for d in range(2):
                        TT(H["kl"][:, 2 * d, :], B["q"], B["P"][:, d, :], ALU.mult)
                    dve.drain()
                    for i in range(5):
                        for d in range(2):
                            n = CHUNKS[d][i]
                            if i == 0:
                                dve.wait_ge(sem("hg_add"), hd * 2 + d + 1)
                            add = psf[:, (4 - 2 * d) * 512 + n * P:(4 - 2 * d) * 512 + (n + 1) * P]
                            at = n * P + (P - 1 if d == 0 else 0)
                            if i == 0:
                                nc.vector.tensor_copy(state(d, i), add).then_inc(sem(f"hg_state{d}"), 1)
                            else:
                                dve.wait_ge(sem(f"hg_state{d}"), hd * 5 + i)
                                STT(state(d, i), state(d, i - 1), B["P"][:, d, at:at + 1], add, ALU.mult, ALU.add) \
                                    .then_inc(sem(f"hg_state{d}"), 1)
                    dve.wait_ge(sem("hg_ms"), hd + 1)
                    TS(rstd[:], psf[:, 2048:2048 + T], 1.0 / P, EPS, ALU.mult, ALU.add).then_inc(sem("hg_ms_out"), 1)
                    if follow:
                        prepare(*follow)
                    dve.drain()
                    nc.vector.reciprocal(rstd[:], rstd[:]).then_inc(sem("hg_inv"), 1)
                    if follow:
                        begin(*follow)
                    dve.wait_ge(sem("hg_ro"), hd + 1)
                    STT(B["z"], B["z"], SM("o_norm"), rstd[:], ALU.mult, ALU.mult)
                    dve.drain()
                    if store:
                        dve.wait_ge(sem("og_out"), 16 * (hd + 1))
                    TT(og_stage if store else one(og_g, g - G8, e), psf[:, 3072:3072 + T], B["z"], ALU.mult) \
                        .then_inc(sem("hg_free"), 1)

                dve.wait_ge(sem("lvl_ready"), NT)
                dve.sem_inc(sem("hg_ms_out"), 1)
                dve.sem_inc(sem("hg_free"), 1)
                dve.sem_inc(sem("og_out"), 16)
                prepare(0, 0)
                begin(0, 0)
                for lo, hi, store in ((0, G8, True), (G8, HEADS // 2 - 1, False)):
                    with dve.Fori(lo, hi) as g:
                        step(g, 0, store, (g, 1))
                        step(g, 1, store, (g + 1, 0))
                g = HEADS // 2 - 1
                step(g, 0, False, (g, 1))
                step(g, 1, False, None)
                dve.drain()
                dve.sem_inc(sem("og_ready"), 1)

            def mla():
                cos, sin = C("cos64")[0:HEAD, :], C("sin64")[0:HEAD, :]
                dve.wait_ge(sem("ml_lowms"), 1)
                TS(M["rq"], ps[:, 0, :], 1.0 / (2 * P), EPS, ALU.mult, ALU.add)
                TS(M["rk"], psf[:, 1024:1024 + T], 1.0 / P, EPS, ALU.mult, ALU.add)
                rope(M["kpe"][0:HEAD, 0:LAT], ps[0:HEAD, 4, :], M["tmp"][0:HEAD, :], cos, sin)
                dve.drain()
                TT(M["kpe"][0:HEAD, 0:LAT], M["kpe"][0:HEAD, 0:LAT], M["tmp"][0:HEAD, :], ALU.add)
                nc.vector.reciprocal(M["rq"], M["rq"])
                nc.vector.reciprocal(M["rk"], M["rk"]).then_inc(sem("ml_inv"), 1)
                dve.wait_ge(sem("ml_rlow"), 1)
                for k in range(2):
                    STT(M["qa"][:, k, :], M["qa"][:, k, :], SM("qa_norm")[:, k:k + 1], M["rq"], ALU.mult, ALU.mult)
                STT(M["kva"], M["kva"], SM("kva_norm"), M["rk"], ALU.mult, ALU.mult).then_inc(sem("ml_lown"), 1)
                dve.sem_inc(sem("ml_free"), 1)
                og_g = M["og"].rearrange("p (g e) t -> p g e t", e=2)

                def rope_q(h, e):
                    q = MP[e]["qp"][0:HEAD, :]
                    dve.wait_ge(sem("ml_rot"), h + 1)
                    rope(q, ps[0:HEAD, 6, :], M["tmp"][0:HEAD, :], cos, sin)
                    dve.drain()
                    TT(q, q, M["tmp"][0:HEAD, :], ALU.add).then_inc(sem("ml_rope"), 1)

                def step(g, e, follow):
                    h = g * 2 + e

                    def maxima(u):
                        c = u % 2
                        dve.wait_ge(sem("ml_sc"), h * 4 + u + 1)
                        nc.vector.reduce_max(st[:, c:c + 1], psf[:, 1024 * c:1024 * c + T], AX_X)
                        dve.drain()
                        TS(st[:, 8 + c:9 + c], st[:, c:c + 1], -MLA_SCALE, None, ALU.mult).then_inc(sem("ml_mx"), 1)

                    def normalise(u):
                        c = u % 2
                        dve.wait_ge(sem("ml_exp"), h * 4 + u + 1)
                        nc.vector.reciprocal(st[:, 24 + c:25 + c], st[:, 16 + c:17 + c])
                        dve.drain()
                        TS(M["p"][:, c, :], M["p"][:, c, :], st[:, 24 + c:25 + c], None, ALU.mult).then_inc(sem("ml_p"), 1)

                    maxima(0)
                    maxima(1)
                    normalise(0)
                    maxima(2)
                    normalise(1)
                    normalise(2)
                    maxima(3)
                    if follow:
                        rope_q(h + 1, 1 - e)
                    normalise(3)
                    dve.wait_ge(sem("ml_pv"), h + 1)
                    TT(one(og_g, g, e), ps[:, 6, :], MP[e]["z"], ALU.mult).then_inc(sem("ml_free"), 1)

                rope_q(0, 0)
                with dve.Fori(0, HEADS // 2 - 1) as g:
                    for e in range(2):
                        step(g, e, True)
                step(HEADS // 2 - 1, 0, True)
                step(HEADS // 2 - 1, 1, False)
                dve.drain()
                dve.sem_inc(sem("ml_og"), 1)

            dve.sem_inc(sem("readC"), RC)
            dve.wait_ge(sem("smalls_in"), 16)
            TT(lbs[:, 0, :], SM("lbl"), SM("lbl"), ALU.subtract).then_inc(sem("lb_diff"), 1)
            TT(E["lam"][:, 0:2], SM("lamv")[:, 0:2], SM("lamv")[:, 2:4], ALU.mult).then_inc(sem("lam_prod"), 1)
            TS(E["lam"][:, 6:7], SM("subln"), 1.0 - LAM_INIT, None, ALU.mult)
            dve.wait_ge(sem("lb_exp"), 1)
            nc.vector.reciprocal(lbs[:, 1, :], lbs[:, 0, :])
            dve.drain()
            TT(lbs[:, 1, :], lbs[:, 0, :], lbs[:, 1, :], ALU.mult)
            dve.drain()
            TT(lbs[:, 2, :], lbs[:, 1, :], lbs[:, 1, :], ALU.subtract)
            dve.drain()
            TS(lbs[:, 3, :], lbs[:, 2, :], -1.0, 1.0, ALU.mult, ALU.add)
            dve.wait_ge(sem("svec_ready"), 1)
            m, b = ada_places(0, 2)
            ada_group(0, 0, 0)
            ada_group(1, 1, 0)
            dve.sem_inc(sem("ada_acc"), 1)
            dve.wait_ge(sem("ada_sum"), 1)
            ada_mod(m[:, 0, :], b[:, 0, :], 2, 0)
            dve.wait_ge(sem("readC"), RC + 16)
            for group in range(2):
                TT(m[:, 1, 8 * group:8 * group + 8].rearrange("p (c v) -> p c v", v=2), ps[:, 4:8, 2 * group:2 * group + 2],
                   b[:, 1, 8 * group:8 * group + 8].rearrange("p (c v) -> p c v", v=2), ALU.add)
            dve.wait_ge(sem("lvl_ready"), NT)
            dve.drain()
            norm(0)
            dve.wait_ge(sem("lam_exp"), 1)
            TT(E["lam"][:, 4:5], E["lam"][:, 3:4], E["lam"][:, 2:3], ALU.subtract)
            dve.drain()
            TS(E["lam"][:, 5:6], E["lam"][:, 4:5], LAM_INIT, None, ALU.subtract)
            dve.drain()
            even()
            residual("even_out", MOD["g1", 0], T, 1, 1)
            norm(1)
            ffn_in(0, T)
            residual("ffn_out0", MOD["g2", 0], T, 3, 2, lambda: ada_one(0, 11))
            norm(2)
            odd()
            residual("odd_out", MOD["g1", 1], LAT, 1, 3)
            norm(3)
            ffn_in(1, LAT)
            residual("ffn_out1", MOD["g2", 1], LAT, 3, 4, lambda: ada_one(1, 11))
            ada_last(1, 7, 256)
            norm(4)
            norm(5)
            hgrn()
            norm(6)
            norm(7)
            mla()
            norm(8)


def make_consts(np):
    c = np.zeros((P, N_CONST), np.float32)

    def put(name, v):
        c[:v.shape[0], CONST[name][0]:CONST[name][0] + v.shape[1]] = v

    put("ident", np.eye(P, dtype=np.float32))
    put("ones", np.ones((P, P), np.float32))
    rot = np.zeros((P, P), np.float32)
    for m in range(P):
        if m % 32 < 16:
            rot[m + 16, m] = -1
        else:
            rot[m - 16, m] = 1
    put("rot128", rot)
    rot = np.zeros((HEAD, P), np.float32)
    for m in range(HEAD):
        if m < 32:
            rot[m + 32, m] = -1
        else:
            rot[m - 32, m] = 1
    put("rot64", rot)
    inv = np.float32(10000.0) ** (-np.arange(16, dtype=np.float32) / np.float32(16))
    t = np.arange(LAT)
    pos = np.stack([t // 64, t % 64]).astype(np.float32)
    d = np.arange(P) % HEAD
    ang = pos[d // 32] * inv[d % 16][:, None]
    put("cos128", np.cos(ang))
    put("sin128", np.sin(ang))
    d = np.arange(HEAD) % 32
    ang = pos[d // 16] * inv[d % 16][:, None]
    put("cos64", np.cos(ang))
    put("sin64", np.sin(ang))
    q, k = np.arange(P)[:, None], np.arange(P)[None, :]
    put("maskl", np.where(k >= q, 0, NEG).astype(np.float32))
    put("maskr", np.where(k <= q, 0, NEG).astype(np.float32))
    lv = np.zeros((P, 2 * LEVELS, 64), np.float32)
    s = np.arange(P)
    for dd in range(2):
        for i in range(LEVELS):
            h = 1 << i
            for j in range(64):
                lv[:, dd * LEVELS + i, j] = (s // (2 * h) == j // h) & ((s // h) % 2 == dd)
    return c, lv


def chunked(np, v):
    return v.reshape(-1, P).T


def blocks(np, w):
    k, n = w.shape
    return w.reshape(k // P, P, n // P, P).transpose(2, 1, 0, 3)


def tiles(np, w):
    k, n = w.shape
    kp, np_ = -(-k // D) * D, -(-n // P) * P
    if (kp, np_) != (k, n):
        full = np.zeros((kp, np_), w.dtype)
        full[:k, :n] = w
        w = full
    b = blocks(np, w)
    nb = b.shape[0]
    return b.reshape(nb, P, kp // D, D).transpose(0, 2, 1, 3).reshape(-1, P, D)


def kernel(**inputs):
    import numpy as np
    import concourse.bacc as bacc
    from concourse.bass_utils import run_bass_kernel_spmd

    i = {k: np.asarray(v) for k, v in inputs.items()}

    def interleave(*ts):
        return np.stack(ts, axis=1).reshape(-1, P, D)

    w = i["even_w_in"][0]
    parts = [tiles(np, w[:, at:at + 512]) for at in (1024, 1536, 2048, 512, 0)]
    even = interleave(*parts)

    def ffn(l):
        f = i["ffn_w_in"][l]
        return interleave(tiles(np, f[:, :HID]), tiles(np, f[:, HID:])), tiles(np, i["ffn_w_out"][l])

    f_in0, f_out0 = ffn(0)
    f_in1, f_out1 = ffn(1)
    w = i["odd_w_qkv"][0]
    odd = []
    for g in range(4):
        kg = w[:, 1024 + g * HEAD:1024 + (g + 1) * HEAD]
        odd += [tiles(np, w[:, g * 256:(g + 1) * 256]), tiles(np, np.concatenate([kg, kg], axis=1)),
                tiles(np, w[:, 1280 + g * HEAD:1280 + (g + 1) * HEAD])]
    odd = np.concatenate(odd)
    w = i["hg_w_in_2"][0]
    W2 = 2 * D
    hg = interleave(*[tiles(np, w[:, W2 * n:W2 * (n + 1)]) for n in range(5)])
    w = i["mla_w_in_2"][0]
    low = np.concatenate([tiles(np, w[:, 0:256]), tiles(np, w[:, 256:384]), tiles(np, w[:, 384:448])])
    qb = i["mla_w_qb_2"][0].reshape(2, P, HEADS, 192)
    kvb = i["mla_w_kvb_2"][0].reshape(P, HEADS, 256)
    wb = np.zeros((HEADS, P, D), np.float32)
    for k in range(2):
        wb[:, :, k * P:(k + 1) * P] = qb[k, :, :, 0:P].transpose(1, 0, 2)
        wb[:, :, 256 + k * HEAD:256 + (k + 1) * HEAD] = qb[k, :, :, P:].transpose(1, 0, 2)
    wb[:, :, 384:640] = kvb.transpose(1, 0, 2)
    mla = interleave(tiles(np, w[:, 448:]), wb)
    streamA = np.concatenate(
        [tiles(np, i["even_w_out"][0]), f_in0, f_out0, odd, tiles(np, i["odd_w_out"][0]), f_in1, f_out1,
         tiles(np, i["hg_w_out_2"][0]), low, mla, tiles(np, i["mla_w_out_2"][0])])
    streamB = np.concatenate([even, hg])
    streamC = np.concatenate([w.reshape(4, 2, P, -1, LAT).transpose(3, 0, 2, 1, 4).reshape(-1, P, D)
                              for w in (*i["ada_w"], *i["ada_w_2"])])
    assert len(streamA) == N_A and len(streamB) == N_B and len(streamC) == 4 * GROUPS

    smalls = np.zeros((P, N_SMALL), np.float32)

    def put(name, v):
        v = v.reshape(v.shape[0], -1)
        assert v.shape[1] == SMALL[name][1] - SMALL[name][0], name
        smalls[:v.shape[0], SMALL[name][0]:SMALL[name][1]] = v

    def twice(v):
        return np.repeat(chunked(np, v)[:, :, None], 2, axis=2)

    for tag, name in (("", "cvec"), ("_2", "cvec2")):
        put(name, np.stack([chunked(np, i["c" + tag][0]), chunked(np, i["c_ctx" + tag])], axis=2))
    put("ada_b", twice(np.concatenate([i["ada_b"].ravel(), i["ada_b_2"].ravel()])))
    for name, src in (("norm1_g", "norm1_g"), ("norm2_g", "norm2_g"), ("norm_pre", "norm_pre_2"), ("norm_post", "norm_post_2")):
        put(name, twice(i[src].ravel()))
    put("final_g", chunked(np, i["final_g"]))
    put("subln", i["diff_subln_g"][0][:, None])
    put("lamv", np.stack([i["diff_lq1"][0], i["diff_lq2"][0], i["diff_lk1"][0], i["diff_lk2"][0]], axis=1))
    put("sink", np.broadcast_to(i["odd_sink"][0][None, :], (P, 16)))
    put("lbl", chunked(np, i["hg_lb_logits_2"][0].ravel()))
    put("o_norm", i["hg_o_norm_2"][0][:, None])
    put("qa_norm", chunked(np, i["mla_qa_norm_2"][0]))
    put("kva_norm", i["mla_kva_norm_2"][0][:, None])
    sgu = np.concatenate([i["sgu_w"][0].transpose(2, 0, 1).reshape(P, 512),
                          np.broadcast_to(i["sgu_b"][0].reshape(1, 512), (P, 512))], axis=1)

    def tokens(v):
        return v.T.reshape(DC, P, -1).transpose(1, 0, 2)

    x_in = np.concatenate([tokens(i["x"][0]), tokens(i["ctx"][0])], axis=2)
    consts, lv = make_consts(np)
    arrays = {"streamA": streamA, "streamB": streamB, "streamC": streamC, "x_in": x_in, "ctx2_in": tokens(i["ctx_2"][0]), "smalls_in": smalls,
              "consts_in": consts, "lvl_in": lv, "sgu_in": sgu}
    arrays = {k: np.ascontiguousarray(v) for k, v in arrays.items()}
    nc = bacc.Bacc("TRN2", target_bir_lowering=False, num_devices=1)
    args = [nc.dram_tensor(k, v.shape, mybir.dt.from_np(v.dtype), kind="ExternalInput").ap() for k, v in arrays.items()]
    out = nc.dram_tensor("out", (P, DC, LAT), F32, kind="ExternalOutput").ap()
    build(nc, *args, out)
    r = run_bass_kernel_spmd(nc, [arrays], core_ids=[0])
    y = r.results[0]["out"]
    return y.transpose(2, 1, 0).reshape(1, LAT, D)
```
